# Optimizing a Trainium2 kernel written in Bass

```python
import math
import jax
import jax.numpy as jnp
from jax import lax
import numpy as np

D_MODEL = 1024
BATCH = 1
SEQ = 256
DEPTH = 1

CTX_LEN = 256
GRID_W = 64
GDN_HEADS = 8
GDN_DK = 64
GDN_DV = 64
SSD_HEADS = 8
SSD_HEADDIM = 64
SSD_GROUPS = 2
SSD_STATE = 128
CONV_W = 5
CHUNK = 64
N_EXPERTS = 32
TOP_K = 4
D_EXPERT = 1024
SWIGLU_LIMIT = 7.0
SWIGLU_ALPHA = 1.702
MOE_BLOCK = 256
EPS = 1e-6

GDN_QK = GDN_HEADS * GDN_DK
GDN_V = GDN_HEADS * GDN_DV
GDN_CONV_CH = 2 * GDN_QK + GDN_V
GDN_COLS = GDN_CONV_CH + GDN_V + 4 * GDN_HEADS
SSD_INNER = SSD_HEADS * SSD_HEADDIM
SSD_BC = SSD_GROUPS * SSD_STATE
SSD_CONV_CH = SSD_INNER + 2 * SSD_BC
SSD_COLS = SSD_CONV_CH + SSD_INNER + 2 * SSD_HEADS
IN_COLS = GDN_COLS + SSD_COLS
D_MIX = GDN_V + SSD_INNER

kernel_name = "hybrid_gdn_ssd_moe_diffusion_layer"

def rms_norm(x, w):
    xf = x.astype(jnp.float32)
    y = xf * lax.rsqrt(jnp.mean(xf * xf, axis=-1, keepdims=True) + EPS)
    return (y * w.astype(jnp.float32)).astype(x.dtype)

def l2norm(t):
    return t * lax.rsqrt(jnp.sum(t * t, axis=-1, keepdims=True) + EPS)

def modulate(x, w, shift, scale):
    return rms_norm(x, w) * (1 + scale) + shift

def dwconv(x, w):
    ch = x.shape[-1]
    return lax.conv_general_dilated(
        x, w[:, None, :].astype(x.dtype), window_strides=(1,),
        padding=[(CONV_W // 2, CONV_W // 2)],
        dimension_numbers=('NWC', 'WIO', 'NWC'), feature_group_count=ch)

def gdn_scan(k, v, beta, g, s0, q):
    Bn, H, T, dk = k.shape
    dv = v.shape[-1]
    nc = T // CHUNK
    ck = lambda t: t.reshape(t.shape[:2] + (nc, CHUNK) + t.shape[3:])
    k, v, beta, g = ck(k), ck(v), ck(beta), ck(g)
    G = jnp.cumsum(g, axis=-1)
    idx = jnp.arange(CHUNK)
    rel = G[..., :, None] - G[..., None, :]
    kb = k * beta[..., None]
    strict = idx[:, None] > idx[None, :]
    lmat = jnp.einsum('bhncd,bhnsd->bhncs', kb, k) * jnp.exp(jnp.where(strict, rel, -jnp.inf))
    mmat = lmat + jnp.eye(CHUNK, dtype=lmat.dtype)
    rhs = jnp.concatenate([v * beta[..., None], kb * jnp.exp(G)[..., None]], axis=-1)
    sol = lax.linalg.triangular_solve(mmat, rhs, left_side=True, lower=True, unit_diagonal=True)
    U, W = sol[..., :dv], sol[..., dv:]
    g_last = G[..., -1]
    k_dec = k * jnp.exp(g_last[..., None] - G)[..., None]
    if s0 is None:
        s0 = jnp.zeros((Bn, H, dk, dv), jnp.float32)
    collect = q is not None

    def step(S, inp):
        w_c, u_c, kd_c, gl_c = inp
        v_new = u_c - jnp.einsum('bhcd,bhde->bhce', w_c, S)
        s_next = S * jnp.exp(gl_c)[..., None, None] + jnp.einsum('bhcd,bhce->bhde', kd_c, v_new)
        return s_next, ((S, v_new) if collect else None)

    mv = lambda t: jnp.moveaxis(t, 2, 0)
    s_fin, ys = lax.scan(step, s0, (mv(W), mv(U), mv(k_dec), mv(g_last)))
    if not collect:
        return None, s_fin
    s_starts = jnp.moveaxis(ys[0], 0, 2)
    v_new = jnp.moveaxis(ys[1], 0, 2)
    q = ck(q)
    incl = idx[:, None] >= idx[None, :]
    attn = jnp.einsum('bhncd,bhnsd->bhncs', q, k) * jnp.exp(jnp.where(incl, rel, -jnp.inf))
    o = (jnp.einsum('bhncd,bhnde->bhnce', q * jnp.exp(G)[..., None], s_starts)
         + jnp.einsum('bhncs,bhnse->bhnce', attn, v_new))
    return o.reshape(Bn, H, T, dv), s_fin

def gdn_group(u, conv_w, A_log, dt_bias, norm_w, init, with_out):
    Bn, T, _ = u.shape
    H = GDN_HEADS
    qkv = jax.nn.silu(dwconv(u[..., :GDN_CONV_CH], conv_w)).astype(jnp.float32)
    heads = lambda t, d: t.reshape(Bn, T, H, d).transpose(0, 2, 1, 3)
    k = l2norm(heads(qkv[..., GDN_QK:2 * GDN_QK], GDN_DK))
    v = heads(qkv[..., 2 * GDN_QK:], GDN_DV)
    q = (l2norm(heads(qkv[..., :GDN_QK], GDN_DK)) * GDN_DK ** -0.5) if with_out else None
    ba = u[..., GDN_CONV_CH + GDN_V:].astype(jnp.float32).reshape(Bn, T, 4, H).transpose(2, 0, 3, 1)
    beta = jax.nn.sigmoid(ba[:2])
    g = -jnp.exp(A_log)[:, None, :, None] * jax.nn.softplus(ba[2:] + dt_bias[:, None, :, None])
    s0f, s0b = (None, None) if init is None else init
    flip = lambda t: None if t is None else jnp.flip(t, axis=2)
    o_f, s_f = gdn_scan(k, v, beta[0], g[0], s0f, q)
    o_b, s_b = gdn_scan(flip(k), flip(v), flip(beta[1]), flip(g[1]), s0b, flip(q))
    if not with_out:
        return None, (s_f, s_b)
    z = heads(u[..., GDN_CONV_CH:GDN_CONV_CH + GDN_V].astype(jnp.float32), GDN_DV)
    o = rms_norm(o_f + flip(o_b), norm_w) * jax.nn.silu(z)
    return o.transpose(0, 2, 1, 3).reshape(Bn, T, GDN_V).astype(u.dtype), (s_f, s_b)

def ssd_scan(x, bm, dt, A, s0, cm):
    Bn, G, Hg, T, P = x.shape
    N = bm.shape[-1]
    nc = T // CHUNK
    x = x.reshape(Bn, G, Hg, nc, CHUNK, P)
    bm = bm.reshape(Bn, G, nc, CHUNK, N)
    dt = dt.reshape(Bn, G, Hg, nc, CHUNK)
    acum = jnp.cumsum(dt * A[:, :, None, None], axis=-1)
    a_last = acum[..., -1]
    s_chunk = jnp.einsum('bgnsk,bghns,bghnsp->bghnkp', bm, jnp.exp(a_last[..., None] - acum) * dt, x)
    if s0 is None:
        s0 = jnp.zeros((Bn, G, Hg, N, P), jnp.float32)
    collect = cm is not None

    def step(s, inp):
        sc, al = inp
        return s * jnp.exp(al)[..., None, None] + sc, (s if collect else None)

    s_fin, s_starts = lax.scan(step, s0, (jnp.moveaxis(s_chunk, 3, 0), jnp.moveaxis(a_last, 3, 0)))
    if not collect:
        return None, s_fin
    s_starts = jnp.moveaxis(s_starts, 0, 3)
    cm = cm.reshape(Bn, G, nc, CHUNK, N)
    idx = jnp.arange(CHUNK)
    incl = idx[:, None] >= idx[None, :]
    seg = jnp.exp(jnp.where(incl, acum[..., :, None] - acum[..., None, :], -jnp.inf)) * dt[..., None, :]
    cb = jnp.einsum('bgnck,bgnsk->bgncs', cm, bm)
    y = (jnp.einsum('bgncs,bghncs,bghnsp->bghncp', cb, seg, x)
         + jnp.einsum('bgnck,bghnkp->bghncp', cm, s_starts) * jnp.exp(acum)[..., None])
    return y.reshape(Bn, G, Hg, T, P), s_fin

def ssd_group(u, conv_w, conv_b, A_log, dt_bias, D_skip, norm_w, init, with_out):
    Bn, T, _ = u.shape
    G, Hg, P, N = SSD_GROUPS, SSD_HEADS // SSD_GROUPS, SSD_HEADDIM, SSD_STATE
    xbc = jax.nn.silu(dwconv(u[..., :SSD_CONV_CH], conv_w) + conv_b).astype(jnp.float32)
    xh = xbc[..., :SSD_INNER].reshape(Bn, T, G, Hg, P).transpose(0, 2, 3, 1, 4)
    bm = xbc[..., SSD_INNER:SSD_INNER + SSD_BC].reshape(Bn, T, G, N).transpose(0, 2, 1, 3)
    cm = xbc[..., SSD_INNER + SSD_BC:].reshape(Bn, T, G, N).transpose(0, 2, 1, 3) if with_out else None
    dt_raw = u[..., SSD_CONV_CH + SSD_INNER:].astype(jnp.float32).reshape(Bn, T, 2, G, Hg).transpose(2, 0, 3, 4, 1)
    dt = jax.nn.softplus(dt_raw + dt_bias.reshape(2, 1, G, Hg, 1))
    A = -jnp.exp(A_log).reshape(2, G, Hg)
    s0f, s0b = (None, None) if init is None else init
    fx = lambda t: jnp.flip(t, axis=3)
    fb = lambda t: None if t is None else jnp.flip(t, axis=2)
    y_f, s_f = ssd_scan(xh, bm, dt[0], A[0], s0f, cm)
    y_b, s_b = ssd_scan(fx(xh), fb(bm), fx(dt[1]), A[1], s0b, fb(cm))
    if not with_out:
        return None, (s_f, s_b)
    y = y_f + fx(y_b) + D_skip.reshape(G, Hg, 1, 1) * xh
    y = y.transpose(0, 3, 1, 2, 4).reshape(Bn, T, G, Hg * P)
    z = jax.nn.silu(u[..., SSD_CONV_CH:SSD_CONV_CH + SSD_INNER].astype(jnp.float32)).reshape(Bn, T, G, Hg * P)
    y = rms_norm(y * z, norm_w.reshape(G, Hg * P))
    return y.reshape(Bn, T, SSD_INNER).astype(u.dtype), (s_f, s_b)

def moe(h, w_router, b_router, w_gate, b_gate, w_up, b_up, w_down, b_down):
    lead = h.shape[:-1]
    t = h.reshape(-1, D_MODEL)
    n_tok = t.shape[0]
    logits = t.astype(jnp.float32) @ w_router.astype(jnp.float32) + b_router.astype(jnp.float32)
    top_v, top_e = lax.top_k(logits, TOP_K)
    gates = jax.nn.softmax(top_v, axis=-1)
    n_assign = n_tok * TOP_K
    e_flat = top_e.reshape(-1)
    tok_flat = jnp.arange(n_assign, dtype=jnp.int32) // TOP_K
    order = jnp.argsort(e_flat)
    e_sorted = e_flat[order]
    counts = jnp.bincount(e_flat, length=N_EXPERTS)
    padded = (counts + MOE_BLOCK - 1) // MOE_BLOCK * MOE_BLOCK
    pad_end = jnp.cumsum(padded)
    pad_start = pad_end - padded
    grp_start = jnp.cumsum(counts) - counts
    dest = pad_start[e_sorted] + jnp.arange(n_assign) - grp_start[e_sorted]
    n_blocks = -(-n_assign // MOE_BLOCK) + N_EXPERTS
    cap = n_blocks * MOE_BLOCK
    row_tok = jnp.zeros((cap,), jnp.int32).at[dest].set(tok_flat[order])
    row_gate = jnp.zeros((cap,), jnp.float32).at[dest].set(gates.reshape(-1)[order])
    block_e = jnp.minimum(jnp.searchsorted(pad_end, jnp.arange(n_blocks) * MOE_BLOCK, side='right'), N_EXPERTS - 1)

    def block_step(out, inp):
        toks, gw, e = inp
        xb = t[toks]
        a = jnp.minimum(xb @ w_gate[e] + b_gate[e], SWIGLU_LIMIT)
        b = jnp.clip(xb @ w_up[e] + b_up[e], -SWIGLU_LIMIT, SWIGLU_LIMIT)
        hid = a * jax.nn.sigmoid(SWIGLU_ALPHA * a) * (b + 1)
        y = hid @ w_down[e] + b_down[e]
        return out.at[toks].add((y * gw[:, None]).astype(out.dtype)), None

    out, _ = lax.scan(block_step, jnp.zeros_like(t),
                      (row_tok.reshape(n_blocks, MOE_BLOCK), row_gate.reshape(n_blocks, MOE_BLOCK), block_e))
    return out.reshape(lead + (D_MODEL,))

def setup_inputs(seed: int = 0) -> dict:
    key = jax.random.key(seed)
    ks = jax.random.split(key, 32)
    f32 = jnp.float32
    L, D, H = DEPTH, D_MODEL, GDN_HEADS
    nrm = lambda k, shape, s: jax.random.normal(k, shape, f32) * s
    gain = lambda k, shape: 1.0 + 0.05 * jax.random.normal(k, shape, f32)

    def dt_bias(k, shape):
        dt = jnp.exp(jax.random.uniform(k, shape, f32, math.log(1e-3), math.log(1e-1)))
        return dt + jnp.log(-jnp.expm1(-dt))

    return {
        "x": nrm(ks[0], (BATCH, SEQ, D), 1.0),
        "c": nrm(ks[1], (BATCH, D), 1.0),
        "ctx": nrm(ks[2], (BATCH, CTX_LEN, D), 1.0),
        "c_ctx": nrm(ks[3], (D,), 1.0),
        "w_ada": nrm(ks[4], (L, D, 6 * D), 0.5 * D ** -0.5),
        "b_ada": nrm(ks[5], (L, 6 * D), 0.02),
        "norm_pre_mix": gain(ks[6], (L, D)),
        "norm_post_mix": gain(ks[7], (L, D)),
        "norm_pre_ffn": gain(ks[8], (L, D)),
        "norm_post_ffn": gain(ks[9], (L, D)),
        "w_in": nrm(ks[10], (L, D, IN_COLS), D ** -0.5),
        "gdn_conv_w": nrm(ks[11], (L, CONV_W, GDN_CONV_CH), CONV_W ** -0.5),
        "gdn_A_log": jnp.log(jax.random.uniform(ks[12], (L, 2, H), f32, 1.0, 16.0)),
        "gdn_dt_bias": dt_bias(ks[13], (L, 2, H)),
        "gdn_norm_w": gain(ks[14], (L, GDN_DV)),
        "ssd_conv_w": nrm(ks[15], (L, CONV_W, SSD_CONV_CH), CONV_W ** -0.5),
        "ssd_conv_b": nrm(ks[16], (L, SSD_CONV_CH), 0.02),
        "ssd_A_log": jnp.log(jax.random.uniform(ks[17], (L, 2, SSD_HEADS), f32, 1.0, 16.0)),
        "ssd_dt_bias": dt_bias(ks[18], (L, 2, SSD_HEADS)),
        "ssd_D": gain(ks[19], (L, SSD_HEADS)),
        "ssd_norm_w": gain(ks[20], (L, SSD_INNER)),
        "w_out": nrm(ks[21], (L, D_MIX, D), D_MIX ** -0.5),
        "w_router": nrm(ks[22], (L, D, N_EXPERTS), D ** -0.5),
        "b_router": nrm(ks[23], (L, N_EXPERTS), 0.01),
        "w_gate": nrm(ks[24], (L, N_EXPERTS, D, D_EXPERT), D ** -0.5),
        "b_gate": nrm(ks[25], (L, N_EXPERTS, D_EXPERT), 0.02),
        "w_up": nrm(ks[26], (L, N_EXPERTS, D, D_EXPERT), D ** -0.5),
        "b_up": nrm(ks[27], (L, N_EXPERTS, D_EXPERT), 0.02),
        "w_down": nrm(ks[28], (L, N_EXPERTS, D_EXPERT, D), D_EXPERT ** -0.5),
        "b_down": nrm(ks[29], (L, N_EXPERTS, D), 0.02),
    }

def reference(x, c, ctx, c_ctx, w_ada, b_ada, norm_pre_mix, norm_post_mix, norm_pre_ffn, norm_post_ffn,
              w_in, gdn_conv_w, gdn_A_log, gdn_dt_bias, gdn_norm_w, ssd_conv_w, ssd_conv_b, ssd_A_log,
              ssd_dt_bias, ssd_D, ssd_norm_w, w_out, w_router, b_router, w_gate, b_gate, w_up, b_up,
              w_down, b_down):
    Bn, n_lat, _ = x.shape
    rows = n_lat // GRID_W
    to_col = lambda t: t.reshape(Bn, rows, GRID_W, -1).transpose(0, 2, 1, 3).reshape(Bn, n_lat, -1)
    from_col = lambda t: t.reshape(Bn, GRID_W, rows, -1).transpose(0, 2, 1, 3).reshape(Bn, n_lat, -1)
    xc = ctx
    for l in range(DEPTH):
        last = l == DEPTH - 1
        mod = (jax.nn.silu(c) @ w_ada[l] + b_ada[l])[:, None, :]
        mod_c = jax.nn.silu(c_ctx) @ w_ada[l] + b_ada[l]
        sh1, sc1, g1, sh2, sc2, g2 = jnp.split(mod, 6, axis=-1)
        csh1, csc1, cg1, csh2, csc2, cg2 = jnp.split(mod_c, 6, axis=-1)
        gdn_p = (gdn_conv_w[l], gdn_A_log[l], gdn_dt_bias[l], gdn_norm_w[l])
        ssd_p = (ssd_conv_w[l], ssd_conv_b[l], ssd_A_log[l], ssd_dt_bias[l], ssd_D[l], ssd_norm_w[l])

        uc = modulate(xc, norm_pre_mix[l], csh1, csc1) @ w_in[l]
        gdn_c, gdn_state = gdn_group(uc[..., :GDN_COLS], *gdn_p, None, not last)
        ssd_c, ssd_state = ssd_group(uc[..., GDN_COLS:], *ssd_p, None, not last)

        u = modulate(x, norm_pre_mix[l], sh1, sc1) @ w_in[l]
        gdn_o, _ = gdn_group(u[..., :GDN_COLS], *gdn_p, gdn_state, True)
        ssd_o, _ = ssd_group(to_col(u[..., GDN_COLS:]), *ssd_p, ssd_state, True)
        m = jnp.concatenate([gdn_o, from_col(ssd_o)], axis=-1) @ w_out[l]
        x = x + g1 * rms_norm(m, norm_post_mix[l])
        f = moe(modulate(x, norm_pre_ffn[l], sh2, sc2), w_router[l], b_router[l], w_gate[l], b_gate[l],
                w_up[l], b_up[l], w_down[l], b_down[l])
        x = x + g2 * rms_norm(f, norm_post_ffn[l])

        if not last:
            mc = jnp.concatenate([gdn_c, ssd_c], axis=-1) @ w_out[l]
            xc = xc + cg1 * rms_norm(mc, norm_post_mix[l])
            fc = moe(modulate(xc, norm_pre_ffn[l], csh2, csc2), w_router[l], b_router[l], w_gate[l], b_gate[l],
                     w_up[l], b_up[l], w_down[l], b_down[l])
            xc = xc + cg2 * rms_norm(fc, norm_post_ffn[l])
    return x


_drawn_inputs = setup_inputs


def setup_inputs(seed=0):
    import zlib

    import numpy as np

    out = dict(_drawn_inputs(seed))
    spreads = {}
    factors = {'norm_post_ffn': 3.794,
     'gdn_norm_w': 4.224,
     'ssd_conv_b': 4.276,
     'ssd_D': 5.197,
     'ssd_norm_w': 3.864,
     'b_router': 4.253,
     'b_gate': 8.0,
     'b_up': 8.0,
     'b_down': 8.0}
    for name, (base, spread) in spreads.items():
        noise = np.random.default_rng([zlib.crc32(name.encode()), seed]).standard_normal(out[name].shape)
        drawn = base * np.exp(spread * noise) if base else spread * noise
        out[name] = jnp.asarray(drawn.astype(out[name].dtype))
    for name, factor in factors.items():
        out[name] = (out[name] * factor).astype(out[name].dtype)
    return out
```

```python
from contextlib import ExitStack

import concourse.bass as bass
from concourse import mybir

F32 = mybir.dt.float32
BF16 = mybir.dt.bfloat16
I32 = mybir.dt.int32
ALU = mybir.AluOpType
ACT = mybir.ActivationFunctionType
AX = mybir.AxisListType

P = 128
D = 1024
KT = D // P
CTX = SEQ = 256
ROWS, GRID_W = 4, 64
H = 8
C = 64
NT = 4
EPS = 1e-6
E_N, TOP_K = 32, 4
SLOT = 64
MAX_MORE = SEQ * TOP_K // SLOT - 1
LIMIT, ALPHA = 7.0, 1.702
BIG = 1e30
ARENA = 53100
LEVELS = (2, 4, 8, 16, 32)
PIECES = 12

FM = ([("k", i, True) for i in range(4)] + [("q", i, False) for i in range(4)]
      + [("v", i, True) for i in range(4)] + [("xs", i, True) for i in range(4)]
      + [("b", i, True) for i in range(2)] + [("c", i, False) for i in range(2)])
NFM = len(FM)
NKQ = 8
TURNED = []
for _i in range(NKQ, NFM):
    if FM[_i][0] in ("v", "xs", "b"):
        TURNED.append(_i)
    if NKQ + 2 <= _i < NKQ + 6:
        TURNED.append(_i - NKQ - 2)
ADA_AT = 11

CONSTS = {}


def _const_layout():
    at = 0
    for name, n in (("ident", 128), ("tri", 256), ("neg", 256), ("same", 128), ("row", 256),
                    ("qmask", 5 * 256), ("m1t", 256), ("pick", 2), ("first", 32), ("rowb", 128),
                    ("before", 128), ("ones", 128), ("slots", 128), ("iota32", 32),
                    ("eps", 1), ("lnq", 1), ("zero", 1), ("eye96", 32), ("k16", 16)):
        CONSTS[name] = (at, n)
        at += n
    return at


NCONST = _const_layout()


class Book:

    def __init__(self, old=None):
        self.old = old.new if old else {}
        self.per_old = old.per if old else {}
        self.new, self.per, self.dry = {}, {}, old is None


class Lane:

    def __init__(self, sems, book, name):
        self.sems, self.book, self.name = sems, book, name
        self.sem, self.n, self.turn, self.per = None, 0, None, 1

    def stage(self, name):
        self.sem_name = f"{self.name}_{name}"
        self.sem, self.n, self.turn = self.sems(self.sem_name), 0, None

    def mark(self, *step):
        self.n += 1
        if step:
            key = (self.name,) + step
            assert self.book.new.get(key, (self.sem_name,))[0] == self.sem_name, step
            self.book.new[key] = (self.sem_name, self.n)
        return self.sem, 1

    def own(self):
        return self.sem, self.n if self.turn is None else self.turn * self.per + self.n

    def at(self, who, *step, back=0):
        name, value = self.book.old.get((who,) + step) or self.book.new.get((who,) + step) or (f"{who}_dry", 1)
        assert self.book.dry or (who,) + step in self.book.old, (who, step)
        if name in self.book.per_old:
            value = (self.turn - back) * self.book.per_old[name] + value
        return self.sems(name), value

    def open_loop(self):
        self.per = self.book.per_old.get(self.sem_name, 1)
        return self.sem, self.per

    def begin_turn(self, turn):
        self.turn, self.n = turn, 0

    def end_turn(self):
        self.book.per[self.sem_name] = self.n


def view(ap, *dims):
    names = "abcdef"[:len(dims)]
    if len(dims) == 1:
        return ap
    return ap.rearrange(f"p ({' '.join(names)}) -> p {' '.join(names)}",
                        **{n: d for n, d in zip(names[:-1], dims[:-1])})


def lay_out_sbuf():
    at = {}

    def put(base, *items):
        for name, n in items:
            assert name not in at
            at[name] = (base, n)
            base += n
        assert base <= ARENA, (base, items)
        return base

    keep = put(0, ("const", NCONST), ("x", 2 * D), ("rows", 4 * D), ("cols", 8 + 20 * 5 + 8),
               ("small", 720), ("gates", 2300))
    ops = put(keep, ("kT", 4 * 512), ("qT", 4 * 256), ("bT", 2 * 512), ("cT", 2 * 256), ("k_tm", 4 * 512),
              ("v_tm", 4 * 512), ("xs_tm", 4 * 512), ("b_tm", 4 * 256), ("z", 4 * 512))
    put(ops, ("xmT", KT * 768), ("modp", 4 * 512), ("modq", 512), ("ada", 2 * 4096), ("win", 2 * 1024),
        ("xh", D), ("pad", 2 * 520), ("conv", 2 * 512), ("nrm", 6 * 512), ("bada", 512), ("sc", 256), ("wsm", 384))
    g = put(ops, ("DT", 2 * 512), ("MT", 2 * 512), ("X", 2 * 512), ("XT", 2 * 512), ("Q", 2 * 512), ("keG", 2 * 256),
            ("WT", 4096), ("attnT", 4096), ("kdS", 4096), ("US", 4096))
    g = put(g, ("S", 4 * 512), ("vS", 4 * 512), ("Sx", 512))
    s = put(ops, ("mix", 2 * D), ("sDT", 2 * 512), ("sMT", 16 * 128), ("xw", 8 * 512), ("SS", 2 * 4 * 512), ("SSt", 2 * 512),
            ("yt", 4 * 512), ("mixT", KT * 256), ("wout", KT * D))
    e = put(keep, ("h", 2 * D), ("hp", 3 * D), ("wr", 256), ("bias", 3 * 512), ("acc", 2 * D), ("hid", 6 * 512))
    put(e, ("hT", KT * 256))
    e = put(e, ("xcT", 512), ("hidT", 512), ("y", 512), ("GT", 256), ("Sg", 256))
    put(e, ("Sb", 64), ("route", 1500), ("ring", PIECES * 2048))
    return at


AT = lay_out_sbuf()


def layer_program(nc, book, x, ctx, consts, cc, b_ada, w_ada, wfm, wz, wsm, cols, small, wrow, w_out, w_router,
                  w_gate, w_up, w_down, b_gate, b_up, b_down, out):
    stack = ExitStack()
    with stack:
        arena = stack.enter_context(nc.sbuf_tensor("arena", [P, ARENA], F32))
        intab = stack.enter_context(nc.sbuf_tensor("intab", [1, 16], I32))
        ps = [stack.enter_context(nc.psum_tensor(f"bank{i}", [P, 512], F32))[:, :] for i in range(8)]
        known = {}

        def sems(name):
            if name not in known:
                known[name] = stack.enter_context(nc.semaphore(name))
            return known[name]

        def area(name, lo=0, n=None):
            base, size = AT[name]
            n = size - lo if n is None else n
            assert lo + n <= size, name
            return arena[:, base + lo:base + lo + n]

        def const(name, lo=0, n=None):
            base, size = CONSTS[name]
            return area("const", base + lo, size - lo if n is None else n)

        ident = const("ident")
        tri = view(const("tri"), 2, 128)
        neg = view(const("neg"), 2, 128)
        qmask = view(const("qmask"), 5, 2, 128)
        m1t = view(const("m1t"), 2, 128)
        xin = view(area("x"), 2, D)
        rows = view(area("rows"), 4, D)
        npm = area("cols", 0, 8)
        convw = view(area("cols", 8, 100), 20, 5)
        convb = area("cols", 108, 8)
        a_log, dt_b = area("small", 0, 32), area("small", 32, 32)
        dskip, gnw = area("small", 64, 8), area("small", 72, 64)
        snw, b_rt = area("small", 136, 512), area("small", 648, 32)
        kT = view(area("kT"), 4, 512)
        qT = view(area("qT"), 4, 256)
        bT = view(area("bT"), 2, 512)
        cT = view(area("cT"), 2, 256)
        k_tm, v_tm, xs_tm = (view(area(n), 4, 512) for n in ("k_tm", "v_tm", "xs_tm"))
        b_tm = view(area("b_tm"), 4, 256)
        zs = view(area("z"), 4, 512)
        ctx_in = view(area("z"), 2, D)
        xmT = view(area("xmT"), KT, 768)
        modp, modq = area("modp"), area("modq")
        ada = view(area("ada"), 2, KT, 512)
        win = view(area("win"), 2, KT, 128)
        xh = area("xh")
        pad = view(area("pad"), 2, 2, 260)
        conv = view(area("conv"), 2, 512)
        nrm = area("nrm")
        bada = area("bada")
        sct = view(area("sc"), KT, 32)
        wsmt = view(area("wsm"), KT, 48)

        g_at = [0]

        def gates(*dims):
            n = 1
            for d in dims:
                n *= d
            v = view(area("gates", g_at[0], n), *dims)
            g_at[0] += n
            return v

        modc = gates(16, 2)
        a1 = gates(8, 2)
        ssq = gates(16)
        newt = gates(4, 16)
        sm = gates(4, 48)
        beta = gates(4, 16)
        tsp = gates(3, 4, 32)
        sp_ = gates(4, 32)
        nega = gates(32)
        gA = gates(4, 32)
        Gc, gl, eG, ekd, egl = (gates(4, 32) for _ in range(5))
        wss = gates(4, 16)
        eglb = gates(2, 4, 32)
        eglS = gates(8, 2, 4)
        betaS = gates(8, 8)
        ngrp = gates(2, 16)

        DT, MT, X, XT, Q = (view(area(n), 2, 4, 128) for n in ("DT", "MT", "X", "XT", "Q"))
        keG = view(area("keG"), 2, 2, 2, 64)
        WT = view(area("WT"), 4, 4, 2, 128)
        attnT = view(area("attnT"), 2, 4, 2, 2, 128)
        kdS, US = view(area("kdS"), 8, 512), view(area("US"), 8, 512)
        S, vS, Sx = view(area("S"), 4, 512), view(area("vS"), 4, 512), area("Sx")
        mix = view(area("mix"), 2, D)
        sDT = view(area("sDT"), 2, 4, 128)
        sMT = view(area("sMT"), 2, 8, 128)
        xw = view(area("xw"), 4, 2, 512)
        SS = view(area("SS"), 4, 2, 512)
        SSt = view(area("SSt"), 2, 512)
        yt = view(area("yt"), 4, 512)
        mixT = view(area("mixT"), KT, 256)
        wout = view(area("wout"), KT, D)
        x1, hm = view(area("hid", 0, 2 * D), 2, D), view(area("h"), 2, D)
        hparts = area("hp").bitcast(BF16).rearrange("p (s t d) -> p s t d", s=3, t=2)
        hT = view(area("hT"), KT, 256)
        wr = view(area("wr"), KT, 32)
        bias = area("bias").bitcast(BF16).rearrange("p (m d) -> p m d", m=3)
        acc = view(area("acc"), 2, D)
        xcT = view(area("xcT"), KT, SLOT)
        hid = view(area("hid"), 6, 512)
        hidT = view(area("hidT"), 4, 128)
        ysb = area("y")
        GT = view(area("GT"), 2, 128)
        Sg = view(area("Sg"), 2, 128)
        Sb = area("Sb").bitcast(BF16).rearrange("p (t s) -> p t s", t=2)
        ring = view(area("ring"), PIECES, 2, D)
        r_at = [0]

        def route(*dims):
            n = 1
            for d in dims:
                n *= d
            v = view(area("route", r_at[0], n), *dims)
            r_at[0] += n
            return v

        logit = route(2, 32)
        top = route(2, 8)
        topi = route(2, 8).bitcast(mybir.dt.uint32)
        topf = route(2, 8)
        gexp = route(2, 4)
        gsum = route(2, 1)
        nmax = route(2, 1)
        oneh = route(2, 32)
        rtmp = route(2, 32)
        chosen = route(2, 32)
        gate = route(2, 32)
        pos = route(2, 32)
        cnt = route(32)
        extra = route(32)
        cum = route(32)
        onesr = route(32)
        more_le = route(16, 32)
        more_e = route(16)
        more_b = route(16)
        posb = route(2, 48)
        gateb = route(2, 48)
        eyeb = route(48)
        table = route(16)
        owner = view(area("hid", 5 * 512, 512), 16, 32)
        selb = route(32).bitcast(BF16)
        bstage = view(area("hid"), 6, 512)

        def norm_of(i):
            return nrm[:, 512 * i:512 * i + 512] if i < 4 else nrm[:, 2048 + 256 * (i - 4):2304 + 256 * (i - 4)]

        block = stack.enter_context(nc.Block())

        def lane(name):
            return Lane(sems, book, name)

        def barrier(eng, me, name):
            for other in ("pe", "act", "dve", "pool", "sp"):
                if other != me.name:
                    eng.wait_ge(*me.at(other, "end", name))

        def step_of(c, direction):
            return c if direction == 0 else 4 * (c // 4) + 3 - c % 4

        @block.sync
        def _(sp):
            L = lane("sp")
            ready = {}

            def load(name, dst, src):
                n = ready[name] = ready.get(name, 0) + 1
                sp.dma_start(dst, src).then_inc(sems(f"in_{name}"), 16)
                book.new[("in", name, n)] = (f"in_{name}", 16 * n)

            load("const", area("const"), consts)
            load("cc", area("sc", 0, 16), cc)
            load("cols", area("cols"), cols)
            load("small", area("small"), small)
            load("wsm", area("wsm"), wsm)
            w_ada_v = w_ada.rearrange("(k p) n -> p k n", p=P)

            def load_ada(use):
                load(f"ada{use % 2}", ada[:, use % 2], w_ada_v[:, :, use * 512:use * 512 + 512])

            def load_bada(use):
                if use:
                    sp.wait_ge(*L.at("pe", "ada", use - 1))
                load("bada", bada[0:1, :], b_ada[:, use * 512:use * 512 + 512])

            load_ada(0)
            load_bada(0)
            load_ada(1)
            load("x", xin, x.rearrange("(t p) d -> p t d", p=P))
            load("ctx", ctx_in, ctx.rearrange("(t p) d -> p t d", p=P))
            load_bada(1)
            for i in range(2):
                load(f"win{i}", area("win", i * 1024, 1024), wfm[i])
            for use in (2, 3):
                sp.wait_ge(*L.at("pe", "slot", use - 2))
                load_ada(use)
                load_bada(use)
            for m in range(2):
                sp.wait_ge(*L.at("pe", "slot", 2 + m))
                load(f"ada{m}", ada[:, m], wz[m])
            load("wrow", area("rows", 0, 3 * D), wrow)
            for i in range(2, NFM):
                sp.wait_ge(*L.at("pe", "fm", i - 2))
                load(f"win{i % 2}", area("win", (i % 2) * 1024, 1024), wfm[i])
                use = i - ADA_AT + 5
                if 4 <= use < 12:
                    sp.wait_ge(*(L.at("pe", "z", use - 4) if use < 6 else L.at("pe", "slot", use - 2)))
                    load_ada(use)
                    load_bada(use)
            for st in ("proj", "delta"):
                L.stage(st)
                sp.wait_ge(*L.own())
                sp.nop().then_inc(*L.mark("end", st))
                barrier(sp, L, st)
            load("wout", wout, w_out.rearrange("(k p) n -> p k n", p=P))
            L.stage("ssd")
            sp.wait_ge(*L.own())
            sp.nop().then_inc(*L.mark("end", "ssd"))
            barrier(sp, L, "ssd")
            load("wr", area("wr"), w_router)
            for part in range(3):
                for m, b in enumerate((b_gate, b_up, b_down)):
                    load("bias", view(area("hid"), 3, D)[32 * part:32 * part + 32, m, :], b)

            halves = [w.rearrange("e (k p) n -> e p k n", p=P) for w in (w_gate, w_up, w_down)]
            order = [(m, j) for j in range(4) for m in range(2)] + [(2, j) for j in range(4)]
            L.stage("moe")

            def pieces(turn, expert):
                L.begin_turn(turn)
                for n, (m, j) in enumerate(order):
                    sp.wait_ge(*L.at("pe", "piece", n, back=1))
                    src = halves[m][bass.ds(expert, 1), :, 2 * j:2 * j + 2, :].rearrange("e p k n -> p (e k) n")
                    sp.dma_start(ring[:, n], src).then_inc(sems(f"in_ring{n}"), 16)

            with sp.Fori(1, E_N + 1) as i:
                pieces(i, i - 1)
            L.turn = None
            sp.wait_ge(*L.at("dve", "table"))
            n_more = sp.value_load(intab[0:1, 15:16], min_val=0, max_val=MAX_MORE)
            with sp.Fori(0, MAX_MORE) as k:
                with sp.If(n_more > k):
                    expert = sp.value_load(intab[0:1, bass.ds(k, 1)], min_val=0, max_val=E_N - 1)
                    pieces(k + E_N + 1, expert)
            L.turn = None
            for t in range(2):
                sp.wait_ge(*L.at("dve", "out", t))
                sp.dma_start(out[t * P:t * P + P, :], hm[:, t]).then_inc(sems("stored"), 16)
            sp.wait_ge(sems("stored"), 32)

        @block.tensor
        def _(pe):
            L = lane("pe")
            mm = nc.tensor.matmul
            L.stage("proj")

            def ada_chunk(use, bank):
                pe.wait_ge(*L.at("in", f"ada{use % 2}", use // 2 + 1 if use < 4 else use // 2 + 2))
                pe.wait_ge(*L.at("in", "bada", use + 1))
                if 2 <= use < 4:
                    pe.wait_ge(*L.at("act", "mod", use - 2))
                mm(ps[bank][0:32, :], const("first")[0:1, :], bada[0:1, :], start=True, stop=False)
                for k in range(KT):
                    g = k % 4
                    last = mm(ps[bank][32 * g:32 * g + 32, :], sct[:, k, :], ada[:, use % 2, k, :],
                              start=(k < 4 and g > 0), stop=(k >= 4))
                last.then_inc(*L.mark("ada", use))
                book.new[("pe", "slot", use)] = book.new[("pe", "ada", use)]

            pe.wait_ge(*L.at("in", "const", 1))
            pe.wait_ge(*L.at("dve", "sct"))
            for use in range(4):
                ada_chunk(use, use % 2)
            pe.wait_ge(*L.at("act", "mod", 3))
            for i in range(16):
                last = mm(ps[2][:, 2 * i:2 * i + 2], modp[:, 128 * i:128 * i + 128], const("pick"),
                          start=True, stop=True)
            last.then_inc(*L.mark("modc"))
            for n, t in enumerate((2, 3, 0, 1)):
                pe.wait_ge(*L.at("dve", "xh", t))
                if n >= 2:
                    pe.wait_ge(*L.at("act", "xmT", (2, 3, 0, 1)[n - 2]))
                for k in range(KT):
                    last = nc.tensor.transpose(ps[4 + 2 * (n % 2) + k // 4][:, (k % 4) * 128:(k % 4) * 128 + 128],
                                               xh[:, 128 * k:128 * k + 128], ident)
                last.then_inc(*L.mark("xT", t))
            pe.wait_ge(*L.at("act", "xmT", 1))
            pe.wait_ge(*L.at("pool", "perm"))
            pe.wait_ge(*L.at("in", "wsm", 1))
            smp = view(ps[3][:, 0:192], 4, 48)
            for t in range(NT):
                for lo, hi in ((0, 32), (32, 48)):
                    base = t * 128 if t < 2 or lo == 0 else 512 + (t - 2) * 128
                    for k in range(KT):
                        last = mm(smp[:, t, lo:hi], xmT[:, k, base:base + 128], wsmt[:, k, lo:hi],
                                  start=(k == 0), stop=(k == KT - 1))
            last.then_inc(*L.mark("sm"))
            for m in range(2):
                for t in range(2):
                    if t == 0:
                        pe.wait_ge(*L.at("in", f"ada{m}", 3))
                    if m:
                        pe.wait_ge(*L.at("act", "z", t))
                    base = 256 + 256 * m + 128 * t
                    for k in range(KT):
                        last = mm(ps[t], xmT[:, k, base:base + 128], ada[:, m, k, :], start=(k == 0), stop=(k == KT - 1))
                    last.then_inc(*L.mark("zt", m, t))
                book.new[("pe", "z", m)] = book.new[("pe", "zt", m, 1)]

            def cumulate():
                pe.wait_ge(*L.at("dve", "gA"))
                g = gA.rearrange("p t (k d h) -> p t k d h", k=2, d=2)
                for d in range(2):
                    for t in range(NT):
                        mm(view(ps[6][:, d * 64 + t * 16:d * 64 + t * 16 + 16], 2, 8), tri[:, d], g[:, t, :, d, :],
                           start=True, stop=True)
                last = mm(ps[6][:, 128:256], const("same"), gA.rearrange("p t c -> p (t c)"), start=True, stop=True)
                last.then_inc(*L.mark("cum"))

            def spread_last():
                pe.wait_ge(*L.at("act", "egl"))
                for half in range(2):
                    last = mm(ps[6][:, 256 + 128 * half:384 + 128 * half], const("row", 128 * half, 128),
                              egl.rearrange("p t c -> p (t c)"), start=True, stop=True)
                last.then_inc(*L.mark("eglb"))

            def fm(i):
                kind, j, both = FM[i]
                pe.wait_ge(*L.at("in", f"win{i % 2}", i // 2 + 1))
                if i >= 2:
                    pe.wait_ge(*L.at("act", "pad", i - 2))
                elif i < 2:
                    pe.wait_ge(*L.at("act", "z", 2 + i))
                for k in range(KT):
                    if kind in ("xs", "b", "c"):
                        cols_ = xmT[:, k, 0:768].rearrange("p (a b) -> p a b", a=3)[:, 0:3:2, :] if both else xmT[:, k, 512:768]
                    else:
                        cols_ = xmT[:, k, 0:512] if both else xmT[:, k, 256:512]
                    dst = ps[i % 2][:, 0:512 if both else 256]
                    if both:
                        dst = view(dst, 2, 256)
                        if kind not in ("xs", "b"):
                            cols_ = view(cols_, 2, 256)
                    last = mm(dst, win[:, i % 2, k, :], cols_, start=(k == 0), stop=(k == KT - 1))
                last.then_inc(*L.mark("fm", i))

            def norms():
                for i in range(NKQ):
                    w = 512 if FM[i][2] else 256
                    pe.wait_ge(*L.at("pool", "sq", i))
                    if i >= 2:
                        pe.wait_ge(*L.at("act", "ln", i - 2))
                    bk = ps[2 if i % 2 == 0 else 7]
                    mm(bk[:, 0:w], const("same"), norm_of(i), start=True, stop=True).then_inc(*L.mark("ssq", i))

            def turn(i):
                kind, j, both = FM[i]
                n = TURNED.index(i)
                pe.wait_ge(*(L.at("pool", "kT", i) if kind == "k" else L.at("act", "silu", i)))
                if n >= 2:
                    pe.wait_ge(*L.at("act", "turned", TURNED[n - 2]))
                src = kT[:, j] if kind == "k" else bT[:, j] if kind == "b" else conv[:, i % 2]
                for t in range(NT):
                    last = nc.tensor.transpose(ps[4 + n % 2][:, 128 * t:128 * t + 128], src[:, 128 * t:128 * t + 128], ident)
                last.then_inc(*L.mark("turn", i))

            for i in range(NFM + 1):
                if i < NFM:
                    fm(i)
                if i == 1:
                    cumulate()
                if i == NKQ + 1:
                    norms()
                if i > NKQ and i - 1 in TURNED:
                    turn(i - 1)
                if NKQ + 3 <= i < NKQ + 7:
                    turn(i - NKQ - 3)
                if i == NKQ + 3:
                    spread_last()
                if ADA_AT <= i < ADA_AT + 8:
                    use = i - ADA_AT + 4
                    if use > 4:
                        pe.wait_ge(*L.at("act", "mod", use - 1))
                    else:
                        pe.wait_ge(*L.at("act", "ln", NKQ - 1))
                    ada_chunk(use, 3)
                    pe.wait_ge(*L.at("act", "mod", use))
                    if use > 4:
                        pe.wait_ge(*L.at("dve", "row", use - 1))
                    mm(ps[7], const("rowb"), modq, start=True, stop=True).then_inc(*L.mark("row", use))
            pe.wait_ge(*L.own())
            pe.nop().then_inc(*L.mark("end", "proj"))
            barrier(pe, L, "proj")

            L.stage("delta")
            groups = [(t, hp) for t in range(NT) for hp in range(4)]

            def bank(g, which):
                return ps[4 * (g % 2) + which]

            def unit(b, u):
                return b[:, 128 * u:128 * u + 128]

            def products(g):
                t, hp = groups[g]
                if g >= 2:
                    pe.wait_ge(*L.at("dve", "U", g - 2))
                    pe.wait_ge(*L.at("act", "WT", g - 2))
                for u in range(4):
                    par, d = divmod(u, 2)
                    last = mm(unit(bank(g, 3), u), gA[:, t, d * 8 + 2 * hp + par:d * 8 + 2 * hp + par + 1].broadcast_to([P, P]),
                              tri[:, d], start=True, stop=True)
                last.then_inc(*L.mark("Gb", g))
                for par in range(2):
                    k_ = kT[64 * par:64 * par + 64, hp, 128 * t:128 * t + 128]
                    last = mm(unit(bank(g, par), 0), k_, k_, start=True, stop=True)
                    if t >= 2:
                        last = mm(unit(bank(g, par), 1), k_, qT[64 * par:64 * par + 64, hp, 128 * (t - 2):128 * (t - 2) + 128],
                                  start=True, stop=True)
                last.then_inc(*L.mark("gram", g))

            def first_turn(g):
                pe.wait_ge(*L.at("pool", "X2T", g))
                for u in range(4):
                    last = nc.tensor.transpose(unit(bank(g, 1), u), XT[:, g % 2, u], ident)
                last.then_inc(*L.mark("X2", g))

            def level_a(g, z):
                b = g % 2
                pe.wait_ge(*L.at("act", "X", g, z))
                if z > LEVELS[0]:
                    pe.wait_ge(*L.at("act", "XT", g, z))
                for u in range(4):
                    last = mm(unit(bank(g, 0), u), MT[:, b, u], X[:, b, u], start=True, stop=True)
                last.then_inc(*L.mark("P", g, z))

            def level_b(g, z):
                b = g % 2
                pe.wait_ge(*L.at("dve", "Q", g, z))
                if z < LEVELS[-1]:
                    for u in range(4):
                        last = mm(unit(bank(g, 1), u), XT[:, b, u], Q[:, b, u], start=True, stop=True)
                    last.then_inc(*L.mark("XQ", g, z))
                for u in range(4):
                    last = mm(unit(bank(g, 2), u), Q[:, b, u], XT[:, b, u], start=True, stop=True)
                last.then_inc(*L.mark("QX", g, z))

            def solved(g):
                t, hp = groups[g]
                b = g % 2
                pe.wait_ge(*L.at("act", "XT", g, 64))
                pe.wait_ge(*L.at("pool", "keG", g))
                for u in range(4):
                    par, d = divmod(u, 2)
                    last = mm(bank(g, 1)[64 * par:64 * par + 64, 128 * d:128 * d + 128], keG[:, b, d, par, :], XT[:, b, u],
                              start=True, stop=True)
                last.then_inc(*L.mark("W", g))
                for u in range(4):
                    par, d = divmod(u, 2)
                    head = 2 * hp + par
                    for half in range(2):
                        r = slice(64 * half, 64 * half + 64)
                        last = mm(bank(g, 3)[r, (2 * d + par) * 64:(2 * d + par) * 64 + 64],
                                  XT[r, b, u, 64 * half:64 * half + 64], v_tm[r, t, 64 * head:64 * head + 64],
                                  start=True, stop=True)
                last.then_inc(*L.mark("U", g))

            for g in range(0, 16, 2):
                pair = (g, g + 1)
                for h_ in pair:
                    products(h_)
                for h_ in pair:
                    first_turn(h_)
                for z in LEVELS:
                    for h_ in pair:
                        level_a(h_, z)
                    for h_ in pair:
                        level_b(h_, z)
                for h_ in pair:
                    solved(h_)

            pe.wait_ge(*L.at("act", "WT", 15))
            pe.wait_ge(*L.at("dve", "U", 15))
            for n in range(8):
                sb_ = n % 2
                if n:
                    pe.wait_ge(*L.at("dve", "S", n))
                    for d in range(2):
                        c_ = n if d == 0 else 4 * (n // 4) + 3 - n % 4
                        t, half = divmod(c_, 2)
                        for head in range(H):
                            hp, par = divmod(head, 2)
                            r = slice(64 * par, 64 * par + 64)
                            last = mm(ps[2 * sb_ + par][64 * half:64 * half + 64, 64 * hp:64 * hp + 64],
                                      WT[r, t, hp, d, 64 * half:64 * half + 64],
                                      (S[:, n - 4] if n >= 4 else Sx)[r, (d * 4 + hp) * 64:(d * 4 + hp) * 64 + 64],
                                      start=True, stop=True)
                    last.then_inc(*L.mark("WS", n))
                if n == 7:
                    break
                pe.wait_ge(*L.at("dve", "v", n))
                pe.wait_ge(*L.at("pool", "kdS"))
                for d in range(2):
                    c_ = n if d == 0 else 4 * (n // 4) + 3 - n % 4
                    half = c_ % 2
                    for head in range(H):
                        hp, par = divmod(head, 2)
                        r = slice(64 * half, 64 * half + 64)
                        last = mm(ps[4 + 2 * sb_ + d][64 * par:64 * par + 64, 64 * hp:64 * hp + 64],
                                  kdS[r, n, 64 * head:64 * head + 64],
                                  vS[r, n % 4, 64 * head:64 * head + 64], start=True, stop=True)
                last.then_inc(*L.mark("KV", n))
            pe.wait_ge(*L.at("dve", "v", 7))
            for t in range(2):
                if t:
                    pe.wait_ge(*L.at("dve", "O", 0))
                for half in range(2):
                    r = slice(64 * half, 64 * half + 64)
                    for d in range(2):
                        n = step_of(4 + 2 * t + half, d) - 4
                        for head in range(H):
                            hp, par = divmod(head, 2)
                            rp = slice(64 * par, 64 * par + 64)
                            mm(ps[par][r, (4 * d + hp) * 64:(4 * d + hp) * 64 + 64], qT[rp, hp, 128 * t + 64 * half:128 * t + 64 * half + 64],
                               S[rp, n, (d * 4 + hp) * 64:(d * 4 + hp) * 64 + 64], start=True, stop=True)
                    for head in range(H):
                        hp, par = divmod(head, 2)
                        for d in range(2):
                            n = step_of(4 + 2 * t + half, d) - 4
                            last = mm(ps[4][r, 64 * head:64 * head + 64], attnT[r, t, hp, par, d, 64 * half:64 * half + 64],
                                      vS[r, n, 64 * head:64 * head + 64], start=(d == 0), stop=(d == 1))
                last.then_inc(*L.mark("O", t))
            pe.wait_ge(*L.at("dve", "O", 1))
            pe.wait_ge(*L.own())
            pe.nop().then_inc(*L.mark("end", "delta"))
            barrier(pe, L, "delta")

            L.stage("ssd")
            for t in range(2):
                for g in range(2):
                    last = mm(ps[7][:, (2 * t + g) * 128:(2 * t + g) * 128 + 128], bT[:, g, 256 + 128 * t:384 + 128 * t],
                              cT[:, g, 128 * t:128 * t + 128], start=True, stop=True)
            last.then_inc(*L.mark("cb"))
            for g in range(8):
                t, hp = divmod(g, 4)
                if g >= 2:
                    pe.wait_ge(*L.at("dve", "srel", g - 2))
                for u in range(4):
                    par, d = divmod(u, 2)
                    ch = 16 + d * 8 + 2 * hp + par
                    last = mm(unit(ps[g % 2], u), gA[:, 2 + t, ch:ch + 1].broadcast_to([P, P]), tri[:, d], start=True, stop=True)
                last.then_inc(*L.mark("sG", g))
            for n in range(7):
                pe.wait_ge(*L.at("pool", "xw"))
                for d in range(2):
                    t, half = divmod(n if d == 0 else 4 * (n // 4) + 3 - n % 4, 2)
                    r = slice(64 * half, 64 * half + 64)
                    bk = 2 + 2 * (n % 2) + d
                    if n >= 2:
                        pe.wait_ge(*L.at("dve", "SS", n - 1, d))
                    for g in range(2):
                        last = mm(ps[bk][:, 256 * g:256 * g + 256], b_tm[r, t, 128 * g:128 * g + 128],
                                  xw[r, t, d, 256 * g:256 * g + 256], start=True, stop=True)
                    last.then_inc(*L.mark("BX", n, d))
            pe.wait_ge(*L.at("dve", "SS", 7, 0))
            pe.wait_ge(*L.at("dve", "SS", 7, 1))
            for t in range(2):
                for d in range(2):
                    if t:
                        pe.wait_ge(*L.at("dve", "Y", 0))
                    for half in range(2):
                        n = step_of(4 + 2 * t + half, d) - 4
                        for g in range(2):
                            last = mm(ps[2 + d][64 * half:64 * half + 64, 256 * g:256 * g + 256],
                                      cT[:, g, 128 * t + 64 * half:128 * t + 64 * half + 64],
                                      SS[:, n, d, 256 * g:256 * g + 256], start=True, stop=True)
                pe.wait_ge(*L.at("pool", "sM", 4 * t + 3))
                for head in range(H):
                    last = mm(ps[4][:, 64 * head:64 * head + 64], sMT[:, t, head], xs_tm[:, 2 + t, 64 * head:64 * head + 64],
                              start=True, stop=True)
                last.then_inc(*L.mark("Y", t))
            for n, (m, t) in enumerate(((0, 0), (0, 1), (1, 0), (1, 1))):
                pe.wait_ge(*L.at("pool", "mix", m, t))
                if n >= 2:
                    pe.wait_ge(*L.at("act", "mixT", *((0, 0), (0, 1))[n - 2]))
                for k in range(4):
                    last = nc.tensor.transpose(unit(ps[5 + n % 2], k), mix[:, t, 512 * m + 128 * k:512 * m + 128 * k + 128], ident)
                last.then_inc(*L.mark("mixT", m, t))
            pe.wait_ge(*L.at("act", "mixT", 1, 1))
            pe.wait_ge(*L.at("in", "wout", 1))
            for t in range(2):
                for c_ in range(2):
                    for k in range(KT):
                        last = mm(ps[2 * t + c_], mixT[:, k, 128 * t:128 * t + 128], wout[:, k, 512 * c_:512 * c_ + 512],
                                  start=(k == 0), stop=(k == KT - 1))
                last.then_inc(*L.mark("m", t))
            pe.wait_ge(*L.at("dve", "x1", 1))
            pe.wait_ge(*L.own())
            pe.nop().then_inc(*L.mark("end", "ssd"))
            barrier(pe, L, "ssd")

            L.stage("route")
            for t in range(2):
                pe.wait_ge(*L.at("dve", "h", t))
                for k in range(KT):
                    last = nc.tensor.transpose(unit(ps[4 + 2 * t + k // 4], k % 4), hm[:, t, 128 * k:128 * k + 128], ident)
                last.then_inc(*L.mark("hT", t))
            pe.wait_ge(*L.at("in", "wr", 1))
            for t in range(2):
                pe.wait_ge(*L.at("act", "hT", t))
                for k in range(KT):
                    last = mm(ps[2 * t][:, 0:32], hT[:, k, 128 * t:128 * t + 128], wr[:, k, :],
                              start=(k == 0), stop=(k == KT - 1))
                last.then_inc(*L.mark("logit", t))
            pe.wait_ge(*L.at("dve", "chosen"))
            mm(ps[1][:, 0:32], const("before"), chosen[:, 0], start=True, stop=True)
            mm(ps[1][:, 32:64], const("ones"), chosen[:, 0], start=True, stop=False)
            mm(ps[1][:, 32:64], const("before"), chosen[:, 1], start=False, stop=True)
            mm(ps[1][:, 64:96], const("ones"), chosen[:, 0], start=True, stop=False)
            mm(ps[1][:, 64:96], const("ones"), chosen[:, 1], start=False, stop=True).then_inc(*L.mark("pos"))
            pe.wait_ge(*L.at("dve", "table"))

            def gather():
                for k in range(KT):
                    for n, (s_, t) in enumerate([(s_, t) for s_ in range(3) for t in range(2)]):
                        last = mm(ps[2][:, SLOT * k:SLOT * k + SLOT], hparts[:, s_, t, 128 * k:128 * k + 128], Sb[:, t, :],
                                  start=(n == 0), stop=(n == 5))
                return last

            def scatter():
                for t in range(2):
                    for c_ in range(2):
                        r = slice(64 * c_, 64 * c_ + 64)
                        last = mm(ps[3 + 2 * t + c_], GT[r, t, :], ysb[r, :], start=True, stop=True)
                return last

            pe.wait_ge(*L.at("dve", "Sb1"))
            gather().then_inc(*L.mark("gather1"))
            pe.wait_ge(*L.own())
            pe.wait_ge(*L.at("act", "xcT1"))
            pe.wait_ge(*L.at("dve", "selb1"))
            L.stage("moe")
            pe.sem_inc(*L.open_loop())

            def block_of_rows(turn):
                L.begin_turn(turn)
                pe.wait_ge(*L.at("act", "xcT", back=1))
                pe.wait_ge(*L.at("act", "hidT", back=1))
                pe.wait_ge(*L.at("dve", "hid", back=1))
                pe.wait_ge(*L.at("dve", "selb", back=1))
                for m in range(2):
                    for c_ in range(2):
                        mm(ps[m][64 * c_:64 * c_ + 64, :], selb[0:96, :], bias[0:96, m, 512 * c_:512 * c_ + 512],
                           start=True, stop=False)
                for j in range(4):
                    for m in range(2):
                        pe.wait_ge(sems(f"in_ring{2 * j + m}"), turn * 16)
                        for k in range(2 * j, 2 * j + 2):
                            for c_ in range(2):
                                last = mm(ps[m][64 * c_:64 * c_ + 64, :], xcT[:, k, :], ring[:, 2 * j + m, k % 2, 512 * c_:512 * c_ + 512],
                                          start=False, stop=(k == KT - 1))
                        last.then_inc(*L.mark("piece", 2 * j + m))
                pe.wait_ge(*L.at("act", "y", back=1))
                pe.wait_ge(*L.at("act", "GT", back=1))
                pe.wait_ge(*L.at("dve", "acc", back=1))
                scatter().then_inc(*L.mark("back"))
                pe.wait_ge(*L.at("dve", "Sb"))
                gather().then_inc(*L.mark("gather"))
                pe.wait_ge(*L.at("dve", "Sg"))
                for t in range(2):
                    last = nc.tensor.transpose(ps[7][:, 128 * t:128 * t + 128], Sg[:, t], ident)
                last.then_inc(*L.mark("GT"))
                pe.wait_ge(*L.at("dve", "hid"))
                for k in range(4):
                    last = nc.tensor.transpose(unit(ps[0], k), hid[:, 4, 128 * k:128 * k + 128], ident)
                last.then_inc(*L.mark("hidT"))
                pe.wait_ge(*L.at("act", "hidT"))
                pe.wait_ge(*L.at("act", "xcT"))
                for c_ in range(2):
                    mm(ps[2][64 * c_:64 * c_ + 64, :], selb[0:96, :], bias[0:96, 2, 512 * c_:512 * c_ + 512], start=True, stop=False)
                for j in range(4):
                    pe.wait_ge(sems(f"in_ring{8 + j}"), turn * 16)
                    for k in range(2 * j, 2 * j + 2):
                        for c_ in range(2):
                            last = mm(ps[2][64 * c_:64 * c_ + 64, :], hidT[:, k % 4, 64 * (k // 4):64 * (k // 4) + 64],
                                      ring[:, 8 + j, k % 2, 512 * c_:512 * c_ + 512], start=False, stop=(k == KT - 1))
                    last.then_inc(*L.mark("piece", 8 + j))
                L.end_turn()

            with pe.Fori(1, E_N + 1) as i:
                block_of_rows(i)
            L.turn = None
            n_more = pe.value_load(intab[0:1, 15:16], min_val=0, max_val=MAX_MORE)
            with pe.Fori(0, MAX_MORE) as k:
                with pe.If(n_more > k):
                    block_of_rows(k + E_N + 1)
            L.turn = n_more + E_N + 1
            pe.wait_ge(*L.at("act", "y", back=1))
            pe.wait_ge(*L.at("act", "GT", back=1))
            pe.wait_ge(*L.at("dve", "acc", back=1))
            L.stage("end")
            scatter().then_inc(*L.mark("back1"))

        @block.scalar
        def _(act):
            L = lane("act")
            f = nc.scalar.activation

            def xt_out(L, f, t, n):
                act.wait_ge(*L.at("pe", "xT", t))
                act.wait_ge(*L.at("dve", "a1"))
                j = 0 if t >= 2 else 1
                base = {2: 256, 3: 384, 0: 0, 1: 128}[t]
                for k in range(KT):
                    src = ps[4 + 2 * (n % 2) + k // 4][:, (k % 4) * 128:(k % 4) * 128 + 128]
                    f(xmT[:, k, base:base + 128], src, ACT.Identity, scale=a1[:, k, j:j + 1], bias=modc[:, k, j:j + 1]).then_inc(*L.mark("xmT", t))
    
            def rsqrt_of(L, f, step, t, src, tmp, dst):
                act.wait_ge(*L.at("dve", step, t))
                act.wait_ge(*L.own())
                f(tmp, src, ACT.Ln, scale=1.0 / D, bias=const("eps")).then_inc(*L.mark())
                act.wait_ge(*L.own())
                f(dst, tmp, ACT.Exp, scale=-0.5).then_inc(*L.mark("r1", t))

            L.stage("proj")
            act.wait_ge(*L.at("in", "cc", 1))
            cin = area("sc", 0, 16)
            f(newt[:, 0, :], cin, ACT.Exp, scale=-1.0).then_inc(*L.mark("ec"))
            act.wait_ge(*L.at("in", "small", 1))
            f(nega, a_log, ACT.Exp).then_inc(*L.mark("eA"))
            for t in (2, 3, 0, 1):
                if t >= 2:
                    act.wait_ge(*L.at("in", "x", 1))
                    src = xin[:, t - 2]
                else:
                    act.wait_ge(*L.at("in", "ctx", 1))
                    src = ctx_in[:, t]
                act.wait_ge(*L.own())
                f(area("conv"), src, ACT.Square, accum_out=ssq[:, t:t + 1]).then_inc(*L.mark("ssq", t))
                act.wait_ge(*L.own())
                act.wait_ge(*L.at("in", "const", 1))
                f(ssq[:, 4 + t:5 + t], ssq[:, t:t + 1], ACT.Ln, scale=1.0 / D, bias=const("eps")).then_inc(*L.mark())
                act.wait_ge(*L.own())
                f(ssq[:, 8 + t:9 + t], ssq[:, 4 + t:5 + t], ACT.Exp, scale=-0.5).then_inc(*L.mark("rstd0", t))
                if t == 2:
                    for use in range(4):
                        act.wait_ge(*L.at("pe", "ada", use))
                        f(modp[:, 512 * use:512 * use + 512], ps[use % 2][:, :], ACT.Copy).then_inc(*L.mark("mod", use))
                if t != 2:
                    n = (3, 0, 1).index(t)
                    xt_out(L, f, (2, 3, 0)[n], n)
            xt_out(L, f, 1, 3)
            act.wait_ge(*L.at("pe", "sm"))
            f(sm.rearrange("p a b -> p (a b)"), ps[3][:, 0:192], ACT.Copy).then_inc(*L.mark("sm"))
            act.wait_ge(*L.own())
            f(beta, sm[:, :, 0:16], ACT.Exp, scale=-1.0).then_inc(*L.mark("eb"))
            act.wait_ge(*L.at("dve", "absy"))
            f(tsp[:, 0], tsp[:, 0], ACT.Exp, scale=-1.0).then_inc(*L.mark("u"))
            act.wait_ge(*L.at("dve", "1+u"))
            f(tsp[:, 2], tsp[:, 1], ACT.Ln).then_inc(*L.mark("lnw"))
            for m in range(2):
                for t in range(2):
                    act.wait_ge(*L.at("pe", "zt", m, t))
                    f(zs[:, 2 * m + t], ps[t][:, :], ACT.Silu).then_inc(*L.mark("z", 2 * m + t))

            def silu_of(i):
                kind, j, both = FM[i]
                w = 512 if both else 256
                act.wait_ge(*L.at("dve", "conv", i))
                dst = {"k": kT, "q": qT, "b": bT, "c": cT}[kind][:, j] if kind in "kqbc" else conv[:, i % 2, 0:w]
                f(dst, conv[:, i % 2, 0:w], ACT.Silu).then_inc(*L.mark("silu", i))

            def turned_of(i):
                kind, j, both = FM[i]
                n = TURNED.index(i)
                act.wait_ge(*L.at("pe", "turn", i))
                dst = {"k": k_tm, "v": v_tm, "xs": xs_tm, "b": b_tm}[kind][:, :, 128 * j:128 * j + 128]
                f(dst, view(ps[4 + n % 2][:, :], 4, 128), ACT.Copy).then_inc(*L.mark("turned", i))

            for i in range(NFM + 1):
                if i < NFM:
                    kind, j, both = FM[i]
                    act.wait_ge(*L.at("pe", "fm", i))
                    act.wait_ge(*(L.at("dve", "padz") if i < 2 else L.at("dve", "conv", i - 2)))
                    w = 2 if both else 1
                    f(pad[:, i % 2, 0:w, 2:258], view(ps[i % 2][:, 0:256 * w], w, 256) if both
                      else ps[i % 2][:, 0:256].rearrange("p (a b) -> p a b", a=1), ACT.Copy).then_inc(*L.mark("pad", i))
                    silu_of(i)
                if i == NKQ + 1:
                    for m in range(NKQ):
                        act.wait_ge(*L.at("pe", "ssq", m))
                        bk = ps[2 if m % 2 == 0 else 7]
                        f(norm_of(m), bk[:, 0:512 if FM[m][2] else 256], ACT.Ln, bias=const("eps")).then_inc(*L.mark("ln", m))
                    act.wait_ge(*L.own())
                    for m in range(NKQ):
                        f(norm_of(m), norm_of(m), ACT.Exp, scale=-0.5,
                          bias=const("lnq") if FM[m][0] == "q" else const("zero")).then_inc(*L.mark("rn", m))
                    act.wait_ge(*L.at("dve", "Gc"))
                    f(eG, Gc, ACT.Exp).then_inc(*L.mark("eG"))
                    f(egl, gl, ACT.Exp).then_inc(*L.mark("egl"))
                    act.wait_ge(*L.at("dve", "gl-G"))
                    f(ekd, ekd, ACT.Exp).then_inc(*L.mark("ekd"))
                if i > NKQ and i - 1 in TURNED:
                    turned_of(i - 1)
                if NKQ + 3 <= i < NKQ + 7:
                    turned_of(i - NKQ - 3)
                if ADA_AT <= i < ADA_AT + 8:
                    use = i - ADA_AT + 4
                    act.wait_ge(*L.at("pe", "ada", use))
                    if use > 4:
                        act.wait_ge(*L.at("pe", "row", use - 1))
                    f(modq, ps[3][:, :], ACT.Copy).then_inc(*L.mark("mod", use))
            act.wait_ge(*L.own())
            act.nop().then_inc(*L.mark("end", "proj"))
            barrier(act, L, "proj")

            L.stage("delta")
            groups = [(t, hp) for t in range(NT) for hp in range(4)]

            def bank(g, which):
                return ps[4 * (g % 2) + which]

            for g in range(0, 16, 2):
                pair = (g, g + 1)
                for h_ in pair:
                    act.wait_ge(*L.at("dve", "rel", h_))
                    f(DT[:, h_ % 2], DT[:, h_ % 2], ACT.Exp).then_inc(*L.mark("DT", h_))
                for h_ in pair:
                    act.wait_ge(*L.at("pe", "X2", h_))
                    act.wait_ge(*L.own())
                    f(X[:, h_ % 2], view(bank(h_, 1)[:, :], 4, 128), ACT.Copy).then_inc(*L.mark("X", h_, LEVELS[0]))
                for z in LEVELS:
                    for h_ in pair:
                        if z < LEVELS[-1]:
                            act.wait_ge(*L.at("pe", "XQ", h_, z))
                            act.wait_ge(*L.own())
                            f(X[:, h_ % 2], view(bank(h_, 1)[:, :], 4, 128), ACT.Copy).then_inc(*L.mark("X", h_, 2 * z))
                        act.wait_ge(*L.at("pe", "QX", h_, z))
                        act.wait_ge(*L.own())
                        f(XT[:, h_ % 2], view(bank(h_, 2)[:, :], 4, 128), ACT.Copy).then_inc(*L.mark("XT", h_, 2 * z))
                for h_ in pair:
                    t, hp = groups[h_]
                    act.wait_ge(*L.at("pe", "W", h_))
                    f(WT[:, t, hp], view(bank(h_, 1)[:, 0:256], 2, 128), ACT.Copy, scale=-1.0).then_inc(*L.mark("WT", h_))
            act.wait_ge(*L.own())
            for t in range(2):
                act.wait_ge(*L.at("dve", "Oss", t))
                f(ssq[:, 8 * t:8 * t + 8], ngrp[:, t, 0:8], ACT.Ln, scale=1.0 / C, bias=const("eps")).then_inc(*L.mark())
                act.wait_ge(*L.own())
                f(ngrp[:, t, 8:16], ssq[:, 8 * t:8 * t + 8], ACT.Exp, scale=-0.5).then_inc(*L.mark("Or", t))
            act.wait_ge(*L.own())
            act.wait_ge(*L.own())
            act.nop().then_inc(*L.mark("end", "delta"))
            barrier(act, L, "delta")

            L.stage("ssd")
            for g in range(8):
                act.wait_ge(*L.at("dve", "srel", g))
                f(sDT[:, g % 2], sDT[:, g % 2], ACT.Exp).then_inc(*L.mark("sDT", g))
            for t in range(2):
                act.wait_ge(*L.at("dve", "Yss", t))
                act.wait_ge(*L.own())
                f(ssq[:, 4 * t:4 * t + 2], ngrp[:, t, 0:2], ACT.Ln, scale=1.0 / 256, bias=const("eps")).then_inc(*L.mark())
                act.wait_ge(*L.own())
                f(ngrp[:, t, 2:4], ssq[:, 4 * t:4 * t + 2], ACT.Exp, scale=-0.5).then_inc(*L.mark("Yr", t))
            for n, (m, t) in enumerate(((0, 0), (0, 1), (1, 0), (1, 1))):
                act.wait_ge(*L.at("pe", "mixT", m, t))
                src = view(ps[5 + n % 2][:, :], 4, 128)
                if m == 0:
                    f(mixT[:, 0:4, 128 * t:128 * t + 128], src, ACT.Copy).then_inc(*L.mark("mixT", m, t))
                else:
                    for k in range(4):
                        dst = mixT[:, 4 + k, :].rearrange("p (r w) -> p w r", r=ROWS)[:, 32 * t:32 * t + 32, :]
                        f(dst, src[:, k].rearrange("p (w r) -> p w r", r=ROWS), ACT.Copy).then_inc(*L.mark("mixT", m, t))
            for t in range(2):
                act.wait_ge(*L.at("pe", "m", t))
                for c_ in range(2):
                    act.wait_ge(*L.own())
                    f(area("yt", 0, 512), ps[2 * t + c_][:, :], ACT.Square, accum_out=newt[:, t, c_:c_ + 1]).then_inc(*L.mark("mss", t))
            for t in range(2):
                rsqrt_of(L, f, "msum", t, newt[:, t, 2:3], newt[:, t, 3:4], newt[:, t, 4:5])
            act.wait_ge(*L.own())
            act.nop().then_inc(*L.mark("end", "ssd"))
            barrier(act, L, "ssd")

            L.stage("route")
            for t in range(2):
                act.wait_ge(*L.at("dve", "x1", t))
                act.wait_ge(*L.own())
                f(area("hT", 0, D), xin[:, t], ACT.Square, accum_out=newt[:, t, 5:6]).then_inc(*L.mark())
                act.wait_ge(*L.own())
                f(newt[:, t, 6:7], newt[:, t, 5:6], ACT.Ln, scale=1.0 / D, bias=const("eps")).then_inc(*L.mark())
                act.wait_ge(*L.own())
                f(newt[:, t, 7:8], newt[:, t, 6:7], ACT.Exp, scale=-0.5).then_inc(*L.mark("r2", t))
            for t in range(2):
                act.wait_ge(*L.at("pe", "hT", t))
                act.wait_ge(*L.own())
                for c_ in range(2):
                    f(hT[:, 4 * c_:4 * c_ + 4, 128 * t:128 * t + 128], view(ps[4 + 2 * t + c_][:, :], 4, 128), ACT.Copy).then_inc(*L.mark("hT", t))
            for t in range(2):
                act.wait_ge(*L.at("dve", "nmax", t))
                f(gexp[:, t], top[:, t, 0:4], ACT.Exp, bias=nmax[:, t], accum_out=gsum[:, t]).then_inc(*L.mark("gexp", t))
            act.wait_ge(*L.at("pe", "gather1"))
            f(xcT, view(ps[2][:, :], KT, SLOT), ACT.Copy).then_inc(*L.mark("xcT1"))
            act.wait_ge(*L.at("dve", "table"))
            act.wait_ge(*L.own())
            L.stage("moe")
            act.sem_inc(*L.open_loop())

            def block_of_rows(turn):
                L.begin_turn(turn)
                act.wait_ge(*L.at("dve", "a"))
                act.wait_ge(*L.at("dve", "hid", back=1))
                f(hid[:, 1], hid[:, 0], ACT.Sigmoid, scale=ALPHA).then_inc(*L.mark("sig"))
                act.wait_ge(*L.at("pe", "gather"))
                f(xcT, view(ps[2][:, :], KT, SLOT), ACT.Copy).then_inc(*L.mark("xcT"))
                act.wait_ge(*L.at("pe", "GT"))
                f(GT, view(ps[7][:, 0:256], 2, 128), ACT.Copy).then_inc(*L.mark("GT"))
                act.wait_ge(*L.at("pe", "hidT"))
                f(hidT, view(ps[0][:, :], 4, 128), ACT.Copy).then_inc(*L.mark("hidT"))
                act.wait_ge(*L.at("pe", "piece", 11))
                f(ysb, ps[2][:, :], ACT.Copy).then_inc(*L.mark("y"))
                L.end_turn()

            with act.Fori(1, E_N + 1) as i:
                block_of_rows(i)
            L.turn = None
            n_more = act.value_load(intab[0:1, 15:16], min_val=0, max_val=MAX_MORE)
            with act.Fori(0, MAX_MORE) as k:
                with act.If(n_more > k):
                    block_of_rows(k + E_N + 1)
            L.stage("end")
            for t in range(2):
                act.wait_ge(*L.at("dve", "sum", t))
                act.wait_ge(*L.own())
                f(area("hid", 0, D), acc[:, t], ACT.Square, accum_out=newt[:, t, 8:9]).then_inc(*L.mark())
                act.wait_ge(*L.own())
                f(newt[:, t, 9:10], newt[:, t, 8:9], ACT.Ln, scale=1.0 / D, bias=const("eps")).then_inc(*L.mark())
                act.wait_ge(*L.own())
                f(newt[:, t, 10:11], newt[:, t, 9:10], ACT.Exp, scale=-0.5).then_inc(*L.mark("r3", t))

        @block.vector
        def _(dve):
            L = lane("dve")
            v = nc.vector

            def refine(y, ms, tmp, scale):
                dve.wait_ge(*L.own())
                v.tensor_scalar(tmp[:, 0:1], ms, scale, EPS, ALU.mult, ALU.add).then_inc(*L.mark())
                dve.wait_ge(*L.own())
                v.tensor_tensor(tmp[:, 0:1], tmp[:, 0:1], y, ALU.mult).then_inc(*L.mark())
                dve.wait_ge(*L.own())
                v.tensor_tensor(tmp[:, 0:1], tmp[:, 0:1], y, ALU.mult).then_inc(*L.mark())
                dve.wait_ge(*L.own())
                v.tensor_scalar(tmp[:, 0:1], tmp[:, 0:1], -0.5, 1.5, ALU.mult, ALU.add).then_inc(*L.mark())
                dve.wait_ge(*L.own())
                v.tensor_tensor(tmp[:, 1:2], tmp[:, 0:1], y, ALU.mult).then_inc(*L.mark())
                dve.wait_ge(*L.own())
                return tmp[:, 1:2]

            L.stage("proj")
            v.memset(pad.rearrange("p a b c -> p (a b c)"), 0.0).then_inc(*L.mark("padz"))
            dve.wait_ge(*L.at("act", "ec"))
            v.tensor_scalar(newt[:, 0, :], newt[:, 0, :], 1.0, None, ALU.add).then_inc(*L.mark())
            dve.wait_ge(*L.own())
            v.reciprocal(newt[:, 0, :], newt[:, 0, :]).then_inc(*L.mark())
            dve.wait_ge(*L.own())
            dve.wait_ge(*L.at("in", "cc", 1))
            v.tensor_tensor(newt[:, 1, :], area("sc", 0, 16), newt[:, 0, :], ALU.mult).then_inc(*L.mark())
            dve.wait_ge(*L.own())
            v.memset(area("sc"), 0.0).then_inc(*L.mark())
            dve.wait_ge(*L.own())
            v.tensor_copy(sct[:, :, 0:2], newt[:, 1, :].rearrange("p (k j) -> p k j", j=2)).then_inc(*L.mark("sct"))
            dve.wait_ge(*L.at("act", "eA"))
            v.tensor_scalar(nega, nega, -1.0, None, ALU.mult).then_inc(*L.mark())
            for n, t in enumerate((2, 3, 0, 1)):
                dve.wait_ge(*L.at("act", "rstd0", t))
                r = refine(ssq[:, 8 + t:9 + t], ssq[:, t:t + 1], newt[:, 2, 2 * t:2 * t + 2], 1.0 / D)
                if n:
                    dve.wait_ge(*L.at("pe", "xT", (2, 3, 0, 1)[n - 1]))
                if t >= 2:
                    v.tensor_scalar(xh, xin[:, t - 2], r, None, ALU.mult).then_inc(*L.mark("xh", t))
                else:
                    dve.wait_ge(*L.at("in", "ctx", 1))
                    v.tensor_scalar(xh, ctx_in[:, t], r, None, ALU.mult).then_inc(*L.mark("xh", t))
                if n == 0:
                    dve.wait_ge(*L.at("pe", "modc"))
                    v.tensor_copy(modc, view(ps[2][:, 0:32], 16, 2)).then_inc(*L.mark())
                    dve.wait_ge(*L.own())
                    dve.wait_ge(*L.at("in", "cols", 1))
                    for j in range(2):
                        v.scalar_tensor_tensor(out=a1[:, :, j], in0=modc[:, 8:16, j], scalar=1.0, in1=npm,
                                                     op0=ALU.add, op1=ALU.mult).then_inc(*L.mark("a1"))
            dve.wait_ge(*L.at("act", "eb"))
            v.tensor_scalar(beta, beta, 1.0, None, ALU.add).then_inc(*L.mark())
            dve.wait_ge(*L.own())
            v.reciprocal(beta, beta).then_inc(*L.mark())
            for t in range(NT):
                v.tensor_tensor(sp_[:, t], sm[:, t, 16:48], dt_b, ALU.add).then_inc(*L.mark())
            dve.wait_ge(*L.own())
            v.scalar_tensor_tensor(out=tsp[:, 0], in0=sp_, scalar=-1.0, in1=sp_, op0=ALU.mult, op1=ALU.max).then_inc(*L.mark("absy"))
            dve.wait_ge(*L.at("act", "u"))
            v.tensor_scalar(tsp[:, 1], tsp[:, 0], 1.0, None, ALU.add).then_inc(*L.mark("1+u"))
            dve.wait_ge(*L.own())
            dve.wait_ge(*L.at("act", "lnw"))
            v.tensor_scalar(tsp[:, 1], tsp[:, 1], -1.0, None, ALU.add).then_inc(*L.mark())
            dve.wait_ge(*L.own())
            v.tensor_scalar(gA, tsp[:, 1], 0.0, None, ALU.is_equal).then_inc(*L.mark())
            dve.wait_ge(*L.own())
            v.tensor_tensor(tsp[:, 1], tsp[:, 1], gA, ALU.add).then_inc(*L.mark())
            dve.wait_ge(*L.own())
            v.reciprocal(tsp[:, 1], tsp[:, 1]).then_inc(*L.mark())
            dve.wait_ge(*L.own())
            v.tensor_tensor(tsp[:, 1], tsp[:, 1], tsp[:, 2], ALU.mult).then_inc(*L.mark())
            dve.wait_ge(*L.own())
            v.tensor_tensor(tsp[:, 1], tsp[:, 1], gA, ALU.add).then_inc(*L.mark())
            dve.wait_ge(*L.own())
            v.tensor_tensor(tsp[:, 1], tsp[:, 1], tsp[:, 0], ALU.mult).then_inc(*L.mark())
            dve.wait_ge(*L.own())
            v.scalar_tensor_tensor(out=sp_, in0=sp_, scalar=0.0, in1=tsp[:, 1], op0=ALU.max, op1=ALU.add).then_inc(*L.mark())
            dve.wait_ge(*L.own())
            for t in range(NT):
                v.tensor_tensor(gA[:, t], sp_[:, t], nega, ALU.mult).then_inc(*L.mark("gA"))
            def conv_of(i):
                kind, j, both = FM[i]
                n, w = (512, 2) if both else (256, 1)
                wi = {"q": 0, "k": 4, "v": 8, "xs": 12, "b": 16, "c": 18}[kind] + j
                dve.wait_ge(*L.at("act", "pad", i))
                if i >= 2:
                    dve.wait_ge(*(L.at("pe", "turn", i - 2) if FM[i - 2][0] in ("v", "xs") else L.at("act", "silu", i - 2)))
                dst = conv[:, i % 2, 0:n].rearrange("p (a b) -> p a b", a=w)
                for tap in range(5):
                    src = pad[:, i % 2, 0:w, tap:tap + 256]
                    if tap == 0:
                        if wi >= 12:
                            v.tensor_scalar(dst, src, convw[:, wi, 0:1], convb[:, wi - 12:wi - 11], ALU.mult, ALU.add).then_inc(*L.mark())
                        else:
                            v.tensor_scalar(dst, src, convw[:, wi, 0:1], None, ALU.mult).then_inc(*L.mark())
                    else:
                        dve.wait_ge(*L.own())
                        v.scalar_tensor_tensor(out=dst, in0=src, scalar=convw[:, wi, tap:tap + 1], in1=dst,
                                                     op0=ALU.mult, op1=ALU.add).then_inc(*L.mark("conv", i))

            def row_out(use):
                dve.wait_ge(*L.at("in", "wrow", 1))
                dve.wait_ge(*L.at("pe", "row", use))
                which, c_ = divmod(use - 4, 2)
                r = slice(512 * c_, 512 * c_ + 512)
                src = ps[7][:, :]
                if which == 0:
                    v.tensor_tensor(rows[:, 0, r], src, rows[:, 0, r], ALU.mult).then_inc(*L.mark("row", use))
                elif which == 1:
                    v.tensor_copy(rows[:, 3, r], src).then_inc(*L.mark("row", use))
                elif which == 2:
                    v.scalar_tensor_tensor(out=rows[:, 1, r], in0=src, scalar=1.0, in1=rows[:, 1, r],
                                                 op0=ALU.add, op1=ALU.mult).then_inc(*L.mark("row", use))
                else:
                    v.tensor_tensor(rows[:, 2, r], src, rows[:, 2, r], ALU.mult).then_inc(*L.mark("row", use))

            for i in range(NFM + 1):
                if i < NFM:
                    conv_of(i)
                if ADA_AT <= i < ADA_AT + 8:
                    row_out(i - ADA_AT + 4)
                if i == 1:
                    dve.wait_ge(*L.at("pe", "cum"))
                    for d in range(2):
                        for t in range(NT):
                            v.tensor_copy(Gc[:, t].rearrange("p (k d h) -> p k d h", k=2, d=2)[:, :, d, :],
                                                view(ps[6][:, d * 64 + t * 16:d * 64 + t * 16 + 16], 2, 8)).then_inc(*L.mark())
                    v.tensor_copy(gl, view(ps[6][:, 128:256], 4, 32)).then_inc(*L.mark("Gc"))
                    dve.wait_ge(*L.own())
                    v.tensor_tensor(ekd, gl, Gc, ALU.subtract).then_inc(*L.mark("gl-G"))
                if i == NKQ + 3:
                    dve.wait_ge(*L.at("pe", "eglb"))
                    v.tensor_copy(eglb.rearrange("p a b c -> p (a b c)"), ps[6][:, 256:512]).then_inc(*L.mark("eglb"))
            dve.wait_ge(*L.own())
            dve.nop().then_inc(*L.mark("end", "proj"))
            barrier(dve, L, "proj")

            L.stage("delta")
            groups = [(t, hp) for t in range(NT) for hp in range(4)]

            def bank(g, which):
                return ps[4 * (g % 2) + which]

            def decay(g):
                t, hp = groups[g]
                dve.wait_ge(*L.at("pe", "Gb", g))
                if g >= 2:
                    dve.wait_ge(*L.at("pool", "unit", g - 2))
                for u in range(4):
                    par, d = divmod(u, 2)
                    ch = d * 8 + 2 * hp + par
                    v.scalar_tensor_tensor(out=DT[:, g % 2, u], in0=bank(g, 3)[:, 128 * u:128 * u + 128],
                                                 scalar=Gc[:, t, ch:ch + 1], in1=neg[:, d], op0=ALU.subtract, op1=ALU.min).then_inc(*L.mark("rel", g))

            def couple(g):
                t, hp = groups[g]
                dve.wait_ge(*L.at("pe", "gram", g))
                dve.wait_ge(*L.at("act", "DT", g))
                if g >= 2:
                    dve.wait_ge(*L.at("pe", "P", g - 2, LEVELS[-1]))
                for u in range(4):
                    par, d = divmod(u, 2)
                    ch = d * 8 + 2 * hp + par
                    v.scalar_tensor_tensor(out=MT[:, g % 2, u], in0=bank(g, par)[:, 0:128],
                                                 scalar=beta[:, t, ch:ch + 1], in1=DT[:, g % 2, u], op0=ALU.mult, op1=ALU.mult).then_inc(*L.mark("N", g))
                if t >= 2:
                    for par in range(2):
                        for d in range(2):
                            v.tensor_tensor(attnT[:, t - 2, hp, par, d], bank(g, par)[:, 128:256],
                                                  DT[:, g % 2, 2 * par + d], ALU.mult).then_inc(*L.mark("N", g))

            def level(g, z):
                dve.wait_ge(*L.at("pe", "P", g, z))
                dve.wait_ge(*L.own())
                zi = LEVELS.index(z)
                for par in range(2):
                    v.tensor_tensor(Q[:, g % 2, 2 * par:2 * par + 2], view(bank(g, 0)[:, 256 * par:256 * par + 256], 2, 128),
                                          qmask[:, zi], ALU.mult).then_inc(*L.mark("Q", g, z))

            def u_out(g):
                t, hp = groups[g]
                dve.wait_ge(*L.at("pe", "U", g))
                for d in range(2):
                    for half in range(2):
                        n = step_of(2 * t + half, d)
                        r = slice(64 * half, 64 * half + 64)
                        v.tensor_copy(US[r, n, 128 * hp:128 * hp + 128], bank(g, 3)[r, 128 * d:128 * d + 128]).then_inc(*L.mark("U", g))

            for g in range(0, 16, 2):
                pair = (g, g + 1)
                for h_ in pair:
                    decay(h_)
                for h_ in pair:
                    couple(h_)
                for z in LEVELS:
                    for h_ in pair:
                        level(h_, z)
                for h_ in pair:
                    u_out(h_)
            dve.wait_ge(*L.at("pool", "betaS"))
            for n in range(8):
                vn = vS[:, n % 4]
                bb = betaS[:, n].unsqueeze(2).broadcast_to([P, H, C])
                if n:
                    dve.wait_ge(*L.at("pe", "WS", n))
                    if n >= 4:
                        dve.wait_ge(*L.at("pe", "KV", n - 4))
                    dve.wait_ge(*L.own())
                    for par in range(2):
                        u_ = US[:, n].rearrange("p (a b c) -> p a b c", a=4, b=2)[:, :, par, :]
                        v.tensor_tensor(u_, u_, view(ps[2 * (n % 2) + par][:, 0:256], 4, C), ALU.add).then_inc(*L.mark())
                dve.wait_ge(*L.own())
                v.tensor_tensor(view(vn, H, C), view(US[:, n], H, C), bb, ALU.mult).then_inc(*L.mark("v", n))
                if n == 7:
                    break
                nxt = S[:, n + 1 - 4] if n + 1 >= 4 else Sx
                dve.wait_ge(*L.at("pe", "KV", n))
                dve.wait_ge(*L.own())
                if n == 0:
                    for d in range(2):
                        v.tensor_copy(nxt[:, 256 * d:256 * d + 256], ps[4 + d][:, 0:256]).then_inc(*L.mark("S", 1))
                else:
                    dve.wait_ge(*L.at("pool", "Se", n))
                    for d in range(2):
                        c_ = slice(256 * d, 256 * d + 256)
                        v.tensor_tensor(nxt[:, c_], US[:, n, c_], ps[4 + 2 * (n % 2) + d][:, 0:256], ALU.add).then_inc(*L.mark("S", n + 1))
            O = view(area("DT"), 2, 512)
            for t in range(2):
                dve.wait_ge(*L.at("pe", "O", t))
                dve.wait_ge(*L.own())
                o_, tmp = O[:, t], area("MT", 512 * t, 512)
                for d in range(2):
                    for par in range(2):
                        e_ = eG[:, 2 + t, 8 * d + par:8 * d + 8:2].unsqueeze(2).broadcast_to([P, 4, C])
                        dst = (o_ if d == 0 else tmp).rearrange("p (a b c) -> p a b c", a=4, b=2)[:, :, par, :]
                        v.tensor_tensor(dst, view(ps[par][:, 256 * d:256 * d + 256], 4, C), e_, ALU.mult).then_inc(*L.mark())
                dve.wait_ge(*L.own())
                v.tensor_tensor(o_, o_, tmp, ALU.add).then_inc(*L.mark())
                dve.wait_ge(*L.own())
                v.tensor_tensor(o_, o_, ps[4][:, :], ALU.add).then_inc(*L.mark("O", t))
                dve.wait_ge(*L.own())
                v.tensor_tensor(tmp, o_, o_, ALU.mult).then_inc(*L.mark())
                dve.wait_ge(*L.own())
                v.tensor_reduce(ngrp[:, t, 0:8], view(tmp, H, C), AX.X, ALU.add).then_inc(*L.mark("Oss", t))
            for t in range(2):
                o_ = O[:, t]
                dve.wait_ge(*L.at("act", "Or", t))
                dve.wait_ge(*L.own())
                v.tensor_tensor(view(o_, H, C), view(o_, H, C), ngrp[:, t, 8:16].unsqueeze(2).broadcast_to([P, H, C]), ALU.mult).then_inc(*L.mark())
                dve.wait_ge(*L.own())
                v.tensor_tensor(view(o_, H, C), view(o_, H, C), gnw.unsqueeze(1).broadcast_to([P, H, C]), ALU.mult).then_inc(*L.mark())
                dve.wait_ge(*L.own())
                v.tensor_tensor(zs[:, t], o_, zs[:, t], ALU.mult).then_inc(*L.mark("gdn", t))
            dve.wait_ge(*L.own())
            dve.nop().then_inc(*L.mark("end", "delta"))
            barrier(dve, L, "delta")

            L.stage("ssd")
            for g in range(8):
                t, hp = divmod(g, 4)
                dve.wait_ge(*L.at("pe", "sG", g))
                if g >= 2:
                    dve.wait_ge(*L.at("pool", "sM", g - 2))
                for u in range(4):
                    par, d = divmod(u, 2)
                    ch = 16 + d * 8 + 2 * hp + par
                    v.scalar_tensor_tensor(out=sDT[:, g % 2, u], in0=ps[g % 2][:, 128 * u:128 * u + 128],
                                                 scalar=Gc[:, 2 + t, ch:ch + 1], in1=neg[:, d], op0=ALU.subtract, op1=ALU.min).then_inc(*L.mark("srel", g))
                dve.wait_ge(*L.at("act", "sDT", g))
                dve.wait_ge(*L.at("pe", "cb"))
                for u in range(4):
                    par, d = divmod(u, 2)
                    ch = 16 + d * 8 + 2 * hp + par
                    grp = (2 * hp + par) // 4
                    v.scalar_tensor_tensor(out=sDT[:, g % 2, u], in0=ps[7][:, (2 * t + grp) * 128:(2 * t + grp) * 128 + 128],
                                                 scalar=sp_[:, 2 + t, ch:ch + 1], in1=sDT[:, g % 2, u], op0=ALU.mult, op1=ALU.mult).then_inc(*L.mark("smt", g))
            for n in range(7):
                for d in range(2):
                    dve.wait_ge(*L.at("pe", "BX", n, d))
                    dst = SS[:, n - 3, d] if n >= 3 else SSt[:, d]
                    dve.wait_ge(*L.own())
                    if n == 0:
                        v.tensor_copy(dst, ps[2 + d][:, :]).then_inc(*L.mark("SS", 1, d))
                    else:
                        dve.wait_ge(*L.at("pool", "SSe", n, d))
                        v.tensor_tensor(dst, dst, ps[2 + 2 * (n % 2) + d][:, :], ALU.add).then_inc(*L.mark("SS", n + 1, d))
            for t in range(2):
                dve.wait_ge(*L.at("pe", "Y", t))
                for d in range(2):
                    e_ = eG[:, 2 + t, 16 + 8 * d:24 + 8 * d].unsqueeze(2).broadcast_to([P, H, C])
                    v.tensor_tensor(view(yt[:, 2 * t + d], H, C), view(ps[2 + d][:, :], H, C), e_, ALU.mult).then_inc(*L.mark())
                dve.wait_ge(*L.own())
                y_ = yt[:, 2 * t]
                v.tensor_tensor(y_, y_, yt[:, 2 * t + 1], ALU.add).then_inc(*L.mark())
                dve.wait_ge(*L.own())
                v.tensor_tensor(y_, y_, ps[4][:, :], ALU.add).then_inc(*L.mark("Y", t))
                v.tensor_tensor(view(yt[:, 2 * t + 1], H, C), view(xs_tm[:, 2 + t], H, C),
                                      dskip.unsqueeze(2).broadcast_to([P, H, C]), ALU.mult).then_inc(*L.mark())
                dve.wait_ge(*L.own())
                v.tensor_tensor(y_, y_, yt[:, 2 * t + 1], ALU.add).then_inc(*L.mark())
                dve.wait_ge(*L.own())
                v.tensor_tensor(y_, y_, zs[:, 2 + t], ALU.mult).then_inc(*L.mark())
                dve.wait_ge(*L.own())
                v.tensor_tensor(yt[:, 2 * t + 1], y_, y_, ALU.mult).then_inc(*L.mark())
                dve.wait_ge(*L.own())
                v.tensor_reduce(ngrp[:, t, 0:2], view(yt[:, 2 * t + 1], 2, 256), AX.X, ALU.add).then_inc(*L.mark("Yss", t))
            for t in range(2):
                dve.wait_ge(*L.at("act", "Yr", t))
                dve.wait_ge(*L.own())
                for g in range(2):
                    v.tensor_scalar(yt[:, 2 * t, 256 * g:256 * g + 256], yt[:, 2 * t, 256 * g:256 * g + 256],
                                          ngrp[:, t, 2 + g:3 + g], None, ALU.mult).then_inc(*L.mark("yn", t))
            for t in range(2):
                dve.wait_ge(*L.at("act", "mss", t))
                dve.wait_ge(*L.own())
                v.tensor_tensor(newt[:, t, 2:3], newt[:, t, 0:1], newt[:, t, 1:2], ALU.add).then_inc(*L.mark("msum", t))
            for t in range(2):
                dve.wait_ge(*L.at("act", "r1", t))
                r = refine(newt[:, t, 4:5], newt[:, t, 2:3], newt[:, t, 11:13], 1.0 / D)
                if t == 0:
                    for tt in range(2):
                        dve.wait_ge(*L.at("pe", "m", tt))
                for c_ in range(2):
                    s_ = slice(512 * c_, 512 * c_ + 512)
                    v.scalar_tensor_tensor(out=mix[:, t, s_], in0=ps[2 * t + c_][:, :], scalar=r, in1=rows[:, 0, s_],
                                                 op0=ALU.mult, op1=ALU.mult).then_inc(*L.mark())
                dve.wait_ge(*L.own())
                v.tensor_tensor(xin[:, t], mix[:, t], xin[:, t], ALU.add).then_inc(*L.mark("x1", t))
            dve.wait_ge(*L.own())
            dve.nop().then_inc(*L.mark("end", "ssd"))
            barrier(dve, L, "ssd")

            L.stage("route")
            v.memset(acc.rearrange("p a b -> p (a b)"), 0.0).then_inc(*L.mark())
            for t in range(2):
                dve.wait_ge(*L.at("act", "r2", t))
                r = refine(newt[:, t, 7:8], newt[:, t, 5:6], newt[:, t, 11:13], 1.0 / D)
                v.scalar_tensor_tensor(out=hm[:, t], in0=xin[:, t], scalar=r, in1=rows[:, 1], op0=ALU.mult, op1=ALU.mult).then_inc(*L.mark())
                dve.wait_ge(*L.own())
                v.tensor_tensor(hm[:, t], hm[:, t], rows[:, 3], ALU.add).then_inc(*L.mark("h", t))
            dve.wait_ge(*L.at("in", "bias", 9))
            bst = view(area("hid"), 3, D)
            for m in range(3):
                for part in range(3):
                    r = slice(32 * part, 32 * part + 32)
                    for s_ in range(part):
                        dve.wait_ge(*L.own())
                        v.tensor_copy(bias[r, m], bst[r, m]).then_inc(*L.mark())
                        dve.wait_ge(*L.own())
                        v.tensor_tensor(bst[r, m], bst[r, m], bias[r, m], ALU.subtract).then_inc(*L.mark())
                    dve.wait_ge(*L.own())
                    v.tensor_copy(bias[r, m], bst[r, m]).then_inc(*L.mark())
            for t in range(2):
                for s_ in range(3):
                    dve.wait_ge(*L.own())
                    v.tensor_copy(hparts[:, s_, t], hm[:, t] if s_ == 0 else x1[:, t]).then_inc(*L.mark())
                    if s_ < 2:
                        dve.wait_ge(*L.own())
                        v.tensor_tensor(x1[:, t], hm[:, t] if s_ == 0 else x1[:, t], hparts[:, s_, t], ALU.subtract).then_inc(*L.mark())
            for t in range(2):
                dve.wait_ge(*L.at("pe", "logit", t))
                v.tensor_tensor(logit[:, t], ps[2 * t][:, 0:32], b_rt, ALU.add).then_inc(*L.mark())
                dve.wait_ge(*L.own())
                v.max(top[:, t], logit[:, t]).then_inc(*L.mark())
                dve.wait_ge(*L.own())
                v.max_index(topi[:, t], top[:, t], logit[:, t]).then_inc(*L.mark())
                v.tensor_scalar(nmax[:, t], top[:, t, 0:1], -1.0, None, ALU.mult).then_inc(*L.mark("nmax", t))
                dve.wait_ge(*L.own())
                v.tensor_copy(topf[:, t], topi[:, t]).then_inc(*L.mark())
                dve.wait_ge(*L.at("act", "gexp", t))
                v.reciprocal(gsum[:, t], gsum[:, t]).then_inc(*L.mark())
                dve.wait_ge(*L.own())
                v.tensor_scalar(gexp[:, t], gexp[:, t], gsum[:, t], None, ALU.mult).then_inc(*L.mark())
                dve.wait_ge(*L.own())
                for k in range(TOP_K):
                    dst = (chosen[:, t], gate[:, t]) if k == 0 else (oneh[:, t], rtmp[:, t])
                    dve.wait_ge(*L.own())
                    v.tensor_scalar(dst[0], const("iota32"), topf[:, t, k:k + 1], None, ALU.is_equal).then_inc(*L.mark())
                    v.tensor_scalar(dst[1], const("iota32"), topf[:, t, k:k + 1], gexp[:, t, k:k + 1], ALU.is_equal, ALU.mult).then_inc(*L.mark())
                    if k:
                        dve.wait_ge(*L.own())
                        v.tensor_tensor(chosen[:, t], chosen[:, t], oneh[:, t], ALU.add).then_inc(*L.mark("chosen"))
                        v.tensor_tensor(gate[:, t], gate[:, t], rtmp[:, t], ALU.add).then_inc(*L.mark())
            dve.wait_ge(*L.at("pe", "pos"))
            dve.wait_ge(*L.own())
            v.scalar_tensor_tensor(out=pos, in0=view(ps[1][:, 0:64], 2, 32), scalar=1.0, in1=chosen, op0=ALU.add, op1=ALU.mult).then_inc(*L.mark())
            v.tensor_copy(cnt, ps[1][:, 64:96]).then_inc(*L.mark())
            dve.wait_ge(*L.own())
            v.tensor_scalar(pos, pos, -1.0, None, ALU.add).then_inc(*L.mark())
            v.tensor_scalar(extra, cnt, float(SLOT), None, ALU.is_gt).then_inc(*L.mark())
            v.memset(onesr, 1.0).then_inc(*L.mark())
            for more in range(2, SEQ // SLOT):
                dve.wait_ge(*L.own())
                v.scalar_tensor_tensor(out=extra, in0=cnt, scalar=float(more * SLOT), in1=extra, op0=ALU.is_gt, op1=ALU.add).then_inc(*L.mark())
            dve.wait_ge(*L.own())
            v.tensor_tensor_scan(cum, onesr, extra, 0.0, ALU.mult, ALU.add).then_inc(*L.mark())
            dve.wait_ge(*L.own())
            v.tensor_tensor(more_le, cum.unsqueeze(1).broadcast_to([P, 16, 32]),
                                  const("k16").unsqueeze(2).broadcast_to([P, 16, 32]), ALU.is_le).then_inc(*L.mark())
            dve.wait_ge(*L.own())
            v.tensor_reduce(more_e, more_le, AX.X, ALU.add).then_inc(*L.mark())
            dve.wait_ge(*L.own())
            v.tensor_tensor(more_le, more_le, extra.unsqueeze(1).broadcast_to([P, 16, 32]), ALU.mult).then_inc(*L.mark())
            dve.wait_ge(*L.own())
            v.tensor_reduce(more_b, more_le, AX.X, ALU.add).then_inc(*L.mark())
            dve.wait_ge(*L.own())
            v.tensor_tensor(more_b, const("k16"), more_b, ALU.subtract).then_inc(*L.mark())
            dve.wait_ge(*L.own())
            v.tensor_scalar(more_b, more_b, 1.0, float(SLOT), ALU.add, ALU.mult).then_inc(*L.mark())
            v.tensor_scalar(table, more_e, float(E_N - 1), None, ALU.min).then_inc(*L.mark())
            dve.wait_ge(*L.own())
            v.tensor_copy(table[:, 15:16], cum[:, 31:32]).then_inc(*L.mark())
            dve.wait_ge(*L.own())
            v.tensor_copy(intab[0:1, :], table[0:1, :]).then_inc(*L.mark("table"))

            v.tensor_tensor(owner, more_e.unsqueeze(2).broadcast_to([P, 16, 32]),
                            const("iota32").unsqueeze(1).broadcast_to([P, 16, 32]), ALU.is_equal).then_inc(*L.mark())
            v.memset(GT.rearrange("p a b -> p (a b)"), 0.0).then_inc(*L.mark())
            v.memset(ysb, 0.0).then_inc(*L.mark())
            for src, dst in ([(pos[:, t], posb[:, t]) for t in range(2)] + [(gate[:, t], gateb[:, t]) for t in range(2)]
                             + [(const("eye96"), eyeb)]):
                dve.wait_ge(*L.own())
                v.tensor_copy(dst[:, 0:E_N], src).then_inc(*L.mark())
                v.tensor_tensor(more_le, owner, src.unsqueeze(1).broadcast_to([P, 16, 32]), ALU.mult).then_inc(*L.mark())
                dve.wait_ge(*L.own())
                v.tensor_reduce(dst[:, E_N:48], more_le, AX.X, ALU.add).then_inc(*L.mark())
            for t in range(2):
                v.tensor_tensor(posb[:, t, E_N:48], posb[:, t, E_N:48], more_b, ALU.subtract).then_inc(*L.mark())

            def choose(column, step):
                for t in range(2):
                    v.tensor_scalar(Sb[:, t], const("slots", 0, SLOT), posb[:, t, column], None, ALU.is_equal).then_inc(*L.mark(*step))

            def choose_bias(column, step):
                v.tensor_scalar(selb[0:96, :], const("ones", 0, 64)[0:96, :], eyeb[0:96, column], None, ALU.mult).then_inc(*L.mark(*step))

            dve.wait_ge(*L.own())
            choose(slice(0, 1), ("Sb1",))
            choose_bias(slice(0, 1), ("selb1",))
            dve.wait_ge(*L.own())
            dve.wait_ge(*L.at("pe", "gather1"))
            L.stage("moe")
            dve.sem_inc(*L.open_loop())

            def add_rows(t):
                for c_ in range(2):
                    s_ = slice(512 * c_, 512 * c_ + 512)
                    v.tensor_tensor(acc[:, t, s_], acc[:, t, s_], ps[3 + 2 * t + c_][:, :], ALU.add).then_inc(*L.mark(*(("acc",) if L.turn is not None else ("sum", t))))

            def block_of_rows(turn):
                L.begin_turn(turn)
                dve.wait_ge(*L.own())
                dve.wait_ge(*L.at("pe", "gather", back=1))
                choose(bass.ds(turn, 1), ("Sb",))
                dve.wait_ge(*L.at("pe", "GT", back=1))
                for t in range(2):
                    v.tensor_scalar(Sg[:, t], const("slots"), posb[:, t, bass.ds(turn - 1, 1)], gateb[:, t, bass.ds(turn - 1, 1)],
                                    ALU.is_equal, ALU.mult).then_inc(*L.mark("Sg"))
                dve.wait_ge(*L.at("pe", "piece", 6))
                dve.wait_ge(*L.at("act", "sig", back=1))
                v.tensor_scalar(hid[:, 0], ps[0][:, :], LIMIT, None, ALU.min).then_inc(*L.mark("a"))
                dve.wait_ge(*L.at("pe", "piece", 7))
                v.tensor_scalar(hid[:, 2], ps[1][:, :], LIMIT, -LIMIT, ALU.min, ALU.max).then_inc(*L.mark())
                dve.wait_ge(*L.own())
                v.scalar_tensor_tensor(out=hid[:, 3], in0=hid[:, 2], scalar=1.0, in1=hid[:, 0], op0=ALU.add, op1=ALU.mult).then_inc(*L.mark())
                dve.wait_ge(*L.at("act", "sig"))
                dve.wait_ge(*L.own())
                v.tensor_tensor(hid[:, 4], hid[:, 3], hid[:, 1], ALU.mult).then_inc(*L.mark("hid"))
                dve.wait_ge(*L.at("pe", "back"))
                for t in range(2):
                    add_rows(t)
                dve.wait_ge(*L.at("pe", "piece", 8))
                choose_bias(bass.ds(turn, 1), ("selb",))
                L.end_turn()

            with dve.Fori(1, E_N + 1) as i:
                block_of_rows(i)
            L.turn = None
            n_more = dve.value_load(intab[0:1, 15:16], min_val=0, max_val=MAX_MORE)
            with dve.Fori(0, MAX_MORE) as k:
                with dve.If(n_more > k):
                    block_of_rows(k + E_N + 1)
            L.begin_turn(n_more + E_N + 1)
            dve.wait_ge(*L.own())
            L.turn = None
            L.stage("end")
            dve.wait_ge(*L.at("pe", "back1"))
            for t in range(2):
                add_rows(t)
            for t in range(2):
                dve.wait_ge(*L.at("act", "r3", t))
                r = refine(newt[:, t, 10:11], newt[:, t, 8:9], newt[:, t, 11:13], 1.0 / D)
                v.scalar_tensor_tensor(out=acc[:, t], in0=acc[:, t], scalar=r, in1=rows[:, 2], op0=ALU.mult, op1=ALU.mult).then_inc(*L.mark())
                dve.wait_ge(*L.own())
                v.tensor_tensor(hm[:, t], acc[:, t], xin[:, t], ALU.add).then_inc(*L.mark("out", t))

        @block.gpsimd
        def _(pool):
            L = lane("pool")
            g_ = nc.gpsimd
            L.stage("proj")
            pool.wait_ge(*L.at("act", "xmT", 3))
            for r in range(ROWS):
                dst = xmT[:, :, 512:768].rearrange("p k (w r) -> p k w r", r=ROWS)[:, :, :, r]
                pool.wait_ge(*L.own())
                g_.tensor_copy(dst, xmT[:, :, 256 + 64 * r:320 + 64 * r]).then_inc(*L.mark("perm"))

            for i in range(NKQ):
                kind, j, both = FM[i]
                src = {"k": kT, "q": qT}[kind][:, j]
                pool.wait_ge(*L.at("act", "silu", i))
                pool.wait_ge(*L.own())
                g_.tensor_tensor(norm_of(i), src, src, ALU.mult).then_inc(*L.mark("sq", i))
            for i in range(NKQ):
                kind, j, both = FM[i]
                dst = {"k": kT, "q": qT}[kind][:, j]
                pool.wait_ge(*L.at("act", "rn", i))
                pool.wait_ge(*L.own())
                g_.tensor_tensor(dst, dst, norm_of(i), ALU.mult).then_inc(*L.mark("kT", i))
            pool.wait_ge(*L.own())
            pool.nop().then_inc(*L.mark("end", "proj"))
            barrier(pool, L, "proj")

            L.stage("delta")
            for half in range(2):
                r = slice(64 * half, 64 * half + 64)
                for t in range(NT):
                    for d in range(2):
                        n = step_of(2 * t + half, d)
                        pool.wait_ge(*L.own())
                        g_.tensor_copy(betaS[r, n], beta[r, t, 8 * d:8 * d + 8]).then_inc(*L.mark("betaS"))
            for par in range(2):
                r = slice(64 * par, 64 * par + 64)
                for c_ in range(8):
                    for d in range(2):
                        pool.wait_ge(*L.own())
                        g_.tensor_copy(eglS[r, step_of(c_, d), d], eglb[r, c_ % 2, c_ // 2, 8 * d + par:8 * d + 8:2]).then_inc(*L.mark("eglS"))

            def keg(g):
                t, hp = divmod(g, 4)
                if g >= 2:
                    pool.wait_ge(*L.at("pe", "W", g - 2))
                for d in range(2):
                    e_ = eG[:, t, 8 * d + 2 * hp:8 * d + 2 * hp + 2].unsqueeze(2).broadcast_to([P, 2, C])
                    pool.wait_ge(*L.own())
                    g_.tensor_tensor(keG[:, g % 2, d], view(k_tm[:, t, 128 * hp:128 * hp + 128], 2, C), e_, ALU.mult).then_inc(*L.mark("keG", g))

            def unit_diagonal(g):
                b = g % 2
                pool.wait_ge(*L.at("dve", "N", g))
                pool.wait_ge(*L.own())
                g_.affine_select(out=MT[:, b], in_=MT[:, b], compare_op=ALU.not_equal, fill=1.0, base=0,
                                       pattern=[[0, 4], [-1, 128]], channel_multiplier=1).then_inc(*L.mark("unit", g))
                pool.wait_ge(*L.own())
                if g >= 2:
                    pool.wait_ge(*L.at("pe", "U", g - 2))
                for par in range(2):
                    pool.wait_ge(*L.own())
                    g_.tensor_tensor(XT[:, b, 2 * par:2 * par + 2], MT[:, b, 2 * par:2 * par + 2], m1t, ALU.mult).then_inc(*L.mark("X2T", g))

            parts = [(t, d, half) for t in range(NT) for d in range(2) for half in range(2)]
            for g in range(0, 16, 2):
                unit_diagonal(g)
                unit_diagonal(g + 1)
                keg(g)
                keg(g + 1)
                for t, d, half in parts[g:g + 2]:
                    r = slice(64 * half, 64 * half + 64)
                    e_ = ekd[r, t, 8 * d:8 * d + 8].unsqueeze(2).broadcast_to([64, H, C])
                    pool.wait_ge(*L.own())
                    g_.tensor_tensor(view(kdS[r, step_of(2 * t + half, d)], H, C), view(k_tm[r, t], H, C), e_, ALU.mult).then_inc(*L.mark("kdS"))
            for n in range(1, 7):
                cur = S[:, n - 4] if n >= 4 else Sx
                pool.wait_ge(*L.at("dve", "v", n))
                pool.wait_ge(*L.own())
                e_ = eglS[:, n].rearrange("p a b -> p (a b)").unsqueeze(2).broadcast_to([P, 8, C])
                pool.wait_ge(*L.own())
                g_.tensor_tensor(view(US[:, n], 8, C), view(cur, 8, C), e_, ALU.mult).then_inc(*L.mark("Se", n))
            pool.wait_ge(*L.own())
            pool.nop().then_inc(*L.mark("end", "delta"))
            barrier(pool, L, "delta")

            L.stage("ssd")
            for d in range(2):
                for t in range(NT):
                    pool.wait_ge(*L.own())
                    g_.tensor_tensor(wss[:, t, 8 * d:8 * d + 8], ekd[:, t, 16 + 8 * d:24 + 8 * d], sp_[:, t, 16 + 8 * d:24 + 8 * d], ALU.mult).then_inc(*L.mark())
            pool.wait_ge(*L.own())
            for t in range(NT):
                for d in range(2):
                    e_ = wss[:, t, 8 * d:8 * d + 8].unsqueeze(2).broadcast_to([P, H, C])
                    pool.wait_ge(*L.own())
                    g_.tensor_tensor(view(xw[:, t, d], H, C), view(xs_tm[:, t], H, C), e_, ALU.mult).then_inc(*L.mark("xw"))
            for g in range(8):
                t, hp = divmod(g, 4)
                pool.wait_ge(*L.at("dve", "smt", g))
                s4 = sDT[:, g % 2].rearrange("p (a b) c -> p a b c", a=2)
                pool.wait_ge(*L.own())
                g_.tensor_tensor(sMT[:, t, 2 * hp:2 * hp + 2], s4[:, :, 0], s4[:, :, 1], ALU.add).then_inc(*L.mark("sM", g))
            for n in range(1, 7):
                for d in range(2):
                    c_ = n if d == 0 else 4 * (n // 4) + 3 - n % 4
                    src = SS[:, n - 4, d] if n >= 4 else SSt[:, d]
                    dst = SS[:, n - 3, d] if n >= 3 else SSt[:, d]
                    pool.wait_ge(*L.at("dve", "SS", n, d))
                    pool.wait_ge(*L.own())
                    e_ = eglb[:, c_ % 2, c_ // 2, 16 + 8 * d:24 + 8 * d].unsqueeze(2).broadcast_to([P, H, C])
                    pool.wait_ge(*L.own())
                    g_.tensor_tensor(view(dst, H, C), view(src, H, C), e_, ALU.mult).then_inc(*L.mark("SSe", n, d))
            for t in range(2):
                pool.wait_ge(*L.own())
                g_.tensor_copy(mix[:, t, 0:512], zs[:, t]).then_inc(*L.mark("mix", 0, t))
            for t in range(2):
                pool.wait_ge(*L.at("dve", "yn", t))
                pool.wait_ge(*L.own())
                g_.tensor_tensor(mix[:, t, 512:1024], yt[:, 2 * t], snw, ALU.mult).then_inc(*L.mark("mix", 1, t))
            pool.wait_ge(*L.at("pe", "mixT", 1, 1))
            pool.wait_ge(*L.own())
            pool.nop().then_inc(*L.mark("end", "ssd"))
            barrier(pool, L, "ssd")


def kernel(**inputs):
    import numpy as np
    import concourse.bacc as bacc
    from concourse.bass_utils import run_bass_kernel_spmd

    a = {k: np.asarray(v) for k, v in inputs.items()}

    def all_rows(v):
        return np.broadcast_to(v.reshape(1, -1), (P, v.size))

    def channels(v, n):
        return v.reshape(n, P).T if v.ndim == 1 else v.T.reshape(n, P, -1).transpose(1, 0, 2)

    w_in = a["w_in"][0]
    fm_at = {"q": 0, "k": 512, "v": 1024, "xs": 2080, "b": 2592, "c": 2848}

    def k_tiles(w):
        return w.reshape(KT, P, -1).transpose(1, 0, 2).reshape(P, -1)

    wfm = np.stack([k_tiles(w_in[:, fm_at[k] + 128 * j:fm_at[k] + 128 * j + 128]) for k, j, _ in FM])
    wz = np.stack([k_tiles(w_in[:, c0:c0 + 512]).reshape(P, KT, 512) for c0 in (1536, 2080 + 1024)])
    wsm = k_tiles(np.concatenate([w_in[:, 2048:2080], w_in[:, 2080 + 1536:2080 + 1552]], axis=1))
    cols = np.concatenate([channels(a["norm_pre_mix"][0], 8),
                           channels(np.concatenate([a["gdn_conv_w"][0], a["ssd_conv_w"][0]], axis=1), 20).reshape(P, 100),
                           channels(a["ssd_conv_b"][0], 8)], axis=1)
    small = np.concatenate([all_rows(a[n][0]) for n in ("gdn_A_log", "ssd_A_log", "gdn_dt_bias", "ssd_dt_bias",
                                                        "ssd_D", "gdn_norm_w", "ssd_norm_w", "b_router")]
                           + [np.zeros((P, 40), np.float32)], axis=1)
    wrow = np.concatenate([all_rows(a[n][0]) for n in ("norm_post_mix", "norm_pre_ffn", "norm_post_ffn")], axis=1)
    cc = np.stack([a["c"][0].reshape(KT, P), a["c_ctx"].reshape(KT, P)]).transpose(2, 1, 0).reshape(P, 2 * KT)

    arrays = {
        "x": a["x"][0], "ctx": a["ctx"][0], "consts": constants(np), "cc": cc, "b_ada": a["b_ada"],
        "w_ada": a["w_ada"][0], "wfm": wfm, "wz": wz, "wsm": wsm, "cols": cols, "small": small, "wrow": wrow,
        "w_out": a["w_out"][0], "w_router": k_tiles(a["w_router"][0]), "w_gate": a["w_gate"][0], "w_up": a["w_up"][0],
        "w_down": a["w_down"][0], "b_gate": a["b_gate"][0], "b_up": a["b_up"][0], "b_down": a["b_down"][0],
    }
    arrays = {k: np.ascontiguousarray(v) for k, v in arrays.items()}
    book = None
    for _ in range(2):
        nc = bacc.Bacc("TRN2", target_bir_lowering=False, num_devices=1)
        aps = {k: nc.dram_tensor(f"in_{k}", v.shape, F32, kind="ExternalInput").ap() for k, v in arrays.items()}
        out = nc.dram_tensor("out_0", (SEQ, D), F32, kind="ExternalOutput").ap()
        book = Book(book)
        layer_program(nc, book, out=out, **aps)
    result = run_bass_kernel_spmd(nc, [{f"in_{k}": v for k, v in arrays.items()}], core_ids=[0])
    return result.results[0]["out_0"].reshape(1, SEQ, D)


def constants(np):
    p, q = np.arange(P)[:, None], np.arange(P)[None, :]
    same = (p // C == q // C)
    z = {}
    z["ident"] = (p == q)
    z["tri"] = np.concatenate([same & (p <= q), same & (p >= q)], axis=1)
    reach = [same & (p <= q), same & (p >= q)]
    z["neg"] = np.concatenate([np.where(r, 0.0, -BIG) for r in reach], axis=1)
    z["same"] = same
    z["row"] = np.concatenate([(p == C * half) & (q >= 0) for half in range(2)], axis=1)

    def level(n, d, c, s):
        if d:
            c, s = s, c
        block = (c // (2 * n) == s // (2 * n)) & (c % (2 * n) >= n) & (s % (2 * n) < n)
        return (c == s) * 1.0 - block
    z["qmask"] = np.concatenate([level(n, d, p, q) for n in LEVELS for d in range(2)], axis=1)
    z["m1t"] = np.concatenate([level(1, d, q, p) for d in range(2)], axis=1)
    z["pick"] = (p % 32 == np.arange(2)[None, :])
    z["first"] = (np.arange(32)[None, :] < 2) & (p == 0)
    z["rowb"] = (p % 32 == 0) & (q >= 0)
    z["before"] = (p < q)
    z["ones"] = np.ones((P, P))
    z["slots"] = (q % SLOT) + 0 * p
    z["iota32"] = np.arange(32)[None, :] + 0 * p
    z["eps"] = np.full((P, 1), EPS)
    z["lnq"] = np.full((P, 1), np.log(C ** -0.5))
    z["zero"] = np.zeros((P, 1))
    z["eye96"] = (p % 32 == np.arange(32)[None, :]) & (p < 96)
    z["k16"] = np.arange(16)[None, :] + 0 * p
    return np.concatenate([np.asarray(z[n], np.float32) for n in CONSTS], axis=1)
```

```python
from contextlib import ExitStack

import concourse.bass as bass
from concourse import mybir

F32 = mybir.dt.float32
BF16 = mybir.dt.bfloat16
I32 = mybir.dt.int32
ALU = mybir.AluOpType
ACT = mybir.ActivationFunctionType
AX = mybir.AxisListType

P = 128
D = 1024
KT = D // P
CTX = SEQ = 256
ROWS, GRID_W = 4, 64
H = 8
C = 64
NT = 4
EPS = 1e-6
E_N, TOP_K = 32, 4
SLOT = 64
MAX_MORE = SEQ * TOP_K // SLOT - 1
LIMIT, ALPHA = 7.0, 1.702
BIG = 1e30
ARENA = 53100
LEVELS = (2, 4, 8, 16, 32)
PIECES = 12

FM = ([("k", i, True) for i in range(4)] + [("q", i, False) for i in range(4)]
      + [("v", i, True) for i in range(4)] + [("xs", i, True) for i in range(4)]
      + [("b", i, True) for i in range(2)] + [("c", i, False) for i in range(2)])
NFM = len(FM)
NKQ = 8
TURNED = []
for _i in range(NKQ, NFM):
    if FM[_i][0] in ("v", "xs", "b"):
        TURNED.append(_i)
    if NKQ + 2 <= _i < NKQ + 6:
        TURNED.append(_i - NKQ - 2)
ADA_AT = 11

CONSTS = {}


def _const_layout():
    at = 0
    for name, n in (("ident", 128), ("tri", 256), ("neg", 256), ("same", 128), ("row", 256),
                    ("qmask", 5 * 256), ("m1t", 256), ("pick", 2), ("first", 32), ("rowb", 128),
                    ("before", 128), ("ones", 128), ("slots", 128), ("iota32", 32),
                    ("eps", 1), ("lnq", 1), ("zero", 1), ("eye96", 32), ("k16", 16)):
        CONSTS[name] = (at, n)
        at += n
    return at


NCONST = _const_layout()


class Book:

    def __init__(self, old=None):
        self.old = old.new if old else {}
        self.per_old = old.per if old else {}
        self.new, self.per, self.dry = {}, {}, old is None


class Lane:

    def __init__(self, sems, book, name):
        self.sems, self.book, self.name = sems, book, name
        self.sem, self.n, self.turn, self.per = None, 0, None, 1

    def stage(self, name):
        self.sem_name = f"{self.name}_{name}"
        self.sem, self.n, self.turn = self.sems(self.sem_name), 0, None

    def mark(self, *step):
        self.n += 1
        if step:
            key = (self.name,) + step
            assert self.book.new.get(key, (self.sem_name,))[0] == self.sem_name, step
            self.book.new[key] = (self.sem_name, self.n)
        return self.sem, 1

    def own(self):
        return self.sem, self.n if self.turn is None else self.turn * self.per + self.n

    def at(self, who, *step, back=0):
        name, value = self.book.old.get((who,) + step) or self.book.new.get((who,) + step) or (f"{who}_dry", 1)
        assert self.book.dry or (who,) + step in self.book.old, (who, step)
        if name in self.book.per_old:
            value = (self.turn - back) * self.book.per_old[name] + value
        return self.sems(name), value

    def open_loop(self):
        self.per = self.book.per_old.get(self.sem_name, 1)
        return self.sem, self.per

    def begin_turn(self, turn):
        self.turn, self.n = turn, 0

    def end_turn(self):
        self.book.per[self.sem_name] = self.n


def view(ap, *dims):
    names = "abcdef"[:len(dims)]
    if len(dims) == 1:
        return ap
    return ap.rearrange(f"p ({' '.join(names)}) -> p {' '.join(names)}",
                        **{n: d for n, d in zip(names[:-1], dims[:-1])})


def lay_out_sbuf():
    at = {}

    def put(base, *items):
        for name, n in items:
            assert name not in at
            at[name] = (base, n)
            base += n
        assert base <= ARENA, (base, items)
        return base

    keep = put(0, ("const", NCONST), ("x", 2 * D), ("rows", 4 * D), ("cols", 8 + 20 * 5 + 8),
               ("small", 720), ("gates", 2300))
    ops = put(keep, ("kT", 4 * 512), ("qT", 4 * 256), ("bT", 2 * 512), ("cT", 2 * 256), ("k_tm", 4 * 512),
              ("v_tm", 4 * 512), ("xs_tm", 4 * 512), ("b_tm", 4 * 256), ("z", 4 * 512))
    put(ops, ("xmT", KT * 768), ("modp", 4 * 512), ("modq", 512), ("ada", 2 * 4096), ("win", 3 * 1024),
        ("xh", D), ("pad", 2 * 520), ("conv", 2 * 512), ("nrm", 6 * 512), ("sc", 256), ("wsm", 384))
    g = put(ops, ("DT", 4 * 512), ("MT", 4 * 512), ("X", 2 * 512), ("XT", 4 * 512),
            ("WT", 4096), ("attnT", 4096), ("kdS", 4096), ("US", 4096))
    g = put(g, ("vS", 4 * 512), ("Sx", 512))
    s = put(ops, ("mix", 2 * D), ("sDT", 2 * 512), ("sMT", 16 * 128), ("xw", 8 * 512), ("SS", 2 * 4 * 512), ("SSt", 2 * 512),
            ("yt", 4 * 512), ("mixT", KT * 256), ("wout", KT * D))
    put(keep, ("bstage", 3 * D))
    e = put(keep, ("h", 2 * D), ("hp", 3 * D), ("wr", 256), ("bias", 3 * 512), ("acc", 2 * D), ("hid", 6 * 512))
    assert at["bstage"][0] + 3 * D <= at["bT"][0] and at["wr"][0] >= at["k_tm"][0]
    assert at["bias"][0] + at["bias"][1] <= at["xs_tm"][0]
    put(e, ("hT", KT * 256))
    e = put(e, ("xcT", 512), ("hidT", 512), ("y", 512), ("GT", 256), ("Sg", 256))
    put(e, ("Sb", 64), ("route", 1500), ("ring", PIECES * 2048))
    return at


AT = lay_out_sbuf()


def layer_program(nc, book, x, ctx, consts, cc, b_ada, w_ada, wfm, wz, wsm, cols, small, wrow, w_out, w_router,
                  w_gate, w_up, w_down, b_gate, b_up, b_down, out):
    stack = ExitStack()
    with stack:
        arena = stack.enter_context(nc.sbuf_tensor("arena", [P, ARENA], F32))
        intab = stack.enter_context(nc.sbuf_tensor("intab", [1, 16], I32))
        ps = [stack.enter_context(nc.psum_tensor(f"bank{i}", [P, 512], F32))[:, :] for i in range(8)]
        known = {}

        def sems(name):
            if name not in known:
                known[name] = stack.enter_context(nc.semaphore(name))
            return known[name]

        def area(name, lo=0, n=None):
            base, size = AT[name]
            n = size - lo if n is None else n
            assert lo + n <= size, name
            return arena[:, base + lo:base + lo + n]

        def const(name, lo=0, n=None):
            base, size = CONSTS[name]
            return area("const", base + lo, size - lo if n is None else n)

        ident = const("ident")
        tri = view(const("tri"), 2, 128)
        neg = view(const("neg"), 2, 128)
        qmask = view(const("qmask"), 5, 2, 128)
        m1t = view(const("m1t"), 2, 128)
        xin = view(area("x"), 2, D)
        rows = view(area("rows"), 4, D)
        npm = area("cols", 0, 8)
        convw = view(area("cols", 8, 100), 20, 5)
        convb = area("cols", 108, 8)
        a_log, dt_b = area("small", 0, 32), area("small", 32, 32)
        dskip, gnw = area("small", 64, 8), area("small", 72, 64)
        snw, b_rt = area("small", 136, 512), area("small", 648, 32)
        kT = view(area("kT"), 4, 512)
        qT = view(area("qT"), 4, 256)
        bT = view(area("bT"), 2, 512)
        cT = view(area("cT"), 2, 256)
        k_tm, v_tm, xs_tm = (view(area(n), 4, 512) for n in ("k_tm", "v_tm", "xs_tm"))
        b_tm = view(area("b_tm"), 4, 256)
        zs = view(area("z"), 4, 512)
        ctx_in = view(area("z"), 2, D)
        xmT = view(area("xmT"), KT, 768)
        modp, modq = area("modp"), area("modq")
        ada = view(area("ada"), 2, KT, 512)
        win = view(area("win"), 3, KT, 128)
        xh = area("xh")
        pad = view(area("pad"), 2, 2, 260)
        conv = view(area("conv"), 2, 512)
        nrm = area("nrm")
        bada = [area("nrm", 0, 4 * 512), modp, area("nrm", 0, 4 * 512)]
        ada_early = [area("xmT", 0, 4096), arena[:, AT["kT"][0]:AT["kT"][0] + 4096]]

        def ada_of(use):
            return view(ada_early[use - 2], KT, 512) if use in (2, 3) else ada[:, use % 2]

        sct = view(area("sc"), KT, 32)
        wsmt = view(area("wsm"), KT, 48)

        g_at = [0]

        def gates(*dims):
            n = 1
            for d in dims:
                n *= d
            v = view(area("gates", g_at[0], n), *dims)
            g_at[0] += n
            return v

        modc = gates(16, 2)
        a1 = gates(8, 2)
        ssq = gates(16)
        newt = gates(4, 16)
        sm = gates(4, 48)
        beta = gates(4, 16)
        tsp = gates(3, 4, 32)
        sp_ = gates(4, 32)
        nega = gates(32)
        gA = gates(4, 32)
        Gc, gl, eG, ekd, egl = (gates(4, 32) for _ in range(5))
        wss = gates(4, 16)
        eglb = gates(2, 4, 32)
        eglS = gates(8, 2, 4)
        betaS = gates(8, 8)
        ngrp = gates(2, 16)

        DT, MT, XT = (view(area(n), 4, 4, 128) for n in ("DT", "MT", "XT"))
        X = view(area("X"), 2, 4, 128)
        Q = DT
        keG = [view(area("MT", 512 * b, 256), 2, 2, 64) for b in range(4)]
        WT = view(area("WT"), 4, 4, 2, 128)
        attnT = view(area("attnT"), 2, 4, 2, 2, 128)
        kdS, US = view(area("kdS"), 8, 512), view(area("US"), 8, 512)
        S, vS, Sx = view(area("XT"), 4, 512), view(area("vS"), 4, 512), area("Sx")
        mix = view(area("mix"), 2, D)
        sDT = view(area("sDT"), 2, 4, 128)
        sMT = view(area("sMT"), 2, 8, 128)
        xw = view(area("xw"), 4, 2, 512)
        SS = view(area("SS"), 4, 2, 512)
        SSt = view(area("SSt"), 2, 512)
        yt = view(area("yt"), 4, 512)
        mixT = view(area("mixT"), KT, 256)
        wout = view(area("wout"), KT, D)
        x1, hm = view(area("hid", 0, 2 * D), 2, D), view(area("h"), 2, D)
        hparts = area("hp").bitcast(BF16).rearrange("p (s t d) -> p s t d", s=3, t=2)
        hT = view(area("hT"), KT, 256)
        wr = view(area("wr"), KT, 32)
        bias = area("bias").bitcast(BF16).rearrange("p (m d) -> p m d", m=3)
        acc = view(area("acc"), 2, D)
        xcT = view(area("xcT"), KT, SLOT)
        hid = view(area("hid"), 6, 512)
        hidT = view(area("hidT"), 4, 128)
        ysb = area("y")
        GT = view(area("GT"), 2, 128)
        Sg = view(area("Sg"), 2, 128)
        Sb = area("Sb").bitcast(BF16).rearrange("p (t s) -> p t s", t=2)
        ring = view(area("ring"), PIECES, 2, D)
        r_at = [0]

        def route(*dims):
            n = 1
            for d in dims:
                n *= d
            v = view(area("route", r_at[0], n), *dims)
            r_at[0] += n
            return v

        logit = route(2, 32)
        top = route(2, 8)
        topi = route(2, 8).bitcast(mybir.dt.uint32)
        topf = route(2, 8)
        gexp = route(2, 4)
        gsum = route(2, 1)
        nmax = route(2, 1)
        oneh = route(2, 32)
        rtmp = route(2, 32)
        chosen = route(2, 32)
        gate = route(2, 32)
        pos = route(2, 32)
        cnt = route(32)
        extra = route(32)
        cum = route(32)
        onesr = route(32)
        more_le = route(16, 32)
        more_e = route(16)
        more_b = route(16)
        posb = route(2, 48)
        gateb = route(2, 48)
        eyeb = route(48)
        table = route(16)
        owner = view(area("hid", 5 * 512, 512), 16, 32)
        selb = route(32).bitcast(BF16)

        def norm_of(i):
            return nrm[:, 512 * i:512 * i + 512] if i < 4 else nrm[:, 2048 + 256 * (i - 4):2304 + 256 * (i - 4)]

        block = stack.enter_context(nc.Block())

        def lane(name):
            return Lane(sems, book, name)

        def barrier(eng, me, name):
            for other in ("pe", "act", "dve", "pool", "sp"):
                if other != me.name:
                    eng.wait_ge(*me.at(other, "end", name))

        def step_of(c, direction):
            return c if direction == 0 else 4 * (c // 4) + 3 - c % 4

        @block.sync
        def _(sp):
            L = lane("sp")
            ready = {}

            def load(name, dst, src):
                n = ready[name] = ready.get(name, 0) + 1
                sp.dma_start(dst, src).then_inc(sems(f"in_{name}"), 16)
                book.new[("in", name, n)] = (f"in_{name}", 16 * n)

            load("cc", area("sc", 0, 16), cc)
            load("const", area("const"), consts)
            w_ada_v = w_ada.rearrange("(k p) n -> p k n", p=P)

            def load_ada(use):
                load(f"ada{use % 4 if use < 4 else use % 2}", ada_of(use), w_ada_v[:, :, use * 512:use * 512 + 512])

            load("bada", bada[0][0:1, :], b_ada[:, 0:4 * 512])
            for use in range(3):
                load_ada(use)
            load("x", xin, x.rearrange("(t p) d -> p t d", p=P))
            load_ada(3)
            load("ctx", ctx_in, ctx.rearrange("(t p) d -> p t d", p=P))
            load("cols", area("cols"), cols)
            load("small", area("small"), small)
            load("wsm", area("wsm"), wsm)
            for i in range(3):
                load(f"win{i}", area("win", i * 1024, 1024), wfm[i])
            for m in range(2):
                sp.wait_ge(*L.at("pe", "slot", m))
                load(f"ada{m}", ada[:, m], wz[m])
            load("wrow", area("rows", 0, 3 * D), wrow)
            sp.wait_ge(*L.at("pe", "modc"))
            load("bada", bada[1][0:1, :], b_ada[:, 4 * 512:8 * 512])
            for i in range(3, NFM):
                sp.wait_ge(*L.at("pe", "fm", i - 3))
                load(f"win{i % 3}", area("win", (i % 3) * 1024, 1024), wfm[i])
                use = i - ADA_AT + 5
                if 4 <= use < 12:
                    sp.wait_ge(*(L.at("pe", "z", use - 4) if use < 6 else L.at("pe", "slot", use - 2)))
                    load_ada(use)
                if i == NKQ + 6:
                    sp.wait_ge(*L.at("pool", "kT", NKQ - 1))
                    load("bada", bada[2][0:1, :], b_ada[:, 8 * 512:12 * 512])
            for st in ("proj", "delta"):
                L.stage(st)
                sp.wait_ge(*L.own())
                sp.nop().then_inc(*L.mark("end", st))
                barrier(sp, L, st)
            load("wout", wout, w_out.rearrange("(k p) n -> p k n", p=P))
            for part in range(3):
                for m, b in enumerate((b_gate, b_up, b_down)):
                    load("bias", view(area("bstage"), 3, D)[32 * part:32 * part + 32, m, :], b)
            load("wr", area("wr"), w_router)
            L.stage("ssd")
            sp.wait_ge(*L.own())
            sp.nop().then_inc(*L.mark("end", "ssd"))
            barrier(sp, L, "ssd")

            halves = [w.rearrange("e (k p) n -> e p k n", p=P) for w in (w_gate, w_up, w_down)]
            order = [(m, j) for j in range(4) for m in range(2)] + [(2, j) for j in range(4)]
            L.stage("moe")

            def pieces(turn, expert):
                L.begin_turn(turn)
                for n, (m, j) in enumerate(order):
                    sp.wait_ge(*L.at("pe", "piece", n, back=1))
                    src = halves[m][bass.ds(expert, 1), :, 2 * j:2 * j + 2, :].rearrange("e p k n -> p (e k) n")
                    sp.dma_start(ring[:, n], src).then_inc(sems(f"in_ring{n}"), 16)

            with sp.Fori(1, E_N + 1) as i:
                pieces(i, i - 1)
            L.turn = None
            sp.wait_ge(*L.at("dve", "table"))
            n_more = sp.value_load(intab[0:1, 15:16], min_val=0, max_val=MAX_MORE)
            with sp.Fori(0, MAX_MORE) as k:
                with sp.If(n_more > k):
                    expert = sp.value_load(intab[0:1, bass.ds(k, 1)], min_val=0, max_val=E_N - 1)
                    pieces(k + E_N + 1, expert)
            L.turn = None
            for t in range(2):
                sp.wait_ge(*L.at("dve", "out", t))
                sp.dma_start(out[t * P:t * P + P, :], hm[:, t]).then_inc(sems("stored"), 16)
            sp.wait_ge(sems("stored"), 32)

        @block.tensor
        def _(pe):
            L = lane("pe")
            mm = nc.tensor.matmul
            L.stage("proj")

            def ada_chunk(use, bank):
                if use < 4:
                    pe.wait_ge(*L.at("in", f"ada{use}", 1))
                else:
                    pe.wait_ge(*L.at("in", f"ada{use % 2}", use // 2 + 1))
                if 2 <= use < 4:
                    pe.wait_ge(*L.at("act", "mod", use - 2))
                pe.wait_ge(*L.at("in", "bada", use // 4 + 1))
                b_row = bada[use // 4][0:1, 512 * (use % 4):512 * (use % 4) + 512]
                mm(ps[bank][0:32, :], const("first")[0:1, :], b_row, start=True, stop=False)
                for k in range(KT):
                    g = k % 4
                    last = mm(ps[bank][32 * g:32 * g + 32, :], sct[:, k, :], ada_of(use)[:, k, :],
                              start=(k < 4 and g > 0), stop=(k >= 4))
                last.then_inc(*L.mark("ada", use))
                book.new[("pe", "slot", use)] = book.new[("pe", "ada", use)]

            pe.wait_ge(*L.at("in", "const", 1))
            pe.wait_ge(*L.at("dve", "sct"))
            for use in range(4):
                ada_chunk(use, use % 2)
            pe.wait_ge(*L.at("act", "mod", 3))
            for i in range(16):
                last = mm(ps[2][:, 2 * i:2 * i + 2], modp[:, 128 * i:128 * i + 128], const("pick"),
                          start=True, stop=True)
            last.then_inc(*L.mark("modc"))
            for n, t in enumerate((2, 3, 0, 1)):
                pe.wait_ge(*L.at("dve", "xh", t))
                if n >= 2:
                    pe.wait_ge(*L.at("act", "xmT", (2, 3, 0, 1)[n - 2]))
                for k in range(KT):
                    last = nc.tensor.transpose(ps[4 + 2 * (n % 2) + k // 4][:, (k % 4) * 128:(k % 4) * 128 + 128],
                                               xh[:, 128 * k:128 * k + 128], ident)
                last.then_inc(*L.mark("xT", t))
            pe.wait_ge(*L.at("act", "xmT", 1))
            pe.wait_ge(*L.at("pool", "perm"))
            pe.wait_ge(*L.at("in", "wsm", 1))
            smp = view(ps[3][:, 0:192], 4, 48)
            for t in range(NT):
                for lo, hi in ((0, 48),) if t < 2 else ((0, 32), (32, 48)):
                    base = t * 128 if t < 2 else 256 + (t - 2) * 128 if lo == 0 else 512 + (t - 2) * 128
                    for k in range(KT):
                        last = mm(smp[:, t, lo:hi], xmT[:, k, base:base + 128], wsmt[:, k, lo:hi],
                                  start=(k == 0), stop=(k == KT - 1))
            last.then_inc(*L.mark("sm"))
            for m in range(2):
                for t in range(2):
                    if t == 0:
                        pe.wait_ge(*L.at("in", f"ada{m}", 2))
                    if m:
                        pe.wait_ge(*L.at("act", "z", t))
                    base = 256 + 256 * m + 128 * t
                    for k in range(KT):
                        last = mm(ps[t], xmT[:, k, base:base + 128], ada[:, m, k, :], start=(k == 0), stop=(k == KT - 1))
                    last.then_inc(*L.mark("zt", m, t))
                book.new[("pe", "z", m)] = book.new[("pe", "zt", m, 1)]

            def cumulate():
                pe.wait_ge(*L.at("dve", "gA"))
                g = gA.rearrange("p t (k d h) -> p t k d h", k=2, d=2)
                for d in range(2):
                    for t in range(NT):
                        mm(view(ps[6][:, d * 64 + t * 16:d * 64 + t * 16 + 16], 2, 8), tri[:, d], g[:, t, :, d, :],
                           start=True, stop=True)
                last = mm(ps[6][:, 128:256], const("same"), gA.rearrange("p t c -> p (t c)"), start=True, stop=True)
                last.then_inc(*L.mark("cum"))

            def spread_last():
                pe.wait_ge(*L.at("act", "egl"))
                for half in range(2):
                    last = mm(ps[6][:, 256 + 128 * half:384 + 128 * half], const("row", 128 * half, 128),
                              egl.rearrange("p t c -> p (t c)"), start=True, stop=True)
                last.then_inc(*L.mark("eglb"))

            def fm(i):
                kind, j, both = FM[i]
                pe.wait_ge(*L.at("in", f"win{i % 3}", i // 3 + 1))
                if i >= 2:
                    pe.wait_ge(*L.at("act", "pad", i - 2))
                elif i < 2:
                    pe.wait_ge(*L.at("act", "z", 2 + i))
                for k in range(KT):
                    if kind in ("xs", "b", "c"):
                        cols_ = xmT[:, k, 0:768].rearrange("p (a b) -> p a b", a=3)[:, 0:3:2, :] if both else xmT[:, k, 512:768]
                    else:
                        cols_ = xmT[:, k, 0:512] if both else xmT[:, k, 256:512]
                    dst = ps[i % 2][:, 0:512 if both else 256]
                    if both:
                        dst = view(dst, 2, 256)
                        if kind not in ("xs", "b"):
                            cols_ = view(cols_, 2, 256)
                    last = mm(dst, win[:, i % 3, k, :], cols_, start=(k == 0), stop=(k == KT - 1))
                last.then_inc(*L.mark("fm", i))

            def norms():
                for i in range(NKQ):
                    w = 512 if FM[i][2] else 256
                    pe.wait_ge(*L.at("pool", "sq", i))
                    if i >= 2:
                        pe.wait_ge(*L.at("act", "ln", i - 2))
                    bk = ps[2 if i % 2 == 0 else 7]
                    mm(bk[:, 0:w], const("same"), norm_of(i), start=True, stop=True).then_inc(*L.mark("ssq", i))

            def turn(i):
                kind, j, both = FM[i]
                n = TURNED.index(i)
                pe.wait_ge(*(L.at("pool", "kT", i) if kind == "k" else L.at("act", "silu", i)))
                if n >= 2:
                    pe.wait_ge(*L.at("act", "turned", TURNED[n - 2]))
                src = kT[:, j] if kind == "k" else bT[:, j] if kind == "b" else conv[:, i % 2]
                for t in range(NT):
                    last = nc.tensor.transpose(ps[4 + n % 2][:, 128 * t:128 * t + 128], src[:, 128 * t:128 * t + 128], ident)
                last.then_inc(*L.mark("turn", i))

            for i in range(NFM + 1):
                if i < NFM:
                    fm(i)
                if i == 1:
                    cumulate()
                if i == NKQ + 1:
                    norms()
                if i > NKQ and i - 1 in TURNED:
                    turn(i - 1)
                if NKQ + 3 <= i < NKQ + 7:
                    turn(i - NKQ - 3)
                if i == NKQ + 3:
                    spread_last()
                if ADA_AT <= i < ADA_AT + 8:
                    use = i - ADA_AT + 4
                    if use > 4:
                        pe.wait_ge(*L.at("act", "mod", use - 1))
                    else:
                        pe.wait_ge(*L.at("act", "ln", NKQ - 1))
                    ada_chunk(use, 3)
                    pe.wait_ge(*L.at("act", "mod", use))
                    if use > 4:
                        pe.wait_ge(*L.at("dve", "row", use - 1))
                    mm(ps[7], const("rowb"), modq, start=True, stop=True).then_inc(*L.mark("row", use))
            pe.wait_ge(*L.own())
            pe.nop().then_inc(*L.mark("end", "proj"))
            barrier(pe, L, "proj")

            L.stage("delta")
            groups = [(t, hp) for t in range(NT) for hp in range(4)]

            def bank(g, which):
                return ps[4 * (g % 2) + which]

            def unit(b, u):
                return b[:, 128 * u:128 * u + 128]

            def gram(par):
                return ps[3 + 4 * par]

            def spread_decays(g):
                t, hp = groups[g]
                if g >= 4:
                    pe.wait_ge(*L.at("dve", "U", g - 4))
                for u in range(4):
                    par, d = divmod(u, 2)
                    last = mm(unit(bank(g, 3), u), gA[:, t, d * 8 + 2 * hp + par:d * 8 + 2 * hp + par + 1].broadcast_to([P, P]),
                              tri[:, d], start=True, stop=True)
                last.then_inc(*L.mark("Gb", g))

            def products(pair):
                pe.wait_ge(*L.at("dve", "rel", pair[0]))
                pe.wait_ge(*L.at("dve", "rel", pair[1]))
                for g in pair:
                    t, hp = groups[g]
                    for par in range(2):
                        k_ = kT[64 * par:64 * par + 64, hp, 128 * t:128 * t + 128]
                        last = mm(gram(par)[:, 256 * (g % 2):256 * (g % 2) + 128], k_, k_, start=True, stop=True)
                        if t >= 2:
                            last = mm(gram(par)[:, 256 * (g % 2) + 128:256 * (g % 2) + 256], k_,
                                      qT[64 * par:64 * par + 64, hp, 128 * (t - 2):128 * (t - 2) + 128], start=True, stop=True)
                last.then_inc(*L.mark("gram", pair[0]))

            def first_turn(g):
                pe.wait_ge(*L.at("pool", "X2T", g))
                if g >= 2:
                    pe.wait_ge(*L.at("act", "WT", g - 2))
                for u in range(4):
                    last = nc.tensor.transpose(unit(bank(g, 1), u), XT[:, g % 4, u], ident)
                last.then_inc(*L.mark("X2", g))

            def level_a(g, z):
                b = g % 4
                pe.wait_ge(*L.at("act", "X", g, z))
                if z > LEVELS[0]:
                    pe.wait_ge(*L.at("act", "XT", g, z))
                for u in range(4):
                    last = mm(unit(bank(g, 0), u), MT[:, b, u], X[:, g % 2, u], start=True, stop=True)
                last.then_inc(*L.mark("P", g, z))

            def level_b(g, z):
                b = g % 4
                pe.wait_ge(*L.at("dve", "Q", g, z))
                if z < LEVELS[-1]:
                    for u in range(4):
                        last = mm(unit(bank(g, 1), u), XT[:, b, u], Q[:, b, u], start=True, stop=True)
                    last.then_inc(*L.mark("XQ", g, z))
                for u in range(4):
                    last = mm(unit(bank(g, 2), u), Q[:, b, u], XT[:, b, u], start=True, stop=True)
                last.then_inc(*L.mark("QX", g, z))

            def solved(g):
                t, hp = groups[g]
                b = g % 4
                pe.wait_ge(*L.at("act", "XT", g, 64))
                pe.wait_ge(*L.at("pool", "keG", g))
                for u in range(4):
                    par, d = divmod(u, 2)
                    last = mm(bank(g, 1)[64 * par:64 * par + 64, 128 * d:128 * d + 128], keG[b][:, d, par, :], XT[:, b, u],
                              start=True, stop=True)
                last.then_inc(*L.mark("W", g))
                if g < 14:
                    for n in (0, 1):
                        pe.wait_ge(*L.at("dve", "N", g - g % 2 + 2 + n))
                for u in range(4):
                    par, d = divmod(u, 2)
                    head = 2 * hp + par
                    for half in range(2):
                        r = slice(64 * half, 64 * half + 64)
                        last = mm(bank(g, 3)[r, (2 * d + par) * 64:(2 * d + par) * 64 + 64],
                                  XT[r, b, u, 64 * half:64 * half + 64], v_tm[r, t, 64 * head:64 * head + 64],
                                  start=True, stop=True)
                last.then_inc(*L.mark("U", g))

            for h_ in (0, 1):
                spread_decays(h_)
            products((0, 1))
            for g in range(0, 16, 2):
                pair, ahead = (g, g + 1), (g + 2, g + 3)
                for h_ in pair:
                    first_turn(h_)
                if g < 14:
                    for h_ in ahead:
                        if g == 0:
                            pe.wait_ge(*L.at("dve", "N", 1))
                        spread_decays(h_)
                for z in LEVELS:
                    for h_ in pair:
                        level_a(h_, z)
                    for h_ in pair:
                        level_b(h_, z)
                    if z == LEVELS[0] and g < 14:
                        products(ahead)
                for h_ in pair:
                    solved(h_)

            pe.wait_ge(*L.at("act", "WT", 15))
            pe.wait_ge(*L.at("dve", "U", 15))
            for n in range(8):
                sb_ = n % 2
                if n:
                    pe.wait_ge(*L.at("dve", "S", n))
                    for d in range(2):
                        c_ = n if d == 0 else 4 * (n // 4) + 3 - n % 4
                        t, half = divmod(c_, 2)
                        for head in range(H):
                            hp, par = divmod(head, 2)
                            r = slice(64 * par, 64 * par + 64)
                            last = mm(ps[2 * sb_ + par][64 * half:64 * half + 64, 64 * hp:64 * hp + 64],
                                      WT[r, t, hp, d, 64 * half:64 * half + 64],
                                      (S[:, n - 4] if n >= 4 else Sx)[r, (d * 4 + hp) * 64:(d * 4 + hp) * 64 + 64],
                                      start=True, stop=True)
                    last.then_inc(*L.mark("WS", n))
                if n == 7:
                    break
                pe.wait_ge(*L.at("dve", "v", n))
                pe.wait_ge(*L.at("pool", "kdS"))
                for d in range(2):
                    c_ = n if d == 0 else 4 * (n // 4) + 3 - n % 4
                    half = c_ % 2
                    for head in range(H):
                        hp, par = divmod(head, 2)
                        r = slice(64 * half, 64 * half + 64)
                        last = mm(ps[4 + 2 * sb_ + d][64 * par:64 * par + 64, 64 * hp:64 * hp + 64],
                                  kdS[r, n, 64 * head:64 * head + 64],
                                  vS[r, n % 4, 64 * head:64 * head + 64], start=True, stop=True)
                last.then_inc(*L.mark("KV", n))
            pe.wait_ge(*L.at("dve", "v", 7))
            for t in range(2):
                if t:
                    pe.wait_ge(*L.at("dve", "O", 0))
                for half in range(2):
                    r = slice(64 * half, 64 * half + 64)
                    for d in range(2):
                        n = step_of(4 + 2 * t + half, d) - 4
                        for head in range(H):
                            hp, par = divmod(head, 2)
                            rp = slice(64 * par, 64 * par + 64)
                            mm(ps[par][r, (4 * d + hp) * 64:(4 * d + hp) * 64 + 64], qT[rp, hp, 128 * t + 64 * half:128 * t + 64 * half + 64],
                               S[rp, n, (d * 4 + hp) * 64:(d * 4 + hp) * 64 + 64], start=True, stop=True)
                    for head in range(H):
                        hp, par = divmod(head, 2)
                        for d in range(2):
                            n = step_of(4 + 2 * t + half, d) - 4
                            last = mm(ps[4][r, 64 * head:64 * head + 64], attnT[r, t, hp, par, d, 64 * half:64 * half + 64],
                                      vS[r, n, 64 * head:64 * head + 64], start=(d == 0), stop=(d == 1))
                last.then_inc(*L.mark("O", t))
            pe.wait_ge(*L.at("dve", "O", 1))
            pe.wait_ge(*L.own())
            pe.nop().then_inc(*L.mark("end", "delta"))
            barrier(pe, L, "delta")

            L.stage("ssd")
            for t in range(2):
                for g in range(2):
                    last = mm(ps[7][:, (2 * t + g) * 128:(2 * t + g) * 128 + 128], bT[:, g, 256 + 128 * t:384 + 128 * t],
                              cT[:, g, 128 * t:128 * t + 128], start=True, stop=True)
            last.then_inc(*L.mark("cb"))
            for g in range(8):
                t, hp = divmod(g, 4)
                if g >= 2:
                    pe.wait_ge(*L.at("dve", "srel", g - 2))
                for u in range(4):
                    par, d = divmod(u, 2)
                    ch = 16 + d * 8 + 2 * hp + par
                    last = mm(unit(ps[g % 2], u), gA[:, 2 + t, ch:ch + 1].broadcast_to([P, P]), tri[:, d], start=True, stop=True)
                last.then_inc(*L.mark("sG", g))
            for n in range(7):
                for d in range(2):
                    t, half = divmod(n if d == 0 else 4 * (n // 4) + 3 - n % 4, 2)
                    r = slice(64 * half, 64 * half + 64)
                    bk = 2 + 2 * (n % 2) + d
                    pe.wait_ge(*L.at("pool", "xw", t, d))
                    if n >= 2:
                        pe.wait_ge(*L.at("dve", "SS", n - 1, d))
                    for g in range(2):
                        last = mm(ps[bk][:, 256 * g:256 * g + 256], b_tm[r, t, 128 * g:128 * g + 128],
                                  xw[r, t, d, 256 * g:256 * g + 256], start=True, stop=True)
                    last.then_inc(*L.mark("BX", n, d))
            pe.wait_ge(*L.at("dve", "SS", 7, 0))
            pe.wait_ge(*L.at("dve", "SS", 7, 1))
            for t in range(2):
                for d in range(2):
                    if t:
                        pe.wait_ge(*L.at("dve", "Y", 0))
                    for half in range(2):
                        n = step_of(4 + 2 * t + half, d) - 4
                        for g in range(2):
                            last = mm(ps[2 + d][64 * half:64 * half + 64, 256 * g:256 * g + 256],
                                      cT[:, g, 128 * t + 64 * half:128 * t + 64 * half + 64],
                                      SS[:, n, d, 256 * g:256 * g + 256], start=True, stop=True)
                pe.wait_ge(*L.at("pool", "sM", 4 * t + 3))
                for head in range(H):
                    last = mm(ps[4][:, 64 * head:64 * head + 64], sMT[:, t, head], xs_tm[:, 2 + t, 64 * head:64 * head + 64],
                              start=True, stop=True)
                last.then_inc(*L.mark("Y", t))
            def mixed(n, m, t):
                pe.wait_ge(*L.at("pool", "mix", m, t))
                if n >= 2:
                    pe.wait_ge(*L.at("act", "mixT", 0, n - 2))
                for k in range(4):
                    last = nc.tensor.transpose(unit(ps[5 + n % 2], k), mix[:, t, 512 * m + 128 * k:512 * m + 128 * k + 128], ident)
                last.then_inc(*L.mark("mixT", m, t))

            def project(t, ks):
                for c_ in range(2):
                    for k in ks:
                        last = mm(ps[2 * t + c_], mixT[:, k, 128 * t:128 * t + 128], wout[:, k, 512 * c_:512 * c_ + 512],
                                  start=(k == 0), stop=(k == KT - 1))
                return last

            mixed(0, 0, 0)
            mixed(1, 0, 1)
            pe.wait_ge(*L.at("act", "mixT", 0, 0))
            pe.wait_ge(*L.at("in", "wout", 1))
            project(0, range(4))
            mixed(2, 1, 0)
            mixed(3, 1, 1)
            pe.wait_ge(*L.at("act", "mixT", 1, 1))
            project(0, range(4, KT)).then_inc(*L.mark("m", 0))
            project(1, range(KT)).then_inc(*L.mark("m", 1))
            pe.wait_ge(*L.at("dve", "x1", 1))
            pe.wait_ge(*L.own())
            pe.nop().then_inc(*L.mark("end", "ssd"))
            barrier(pe, L, "ssd")

            L.stage("moe")
            pe.sem_inc(*L.open_loop())

            L.stage("route")
            for t in range(2):
                pe.wait_ge(*L.at("dve", "h", t))
                for k in range(KT):
                    last = nc.tensor.transpose(unit(ps[4 + 2 * t + k // 4], k % 4), hm[:, t, 128 * k:128 * k + 128], ident)
                last.then_inc(*L.mark("hT", t))
            pe.wait_ge(*L.at("in", "wr", 1))
            for t in range(2):
                pe.wait_ge(*L.at("act", "hT", t))
                for k in range(KT):
                    last = mm(ps[2 * t][:, 0:32], hT[:, k, 128 * t:128 * t + 128], wr[:, k, :],
                              start=(k == 0), stop=(k == KT - 1))
                last.then_inc(*L.mark("logit", t))
            pe.wait_ge(*L.at("dve", "chosen"))
            mm(ps[1][:, 0:32], const("before"), chosen[:, 0], start=True, stop=True)
            mm(ps[1][:, 32:64], const("ones"), chosen[:, 0], start=True, stop=False)
            mm(ps[1][:, 32:64], const("before"), chosen[:, 1], start=False, stop=True)
            mm(ps[1][:, 64:96], const("ones"), chosen[:, 0], start=True, stop=False)
            mm(ps[1][:, 64:96], const("ones"), chosen[:, 1], start=False, stop=True).then_inc(*L.mark("pos"))

            def gather():
                for k in range(KT):
                    for n, (s_, t) in enumerate([(s_, t) for s_ in range(3) for t in range(2)]):
                        last = mm(ps[2][:, SLOT * k:SLOT * k + SLOT], hparts[:, s_, t, 128 * k:128 * k + 128], Sb[:, t, :],
                                  start=(n == 0), stop=(n == 5))
                return last

            def scatter():
                for t in range(2):
                    for c_ in range(2):
                        r = slice(64 * c_, 64 * c_ + 64)
                        last = mm(ps[3 + 2 * t + c_], GT[r, t, :], ysb[r, :], start=True, stop=True)
                return last

            pe.wait_ge(*L.at("dve", "Sb1"))
            pe.wait_ge(*L.at("pool", "hparts"))
            pe.wait_ge(*L.at("pool", "zeros"))
            gather().then_inc(*L.mark("gather1"))
            pe.wait_ge(*L.own())
            pe.wait_ge(*L.at("act", "xcT1"))
            pe.wait_ge(*L.at("dve", "selb1"))
            L.stage("moe")

            def block_of_rows(turn):
                L.begin_turn(turn)
                pe.wait_ge(*L.at("act", "xcT", back=1))
                pe.wait_ge(*L.at("act", "hidT", back=1))
                pe.wait_ge(*L.at("dve", "hid", back=1))
                pe.wait_ge(*L.at("dve", "selb", back=1))
                for m in range(2):
                    for c_ in range(2):
                        mm(ps[m][64 * c_:64 * c_ + 64, :], selb[0:96, :], bias[0:96, m, 512 * c_:512 * c_ + 512],
                           start=True, stop=False)
                for j in range(4):
                    for m in range(2):
                        pe.wait_ge(sems(f"in_ring{2 * j + m}"), turn * 16)
                        for k in range(2 * j, 2 * j + 2):
                            for c_ in range(2):
                                last = mm(ps[m][64 * c_:64 * c_ + 64, :], xcT[:, k, :], ring[:, 2 * j + m, k % 2, 512 * c_:512 * c_ + 512],
                                          start=False, stop=(k == KT - 1))
                        last.then_inc(*L.mark("piece", 2 * j + m))
                pe.wait_ge(*L.at("act", "y", back=1))
                pe.wait_ge(*L.at("act", "GT", back=1))
                pe.wait_ge(*L.at("dve", "acc", back=1))
                scatter().then_inc(*L.mark("back"))
                pe.wait_ge(*L.at("dve", "Sb"))
                gather().then_inc(*L.mark("gather"))
                pe.wait_ge(*L.at("dve", "Sg"))
                for t in range(2):
                    last = nc.tensor.transpose(ps[7][:, 128 * t:128 * t + 128], Sg[:, t], ident)
                last.then_inc(*L.mark("GT"))
                pe.wait_ge(*L.at("dve", "hid"))
                for k in range(4):
                    last = nc.tensor.transpose(unit(ps[0], k), hid[:, 4, 128 * k:128 * k + 128], ident)
                last.then_inc(*L.mark("hidT"))
                pe.wait_ge(*L.at("act", "hidT"))
                pe.wait_ge(*L.at("act", "xcT"))
                for c_ in range(2):
                    mm(ps[2][64 * c_:64 * c_ + 64, :], selb[0:96, :], bias[0:96, 2, 512 * c_:512 * c_ + 512], start=True, stop=False)
                for j in range(4):
                    pe.wait_ge(sems(f"in_ring{8 + j}"), turn * 16)
                    for k in range(2 * j, 2 * j + 2):
                        for c_ in range(2):
                            last = mm(ps[2][64 * c_:64 * c_ + 64, :], hidT[:, k % 4, 64 * (k // 4):64 * (k // 4) + 64],
                                      ring[:, 8 + j, k % 2, 512 * c_:512 * c_ + 512], start=False, stop=(k == KT - 1))
                    last.then_inc(*L.mark("piece", 8 + j))
                L.end_turn()

            with pe.Fori(1, E_N + 1) as i:
                block_of_rows(i)
            L.turn = None
            pe.wait_ge(*L.at("dve", "table"))
            n_more = pe.value_load(intab[0:1, 15:16], min_val=0, max_val=MAX_MORE)
            with pe.Fori(0, MAX_MORE) as k:
                with pe.If(n_more > k):
                    block_of_rows(k + E_N + 1)
            L.turn = n_more + E_N + 1
            pe.wait_ge(*L.at("act", "y", back=1))
            pe.wait_ge(*L.at("act", "GT", back=1))
            pe.wait_ge(*L.at("dve", "acc", back=1))
            L.stage("end")
            scatter().then_inc(*L.mark("back1"))

        @block.scalar
        def _(act):
            L = lane("act")
            f = nc.scalar.activation

            def xt_out(L, f, t, n):
                act.wait_ge(*L.at("pe", "xT", t))
                act.wait_ge(*L.at("dve", "a1"))
                j = 0 if t >= 2 else 1
                base = {2: 256, 3: 384, 0: 0, 1: 128}[t]
                for k in range(KT):
                    src = ps[4 + 2 * (n % 2) + k // 4][:, (k % 4) * 128:(k % 4) * 128 + 128]
                    f(xmT[:, k, base:base + 128], src, ACT.Identity, scale=a1[:, k, j:j + 1], bias=modc[:, k, j:j + 1]).then_inc(*L.mark("xmT", t))
    
            def rsqrt_of(sums, step):
                act.wait_ge(*L.own())
                f(newt[:, 0:2, sums + 1:sums + 2], newt[:, 0:2, sums:sums + 1], ACT.Ln, scale=1.0 / D, bias=const("eps")).then_inc(*L.mark())
                act.wait_ge(*L.own())
                f(newt[:, 0:2, sums + 2:sums + 3], newt[:, 0:2, sums + 1:sums + 2], ACT.Exp, scale=-0.5).then_inc(*L.mark(step))

            L.stage("proj")
            act.wait_ge(*L.at("in", "cc", 1))
            cin = area("sc", 0, 16)
            f(newt[:, 0, :], cin, ACT.Exp, scale=-1.0).then_inc(*L.mark("ec"))
            act.wait_ge(*L.at("in", "const", 1))

            def mod_out(use):
                act.wait_ge(*L.at("pe", "ada", use))
                f(modp[:, 512 * use:512 * use + 512], ps[use % 2][:, :], ACT.Copy).then_inc(*L.mark("mod", use))

            def rstd(name, first, src):
                act.wait_ge(*L.at("in", name, 1))
                for t in range(2):
                    act.wait_ge(*L.own())
                    f(area("conv"), src[:, t], ACT.Square, accum_out=ssq[:, first + t:first + t + 1]).then_inc(*L.mark("ssq", first + t))
                act.wait_ge(*L.own())
                f(ssq[:, 4 + first:6 + first], ssq[:, first:first + 2], ACT.Ln, scale=1.0 / D, bias=const("eps")).then_inc(*L.mark())
                act.wait_ge(*L.own())
                f(ssq[:, 8 + first:10 + first], ssq[:, 4 + first:6 + first], ACT.Exp, scale=-0.5).then_inc(*L.mark("rstd0", first))
                book.new[("act", "rstd0", first + 1)] = book.new[("act", "rstd0", first)]

            for use in range(3):
                mod_out(use)
            rstd("x", 2, xin)
            mod_out(3)
            rstd("ctx", 0, ctx_in)
            act.wait_ge(*L.at("in", "small", 1))
            f(nega, a_log, ACT.Exp).then_inc(*L.mark("eA"))
            for n, t in enumerate((2, 3, 0, 1)):
                xt_out(L, f, t, n)
            act.wait_ge(*L.at("pe", "sm"))
            f(sm.rearrange("p a b -> p (a b)"), ps[3][:, 0:192], ACT.Copy).then_inc(*L.mark("sm"))
            act.wait_ge(*L.own())
            f(beta, sm[:, :, 0:16], ACT.Exp, scale=-1.0).then_inc(*L.mark("eb"))
            act.wait_ge(*L.at("dve", "absy"))
            f(tsp[:, 0], tsp[:, 0], ACT.Exp, scale=-1.0).then_inc(*L.mark("u"))
            act.wait_ge(*L.at("dve", "1+u"))
            f(tsp[:, 2], tsp[:, 1], ACT.Ln).then_inc(*L.mark("lnw"))
            for m in range(2):
                for t in range(2):
                    act.wait_ge(*L.at("pe", "zt", m, t))
                    f(zs[:, 2 * m + t], ps[t][:, :], ACT.Silu).then_inc(*L.mark("z", 2 * m + t))

            def silu_of(i):
                kind, j, both = FM[i]
                w = 512 if both else 256
                act.wait_ge(*L.at("dve", "conv", i))
                dst = {"k": kT, "q": qT, "b": bT, "c": cT}[kind][:, j] if kind in "kqbc" else conv[:, i % 2, 0:w]
                f(dst, conv[:, i % 2, 0:w], ACT.Silu).then_inc(*L.mark("silu", i))

            def turned_of(i):
                kind, j, both = FM[i]
                n = TURNED.index(i)
                act.wait_ge(*L.at("pe", "turn", i))
                dst = {"k": k_tm, "v": v_tm, "xs": xs_tm, "b": b_tm}[kind][:, :, 128 * j:128 * j + 128]
                f(dst, view(ps[4 + n % 2][:, :], 4, 128), ACT.Copy).then_inc(*L.mark("turned", i))

            for i in range(NFM + 1):
                if i < NFM:
                    kind, j, both = FM[i]
                    act.wait_ge(*L.at("pe", "fm", i))
                    act.wait_ge(*(L.at("dve", "padz") if i < 2 else L.at("dve", "conv", i - 2)))
                    w = 2 if both else 1
                    f(pad[:, i % 2, 0:w, 2:258], view(ps[i % 2][:, 0:256 * w], w, 256) if both
                      else ps[i % 2][:, 0:256].rearrange("p (a b) -> p a b", a=1), ACT.Copy).then_inc(*L.mark("pad", i))
                    if i <= NKQ + 1:
                        silu_of(i)
                if i == NKQ + 1:
                    for m in range(NKQ):
                        act.wait_ge(*L.at("pe", "ssq", m))
                        bk = ps[2 if m % 2 == 0 else 7]
                        f(norm_of(m), bk[:, 0:512 if FM[m][2] else 256], ACT.Ln, bias=const("eps")).then_inc(*L.mark("ln", m))
                    act.wait_ge(*L.own())
                    for m in range(NKQ):
                        f(norm_of(m), norm_of(m), ACT.Exp, scale=-0.5,
                          bias=const("lnq") if FM[m][0] == "q" else const("zero")).then_inc(*L.mark("rn", m))
                    act.wait_ge(*L.at("dve", "Gc"))
                    f(eG, Gc, ACT.Exp).then_inc(*L.mark("eG"))
                    f(egl, gl, ACT.Exp).then_inc(*L.mark("egl"))
                    act.wait_ge(*L.at("dve", "gl-G"))
                    f(ekd, ekd, ACT.Exp).then_inc(*L.mark("ekd"))
                if i > NKQ and i - 1 in TURNED:
                    turned_of(i - 1)
                if NKQ + 3 <= i < NKQ + 7:
                    turned_of(i - NKQ - 3)
                if ADA_AT <= i < ADA_AT + 8:
                    use = i - ADA_AT + 4
                    act.wait_ge(*L.at("pe", "ada", use))
                    if use > 4:
                        act.wait_ge(*L.at("pe", "row", use - 1))
                    f(modq, ps[3][:, :], ACT.Copy).then_inc(*L.mark("mod", use))
                if NKQ + 1 < i < NFM:
                    silu_of(i)
            act.wait_ge(*L.own())
            act.nop().then_inc(*L.mark("end", "proj"))
            barrier(act, L, "proj")

            L.stage("delta")
            groups = [(t, hp) for t in range(NT) for hp in range(4)]

            def bank(g, which):
                return ps[4 * (g % 2) + which]

            def decays(g):
                act.wait_ge(*L.at("dve", "rel", g))
                f(DT[:, g % 4], DT[:, g % 4], ACT.Exp).then_inc(*L.mark("DT", g))

            for h_ in (0, 1):
                decays(h_)
            for g in range(0, 16, 2):
                pair = (g, g + 1)
                for h_ in pair:
                    act.wait_ge(*L.at("pe", "X2", h_))
                    act.wait_ge(*L.own())
                    f(X[:, h_ % 2], view(bank(h_, 1)[:, :], 4, 128), ACT.Copy).then_inc(*L.mark("X", h_, LEVELS[0]))
                if g < 14:
                    for h_ in (g + 2, g + 3):
                        decays(h_)
                for z in LEVELS:
                    for h_ in pair:
                        if z < LEVELS[-1]:
                            act.wait_ge(*L.at("pe", "XQ", h_, z))
                            act.wait_ge(*L.own())
                            f(X[:, h_ % 2], view(bank(h_, 1)[:, :], 4, 128), ACT.Copy).then_inc(*L.mark("X", h_, 2 * z))
                        act.wait_ge(*L.at("pe", "QX", h_, z))
                        act.wait_ge(*L.own())
                        f(XT[:, h_ % 4], view(bank(h_, 2)[:, :], 4, 128), ACT.Copy).then_inc(*L.mark("XT", h_, 2 * z))
                for h_ in pair:
                    t, hp = groups[h_]
                    act.wait_ge(*L.at("pe", "W", h_))
                    f(WT[:, t, hp], view(bank(h_, 1)[:, 0:256], 2, 128), ACT.Copy, scale=-1.0).then_inc(*L.mark("WT", h_))
            act.wait_ge(*L.own())
            for t in range(2):
                act.wait_ge(*L.at("dve", "Oss", t))
                f(ssq[:, 8 * t:8 * t + 8], ngrp[:, t, 0:8], ACT.Ln, scale=1.0 / C, bias=const("eps")).then_inc(*L.mark())
                act.wait_ge(*L.own())
                f(ngrp[:, t, 8:16], ssq[:, 8 * t:8 * t + 8], ACT.Exp, scale=-0.5).then_inc(*L.mark("Or", t))
            act.wait_ge(*L.own())
            act.wait_ge(*L.own())
            act.nop().then_inc(*L.mark("end", "delta"))
            barrier(act, L, "delta")

            L.stage("ssd")
            for g in range(8):
                act.wait_ge(*L.at("dve", "srel", g))
                f(sDT[:, g % 2], sDT[:, g % 2], ACT.Exp).then_inc(*L.mark("sDT", g))
            def mixed_out(n, m, t):
                act.wait_ge(*L.at("pe", "mixT", m, t))
                src = view(ps[5 + n % 2][:, :], 4, 128)
                if m == 0:
                    f(mixT[:, 0:4, 128 * t:128 * t + 128], src, ACT.Copy).then_inc(*L.mark("mixT", m, t))
                else:
                    for k in range(4):
                        dst = mixT[:, 4 + k, :].rearrange("p (r w) -> p w r", r=ROWS)[:, 32 * t:32 * t + 32, :]
                        f(dst, src[:, k].rearrange("p (w r) -> p w r", r=ROWS), ACT.Copy).then_inc(*L.mark("mixT", m, t))

            for t in range(2):
                mixed_out(t, 0, t)
            act.wait_ge(*L.at("dve", "Yss", 1))
            act.wait_ge(*L.own())
            f(newt[:, 0:2, 13:15], ngrp[:, 0:2, 0:2], ACT.Ln, scale=1.0 / 256, bias=const("eps")).then_inc(*L.mark())
            act.wait_ge(*L.own())
            f(ngrp[:, 0:2, 2:4], newt[:, 0:2, 13:15], ACT.Exp, scale=-0.5).then_inc(*L.mark("Yr", 1))
            for n, (m, t) in ((2, (1, 0)), (3, (1, 1))):
                mixed_out(n, m, t)
            for t in range(2):
                act.wait_ge(*L.at("pe", "m", t))
                for c_ in range(2):
                    act.wait_ge(*L.own())
                    f(area("yt", 0, 512), ps[2 * t + c_][:, :], ACT.Square, accum_out=newt[:, t, c_:c_ + 1]).then_inc(*L.mark("mss", t))
            act.wait_ge(*L.at("dve", "msum"))
            rsqrt_of(2, "r1")
            act.wait_ge(*L.own())
            act.nop().then_inc(*L.mark("end", "ssd"))
            barrier(act, L, "ssd")

            L.stage("route")
            for t in range(2):
                act.wait_ge(*L.at("dve", "x1", t))
                act.wait_ge(*L.own())
                f(area("hT", 0, D), xin[:, t], ACT.Square, accum_out=newt[:, t, 5:6]).then_inc(*L.mark())
            rsqrt_of(5, "r2")
            for t in range(2):
                act.wait_ge(*L.at("pe", "hT", t))
                act.wait_ge(*L.own())
                for c_ in range(2):
                    f(hT[:, 4 * c_:4 * c_ + 4, 128 * t:128 * t + 128], view(ps[4 + 2 * t + c_][:, :], 4, 128), ACT.Copy).then_inc(*L.mark("hT", t))
            for t in range(2):
                act.wait_ge(*L.at("dve", "nmax", t))
                f(gexp[:, t], top[:, t, 0:4], ACT.Exp, bias=nmax[:, t], accum_out=gsum[:, t]).then_inc(*L.mark("gexp", t))
            act.wait_ge(*L.at("pe", "gather1"))
            f(xcT, view(ps[2][:, :], KT, SLOT), ACT.Copy).then_inc(*L.mark("xcT1"))
            act.wait_ge(*L.own())
            L.stage("moe")
            act.sem_inc(*L.open_loop())

            def block_of_rows(turn):
                L.begin_turn(turn)
                act.wait_ge(*L.at("dve", "a"))
                act.wait_ge(*L.at("dve", "hid", back=1))
                f(hid[:, 1], hid[:, 0], ACT.Sigmoid, scale=ALPHA).then_inc(*L.mark("sig"))
                act.wait_ge(*L.at("pe", "gather"))
                f(xcT, view(ps[2][:, :], KT, SLOT), ACT.Copy).then_inc(*L.mark("xcT"))
                act.wait_ge(*L.at("pe", "GT"))
                f(GT, view(ps[7][:, 0:256], 2, 128), ACT.Copy).then_inc(*L.mark("GT"))
                act.wait_ge(*L.at("pe", "hidT"))
                f(hidT, view(ps[0][:, :], 4, 128), ACT.Copy).then_inc(*L.mark("hidT"))
                act.wait_ge(*L.at("pe", "piece", 11))
                f(ysb, ps[2][:, :], ACT.Copy).then_inc(*L.mark("y"))
                L.end_turn()

            with act.Fori(1, E_N + 1) as i:
                block_of_rows(i)
            L.turn = None
            act.wait_ge(*L.at("dve", "table"))
            n_more = act.value_load(intab[0:1, 15:16], min_val=0, max_val=MAX_MORE)
            with act.Fori(0, MAX_MORE) as k:
                with act.If(n_more > k):
                    block_of_rows(k + E_N + 1)
            L.stage("end")
            for t in range(2):
                act.wait_ge(*L.at("dve", "sum", t))
                act.wait_ge(*L.own())
                f(area("hid", 0, D), acc[:, t], ACT.Square, accum_out=newt[:, t, 8:9]).then_inc(*L.mark())
            rsqrt_of(8, "r3")

        @block.vector
        def _(dve):
            L = lane("dve")
            v = nc.vector

            def refine(y, ms, tmp, scale):
                dve.wait_ge(*L.own())
                v.tensor_scalar(tmp[:, 0:1], ms, scale, EPS, ALU.mult, ALU.add).then_inc(*L.mark())
                dve.wait_ge(*L.own())
                v.tensor_tensor(tmp[:, 0:1], tmp[:, 0:1], y, ALU.mult).then_inc(*L.mark())
                dve.wait_ge(*L.own())
                v.tensor_tensor(tmp[:, 0:1], tmp[:, 0:1], y, ALU.mult).then_inc(*L.mark())
                dve.wait_ge(*L.own())
                v.tensor_scalar(tmp[:, 0:1], tmp[:, 0:1], -0.5, 1.5, ALU.mult, ALU.add).then_inc(*L.mark())
                dve.wait_ge(*L.own())
                v.tensor_tensor(tmp[:, 1:2], tmp[:, 0:1], y, ALU.mult).then_inc(*L.mark())
                dve.wait_ge(*L.own())
                return tmp[:, 1:2]

            def refine_both(sums):
                dve.wait_ge(*L.own())
                y, a, b = newt[:, 0:2, sums + 2:sums + 3], newt[:, 0:2, 11:12], newt[:, 0:2, 12:13]
                v.tensor_scalar(a, newt[:, 0:2, sums:sums + 1], 1.0 / D, EPS, ALU.mult, ALU.add).then_inc(*L.mark())
                dve.wait_ge(*L.own())
                v.tensor_tensor(a, a, y, ALU.mult).then_inc(*L.mark())
                dve.wait_ge(*L.own())
                v.tensor_tensor(a, a, y, ALU.mult).then_inc(*L.mark())
                dve.wait_ge(*L.own())
                v.tensor_scalar(a, a, -0.5, 1.5, ALU.mult, ALU.add).then_inc(*L.mark())
                dve.wait_ge(*L.own())
                v.tensor_tensor(b, a, y, ALU.mult).then_inc(*L.mark())
                dve.wait_ge(*L.own())

            L.stage("proj")
            v.memset(pad.rearrange("p a b c -> p (a b c)"), 0.0).then_inc(*L.mark("padz"))
            dve.wait_ge(*L.at("act", "ec"))
            v.tensor_scalar(newt[:, 0, :], newt[:, 0, :], 1.0, None, ALU.add).then_inc(*L.mark())
            dve.wait_ge(*L.own())
            v.reciprocal(newt[:, 0, :], newt[:, 0, :]).then_inc(*L.mark())
            dve.wait_ge(*L.own())
            dve.wait_ge(*L.at("in", "cc", 1))
            v.tensor_tensor(newt[:, 1, :], area("sc", 0, 16), newt[:, 0, :], ALU.mult).then_inc(*L.mark())
            dve.wait_ge(*L.own())
            v.memset(area("sc"), 0.0).then_inc(*L.mark())
            dve.wait_ge(*L.own())
            v.tensor_copy(sct[:, :, 0:2], newt[:, 1, :].rearrange("p (k j) -> p k j", j=2)).then_inc(*L.mark("sct"))
            for n, t in enumerate((2, 3, 0, 1)):
                dve.wait_ge(*L.at("act", "rstd0", t))
                r = refine(ssq[:, 8 + t:9 + t], ssq[:, t:t + 1], newt[:, 2, 2 * t:2 * t + 2], 1.0 / D)
                if n:
                    dve.wait_ge(*L.at("pe", "xT", (2, 3, 0, 1)[n - 1]))
                if t >= 2:
                    v.tensor_scalar(xh, xin[:, t - 2], r, None, ALU.mult).then_inc(*L.mark("xh", t))
                else:
                    dve.wait_ge(*L.at("in", "ctx", 1))
                    v.tensor_scalar(xh, ctx_in[:, t], r, None, ALU.mult).then_inc(*L.mark("xh", t))
                if n == 0:
                    dve.wait_ge(*L.at("pe", "modc"))
                    v.tensor_copy(modc, view(ps[2][:, 0:32], 16, 2)).then_inc(*L.mark())
                    dve.wait_ge(*L.own())
                    dve.wait_ge(*L.at("in", "cols", 1))
                    for j in range(2):
                        v.scalar_tensor_tensor(out=a1[:, :, j], in0=modc[:, 8:16, j], scalar=1.0, in1=npm,
                                                     op0=ALU.add, op1=ALU.mult).then_inc(*L.mark("a1"))
            dve.wait_ge(*L.at("act", "eA"))
            v.tensor_scalar(nega, nega, -1.0, None, ALU.mult).then_inc(*L.mark())
            dve.wait_ge(*L.at("act", "eb"))
            v.tensor_scalar(beta, beta, 1.0, None, ALU.add).then_inc(*L.mark())
            dve.wait_ge(*L.own())
            v.reciprocal(beta, beta).then_inc(*L.mark())
            for t in range(NT):
                v.tensor_tensor(sp_[:, t], sm[:, t, 16:48], dt_b, ALU.add).then_inc(*L.mark())
            dve.wait_ge(*L.own())
            v.scalar_tensor_tensor(out=tsp[:, 0], in0=sp_, scalar=-1.0, in1=sp_, op0=ALU.mult, op1=ALU.max).then_inc(*L.mark("absy"))
            dve.wait_ge(*L.at("act", "u"))
            v.tensor_scalar(tsp[:, 1], tsp[:, 0], 1.0, None, ALU.add).then_inc(*L.mark("1+u"))
            dve.wait_ge(*L.own())
            dve.wait_ge(*L.at("act", "lnw"))
            v.tensor_scalar(tsp[:, 1], tsp[:, 1], -1.0, None, ALU.add).then_inc(*L.mark())
            dve.wait_ge(*L.own())
            v.tensor_scalar(gA, tsp[:, 1], 0.0, None, ALU.is_equal).then_inc(*L.mark())
            dve.wait_ge(*L.own())
            v.tensor_tensor(tsp[:, 1], tsp[:, 1], gA, ALU.add).then_inc(*L.mark())
            dve.wait_ge(*L.own())
            v.reciprocal(tsp[:, 1], tsp[:, 1]).then_inc(*L.mark())
            dve.wait_ge(*L.own())
            v.tensor_tensor(tsp[:, 1], tsp[:, 1], tsp[:, 2], ALU.mult).then_inc(*L.mark())
            dve.wait_ge(*L.own())
            v.tensor_tensor(tsp[:, 1], tsp[:, 1], gA, ALU.add).then_inc(*L.mark())
            dve.wait_ge(*L.own())
            v.tensor_tensor(tsp[:, 1], tsp[:, 1], tsp[:, 0], ALU.mult).then_inc(*L.mark())
            dve.wait_ge(*L.own())
            v.scalar_tensor_tensor(out=sp_, in0=sp_, scalar=0.0, in1=tsp[:, 1], op0=ALU.max, op1=ALU.add).then_inc(*L.mark())
            dve.wait_ge(*L.own())
            for t in range(NT):
                v.tensor_tensor(gA[:, t], sp_[:, t], nega, ALU.mult).then_inc(*L.mark("gA"))
            def conv_of(i):
                kind, j, both = FM[i]
                n, w = (512, 2) if both else (256, 1)
                wi = {"q": 0, "k": 4, "v": 8, "xs": 12, "b": 16, "c": 18}[kind] + j
                dve.wait_ge(*L.at("act", "pad", i))
                if i >= 2:
                    dve.wait_ge(*(L.at("pe", "turn", i - 2) if FM[i - 2][0] in ("v", "xs") else L.at("act", "silu", i - 2)))
                dst = conv[:, i % 2, 0:n].rearrange("p (a b) -> p a b", a=w)
                for tap in range(5):
                    src = pad[:, i % 2, 0:w, tap:tap + 256]
                    if tap == 0:
                        if wi >= 12:
                            v.tensor_scalar(dst, src, convw[:, wi, 0:1], convb[:, wi - 12:wi - 11], ALU.mult, ALU.add).then_inc(*L.mark())
                        else:
                            v.tensor_scalar(dst, src, convw[:, wi, 0:1], None, ALU.mult).then_inc(*L.mark())
                    else:
                        dve.wait_ge(*L.own())
                        v.scalar_tensor_tensor(out=dst, in0=src, scalar=convw[:, wi, tap:tap + 1], in1=dst,
                                                     op0=ALU.mult, op1=ALU.add).then_inc(*L.mark("conv", i))

            def row_out(use):
                dve.wait_ge(*L.at("in", "wrow", 1))
                dve.wait_ge(*L.at("pe", "row", use))
                which, c_ = divmod(use - 4, 2)
                r = slice(512 * c_, 512 * c_ + 512)
                src = ps[7][:, :]
                if which == 0:
                    v.tensor_tensor(rows[:, 0, r], src, rows[:, 0, r], ALU.mult).then_inc(*L.mark("row", use))
                elif which == 1:
                    v.tensor_copy(rows[:, 3, r], src).then_inc(*L.mark("row", use))
                elif which == 2:
                    v.scalar_tensor_tensor(out=rows[:, 1, r], in0=src, scalar=1.0, in1=rows[:, 1, r],
                                                 op0=ALU.add, op1=ALU.mult).then_inc(*L.mark("row", use))
                else:
                    v.tensor_tensor(rows[:, 2, r], src, rows[:, 2, r], ALU.mult).then_inc(*L.mark("row", use))

            for i in range(NFM + 1):
                if i < NFM:
                    conv_of(i)
                if ADA_AT <= i < ADA_AT + 8:
                    row_out(i - ADA_AT + 4)
                if i == 1:
                    dve.wait_ge(*L.at("pe", "cum"))
                    for d in range(2):
                        for t in range(NT):
                            v.tensor_copy(Gc[:, t].rearrange("p (k d h) -> p k d h", k=2, d=2)[:, :, d, :],
                                                view(ps[6][:, d * 64 + t * 16:d * 64 + t * 16 + 16], 2, 8)).then_inc(*L.mark())
                    v.tensor_copy(gl, view(ps[6][:, 128:256], 4, 32)).then_inc(*L.mark("Gc"))
                    dve.wait_ge(*L.own())
                    v.tensor_tensor(ekd, gl, Gc, ALU.subtract).then_inc(*L.mark("gl-G"))
                if i == NKQ + 3:
                    dve.wait_ge(*L.at("pe", "eglb"))
                    v.tensor_copy(eglb.rearrange("p a b c -> p (a b c)"), ps[6][:, 256:512]).then_inc(*L.mark("eglb"))
            dve.wait_ge(*L.own())
            dve.nop().then_inc(*L.mark("end", "proj"))
            barrier(dve, L, "proj")

            L.stage("delta")
            groups = [(t, hp) for t in range(NT) for hp in range(4)]

            def bank(g, which):
                return ps[4 * (g % 2) + which]

            def decay(g):
                t, hp = groups[g]
                dve.wait_ge(*L.at("pe", "Gb", g))
                if g >= 4:
                    dve.wait_ge(*L.at("pe", "QX", g - 4, LEVELS[-1]))
                dve.wait_ge(*L.own())
                for u in range(4):
                    par, d = divmod(u, 2)
                    ch = d * 8 + 2 * hp + par
                    v.scalar_tensor_tensor(out=DT[:, g % 4, u], in0=bank(g, 3)[:, 128 * u:128 * u + 128],
                                                 scalar=Gc[:, t, ch:ch + 1], in1=neg[:, d], op0=ALU.subtract, op1=ALU.min).then_inc(*L.mark("rel", g))

            def gram(par):
                return ps[3 + 4 * par]

            def couple(g):
                t, hp = groups[g]
                dve.wait_ge(*L.at("pe", "gram", g - g % 2))
                dve.wait_ge(*L.at("act", "DT", g))
                if g >= 4:
                    dve.wait_ge(*L.at("pe", "W", g - 4))
                for u in range(4):
                    par, d = divmod(u, 2)
                    ch = d * 8 + 2 * hp + par
                    v.scalar_tensor_tensor(out=MT[:, g % 4, u], in0=gram(par)[:, 256 * (g % 2):256 * (g % 2) + 128],
                                                 scalar=beta[:, t, ch:ch + 1], in1=DT[:, g % 4, u], op0=ALU.mult, op1=ALU.mult).then_inc(*L.mark("N", g))
                if t >= 2:
                    for par in range(2):
                        for d in range(2):
                            v.tensor_tensor(attnT[:, t - 2, hp, par, d], gram(par)[:, 256 * (g % 2) + 128:256 * (g % 2) + 256],
                                                  DT[:, g % 4, 2 * par + d], ALU.mult).then_inc(*L.mark("N", g))

            def level(g, z):
                dve.wait_ge(*L.at("pe", "P", g, z))
                dve.wait_ge(*L.own())
                zi = LEVELS.index(z)
                for par in range(2):
                    v.tensor_tensor(Q[:, g % 4, 2 * par:2 * par + 2], view(bank(g, 0)[:, 256 * par:256 * par + 256], 2, 128),
                                          qmask[:, zi], ALU.mult).then_inc(*L.mark("Q", g, z))

            def u_out(g):
                t, hp = groups[g]
                dve.wait_ge(*L.at("pe", "U", g))
                for d in range(2):
                    for half in range(2):
                        n = step_of(2 * t + half, d)
                        r = slice(64 * half, 64 * half + 64)
                        v.tensor_copy(US[r, n, 128 * hp:128 * hp + 128], bank(g, 3)[r, 128 * d:128 * d + 128]).then_inc(*L.mark("U", g))

            for h_ in (0, 1):
                decay(h_)
            for h_ in (0, 1):
                couple(h_)
            for g in range(0, 16, 2):
                pair, more = (g, g + 1), g < 14
                if more:
                    decay(g + 2)
                    decay(g + 3)
                for n, z in enumerate(LEVELS):
                    for h_ in pair:
                        level(h_, z)
                    if more and n in (1, 2):
                        couple(g + 1 + n)
                for h_ in pair:
                    u_out(h_)
            dve.wait_ge(*L.at("pool", "betaS"))
            for n in range(8):
                vn = vS[:, n % 4]
                bb = betaS[:, n].unsqueeze(2).broadcast_to([P, H, C])
                if n:
                    dve.wait_ge(*L.at("pe", "WS", n))
                    if n >= 4:
                        dve.wait_ge(*L.at("pe", "KV", n - 4))
                    dve.wait_ge(*L.own())
                    for par in range(2):
                        u_ = US[:, n].rearrange("p (a b c) -> p a b c", a=4, b=2)[:, :, par, :]
                        v.tensor_tensor(u_, u_, view(ps[2 * (n % 2) + par][:, 0:256], 4, C), ALU.add).then_inc(*L.mark())
                dve.wait_ge(*L.own())
                v.tensor_tensor(view(vn, H, C), view(US[:, n], H, C), bb, ALU.mult).then_inc(*L.mark("v", n))
                if n == 7:
                    break
                nxt = S[:, n + 1 - 4] if n + 1 >= 4 else Sx
                dve.wait_ge(*L.at("pe", "KV", n))
                dve.wait_ge(*L.own())
                if n == 0:
                    for d in range(2):
                        v.tensor_copy(nxt[:, 256 * d:256 * d + 256], ps[4 + d][:, 0:256]).then_inc(*L.mark("S", 1))
                else:
                    dve.wait_ge(*L.at("pool", "Se", n))
                    for d in range(2):
                        c_ = slice(256 * d, 256 * d + 256)
                        v.tensor_tensor(nxt[:, c_], US[:, n, c_], ps[4 + 2 * (n % 2) + d][:, 0:256], ALU.add).then_inc(*L.mark("S", n + 1))
            O = view(area("DT", 0, 1024), 2, 512)
            for t in range(2):
                dve.wait_ge(*L.at("pe", "O", t))
                dve.wait_ge(*L.own())
                o_, tmp = O[:, t], area("MT", 512 * t, 512)
                for d in range(2):
                    for par in range(2):
                        e_ = eG[:, 2 + t, 8 * d + par:8 * d + 8:2].unsqueeze(2).broadcast_to([P, 4, C])
                        dst = (o_ if d == 0 else tmp).rearrange("p (a b c) -> p a b c", a=4, b=2)[:, :, par, :]
                        v.tensor_tensor(dst, view(ps[par][:, 256 * d:256 * d + 256], 4, C), e_, ALU.mult).then_inc(*L.mark())
                dve.wait_ge(*L.own())
                v.tensor_tensor(o_, o_, tmp, ALU.add).then_inc(*L.mark())
                dve.wait_ge(*L.own())
                v.tensor_tensor(o_, o_, ps[4][:, :], ALU.add).then_inc(*L.mark("O", t))
                dve.wait_ge(*L.own())
                v.tensor_tensor(tmp, o_, o_, ALU.mult).then_inc(*L.mark())
                dve.wait_ge(*L.own())
                v.tensor_reduce(ngrp[:, t, 0:8], view(tmp, H, C), AX.X, ALU.add).then_inc(*L.mark("Oss", t))
            for t in range(2):
                o_ = O[:, t]
                dve.wait_ge(*L.at("act", "Or", t))
                dve.wait_ge(*L.own())
                v.tensor_tensor(view(o_, H, C), view(o_, H, C), ngrp[:, t, 8:16].unsqueeze(2).broadcast_to([P, H, C]), ALU.mult).then_inc(*L.mark())
                dve.wait_ge(*L.own())
                v.tensor_tensor(view(o_, H, C), view(o_, H, C), gnw.unsqueeze(1).broadcast_to([P, H, C]), ALU.mult).then_inc(*L.mark())
                dve.wait_ge(*L.own())
                v.tensor_tensor(zs[:, t], o_, zs[:, t], ALU.mult).then_inc(*L.mark("gdn", t))
            dve.wait_ge(*L.own())
            dve.nop().then_inc(*L.mark("end", "delta"))
            barrier(dve, L, "delta")

            L.stage("ssd")
            for g in range(8):
                t, hp = divmod(g, 4)
                dve.wait_ge(*L.at("pe", "sG", g))
                if g >= 2:
                    dve.wait_ge(*L.at("pool", "sM", g - 2))
                for u in range(4):
                    par, d = divmod(u, 2)
                    ch = 16 + d * 8 + 2 * hp + par
                    v.scalar_tensor_tensor(out=sDT[:, g % 2, u], in0=ps[g % 2][:, 128 * u:128 * u + 128],
                                                 scalar=Gc[:, 2 + t, ch:ch + 1], in1=neg[:, d], op0=ALU.subtract, op1=ALU.min).then_inc(*L.mark("srel", g))
                dve.wait_ge(*L.at("act", "sDT", g))
                dve.wait_ge(*L.at("pe", "cb"))
                for u in range(4):
                    par, d = divmod(u, 2)
                    ch = 16 + d * 8 + 2 * hp + par
                    grp = (2 * hp + par) // 4
                    v.scalar_tensor_tensor(out=sDT[:, g % 2, u], in0=ps[7][:, (2 * t + grp) * 128:(2 * t + grp) * 128 + 128],
                                                 scalar=sp_[:, 2 + t, ch:ch + 1], in1=sDT[:, g % 2, u], op0=ALU.mult, op1=ALU.mult).then_inc(*L.mark("smt", g))
            for n in range(7):
                for d in range(2):
                    dve.wait_ge(*L.at("pe", "BX", n, d))
                    dst = SS[:, n - 3, d] if n >= 3 else SSt[:, d]
                    dve.wait_ge(*L.own())
                    if n == 0:
                        v.tensor_copy(dst, ps[2 + d][:, :]).then_inc(*L.mark("SS", 1, d))
                    else:
                        dve.wait_ge(*L.at("pool", "SSe", n, d))
                        v.tensor_tensor(dst, dst, ps[2 + 2 * (n % 2) + d][:, :], ALU.add).then_inc(*L.mark("SS", n + 1, d))
            for t in range(2):
                dve.wait_ge(*L.at("pe", "Y", t))
                for d in range(2):
                    e_ = eG[:, 2 + t, 16 + 8 * d:24 + 8 * d].unsqueeze(2).broadcast_to([P, H, C])
                    v.tensor_tensor(view(yt[:, 2 * t + d], H, C), view(ps[2 + d][:, :], H, C), e_, ALU.mult).then_inc(*L.mark())
                dve.wait_ge(*L.own())
                y_ = yt[:, 2 * t]
                v.tensor_tensor(y_, y_, yt[:, 2 * t + 1], ALU.add).then_inc(*L.mark())
                dve.wait_ge(*L.own())
                v.tensor_tensor(y_, y_, ps[4][:, :], ALU.add).then_inc(*L.mark("Y", t))
                v.tensor_tensor(view(yt[:, 2 * t + 1], H, C), view(xs_tm[:, 2 + t], H, C),
                                      dskip.unsqueeze(2).broadcast_to([P, H, C]), ALU.mult).then_inc(*L.mark())
                dve.wait_ge(*L.own())
                v.tensor_tensor(y_, y_, yt[:, 2 * t + 1], ALU.add).then_inc(*L.mark())
                dve.wait_ge(*L.own())
                v.tensor_tensor(y_, y_, zs[:, 2 + t], ALU.mult).then_inc(*L.mark())
                dve.wait_ge(*L.own())
                v.tensor_tensor(yt[:, 2 * t + 1], y_, y_, ALU.mult).then_inc(*L.mark())
                dve.wait_ge(*L.own())
                v.tensor_reduce(ngrp[:, t, 0:2], view(yt[:, 2 * t + 1], 2, 256), AX.X, ALU.add).then_inc(*L.mark("Yss", t))
            for t in range(2):
                dve.wait_ge(*L.at("act", "Yr", 1))
                dve.wait_ge(*L.own())
                for g in range(2):
                    v.tensor_scalar(yt[:, 2 * t, 256 * g:256 * g + 256], yt[:, 2 * t, 256 * g:256 * g + 256],
                                          ngrp[:, t, 2 + g:3 + g], None, ALU.mult).then_inc(*L.mark("yn", t))
            dve.wait_ge(*L.at("in", "bias", 9))
            bst, biasf = area("bstage"), area("bias").bitcast(BF16)
            parts = [slice(32 * part, 32 * part + 32) for part in range(3)]
            v.tensor_copy(biasf[0:96, :], bst[0:96, :]).then_inc(*L.mark())
            for first in (1, 2):
                dve.wait_ge(*L.own())
                for r in parts[first:]:
                    v.tensor_tensor(bst[r, :], bst[r, :], biasf[r, :], ALU.subtract).then_inc(*L.mark())
                dve.wait_ge(*L.own())
                for r in parts[first:]:
                    v.tensor_copy(biasf[r, :], bst[r, :]).then_inc(*L.mark())
            for t in range(2):
                dve.wait_ge(*L.at("act", "mss", t))
                dve.wait_ge(*L.own())
                v.tensor_tensor(newt[:, t, 2:3], newt[:, t, 0:1], newt[:, t, 1:2], ALU.add).then_inc(*L.mark("msum"))
            dve.wait_ge(*L.at("act", "r1"))
            refine_both(2)
            for t in range(2):
                r = newt[:, t, 12:13]
                if t == 0:
                    for tt in range(2):
                        dve.wait_ge(*L.at("pe", "m", tt))
                for c_ in range(2):
                    s_ = slice(512 * c_, 512 * c_ + 512)
                    v.scalar_tensor_tensor(out=mix[:, t, s_], in0=ps[2 * t + c_][:, :], scalar=r, in1=rows[:, 0, s_],
                                                 op0=ALU.mult, op1=ALU.mult).then_inc(*L.mark())
                dve.wait_ge(*L.own())
                v.tensor_tensor(xin[:, t], mix[:, t], xin[:, t], ALU.add).then_inc(*L.mark("x1", t))
            dve.wait_ge(*L.own())
            dve.nop().then_inc(*L.mark("end", "ssd"))
            barrier(dve, L, "ssd")

            L.stage("route")
            dve.wait_ge(*L.at("act", "r2"))
            refine_both(5)
            for t in range(2):
                r = newt[:, t, 12:13]
                v.scalar_tensor_tensor(out=hm[:, t], in0=xin[:, t], scalar=r, in1=rows[:, 1], op0=ALU.mult, op1=ALU.mult).then_inc(*L.mark())
                dve.wait_ge(*L.own())
                v.tensor_tensor(hm[:, t], hm[:, t], rows[:, 3], ALU.add).then_inc(*L.mark("h", t))
            for s_ in range(3):
                dve.wait_ge(*L.own())
                v.tensor_copy(hparts[:, s_, 0], hm[:, 0] if s_ == 0 else x1[:, 0]).then_inc(*L.mark())
                if s_ < 2:
                    dve.wait_ge(*L.own())
                    v.tensor_tensor(x1[:, 0], hm[:, 0] if s_ == 0 else x1[:, 0], hparts[:, s_, 0], ALU.subtract).then_inc(*L.mark())
            for t in range(2):
                dve.wait_ge(*L.at("pe", "logit", t))
                v.tensor_tensor(logit[:, t], ps[2 * t][:, 0:32], b_rt, ALU.add).then_inc(*L.mark())
                dve.wait_ge(*L.own())
                v.max(top[:, t], logit[:, t]).then_inc(*L.mark())
                dve.wait_ge(*L.own())
                v.max_index(topi[:, t], top[:, t], logit[:, t]).then_inc(*L.mark())
                v.tensor_scalar(nmax[:, t], top[:, t, 0:1], -1.0, None, ALU.mult).then_inc(*L.mark("nmax", t))
                dve.wait_ge(*L.own())
                v.tensor_copy(topf[:, t], topi[:, t]).then_inc(*L.mark())
                dve.wait_ge(*L.at("act", "gexp", t))
                v.reciprocal(gsum[:, t], gsum[:, t]).then_inc(*L.mark())
                dve.wait_ge(*L.own())
                v.tensor_scalar(gexp[:, t], gexp[:, t], gsum[:, t], None, ALU.mult).then_inc(*L.mark())
                dve.wait_ge(*L.own())
                for k in range(TOP_K):
                    dst = (chosen[:, t], gate[:, t]) if k == 0 else (oneh[:, t], rtmp[:, t])
                    dve.wait_ge(*L.own())
                    v.tensor_scalar(dst[0], const("iota32"), topf[:, t, k:k + 1], None, ALU.is_equal).then_inc(*L.mark())
                    v.tensor_scalar(dst[1], const("iota32"), topf[:, t, k:k + 1], gexp[:, t, k:k + 1], ALU.is_equal, ALU.mult).then_inc(*L.mark())
                    if k:
                        dve.wait_ge(*L.own())
                        v.tensor_tensor(chosen[:, t], chosen[:, t], oneh[:, t], ALU.add).then_inc(*L.mark("chosen"))
                        v.tensor_tensor(gate[:, t], gate[:, t], rtmp[:, t], ALU.add).then_inc(*L.mark())
            def choose(slots, column, step):
                for t in range(2):
                    v.tensor_scalar(Sb[:, t], const("slots", 0, SLOT), slots[:, t, column], None, ALU.is_equal).then_inc(*L.mark(*step))

            def choose_bias(rows_of, column, step):
                v.tensor_scalar(selb[0:96, :], const("ones", 0, 64)[0:96, :], rows_of[0:96, column], None, ALU.mult).then_inc(*L.mark(*step))

            dve.wait_ge(*L.at("pe", "pos"))
            dve.wait_ge(*L.own())
            v.scalar_tensor_tensor(out=pos, in0=view(ps[1][:, 0:64], 2, 32), scalar=1.0, in1=chosen, op0=ALU.add, op1=ALU.mult).then_inc(*L.mark())
            v.tensor_copy(cnt, ps[1][:, 64:96]).then_inc(*L.mark())
            dve.wait_ge(*L.own())
            v.tensor_scalar(pos, pos, -1.0, None, ALU.add).then_inc(*L.mark())
            dve.wait_ge(*L.own())
            choose(pos, slice(0, 1), ("Sb1",))
            choose_bias(const("eye96"), slice(0, 1), ("selb1",))
            v.tensor_scalar(extra, cnt, float(SLOT), None, ALU.is_gt).then_inc(*L.mark())
            v.memset(onesr, 1.0).then_inc(*L.mark())
            for more in range(2, SEQ // SLOT):
                dve.wait_ge(*L.own())
                v.scalar_tensor_tensor(out=extra, in0=cnt, scalar=float(more * SLOT), in1=extra, op0=ALU.is_gt, op1=ALU.add).then_inc(*L.mark())
            dve.wait_ge(*L.own())
            v.tensor_tensor_scan(cum, onesr, extra, 0.0, ALU.mult, ALU.add).then_inc(*L.mark())
            dve.wait_ge(*L.own())
            v.tensor_tensor(more_le, cum.unsqueeze(1).broadcast_to([P, 16, 32]),
                                  const("k16").unsqueeze(2).broadcast_to([P, 16, 32]), ALU.is_le).then_inc(*L.mark())
            dve.wait_ge(*L.own())
            v.tensor_reduce(more_e, more_le, AX.X, ALU.add).then_inc(*L.mark())
            dve.wait_ge(*L.own())
            v.tensor_tensor(more_le, more_le, extra.unsqueeze(1).broadcast_to([P, 16, 32]), ALU.mult).then_inc(*L.mark())
            dve.wait_ge(*L.own())
            v.tensor_reduce(more_b, more_le, AX.X, ALU.add).then_inc(*L.mark())
            dve.wait_ge(*L.own())
            v.tensor_tensor(more_b, const("k16"), more_b, ALU.subtract).then_inc(*L.mark())
            dve.wait_ge(*L.own())
            v.tensor_scalar(more_b, more_b, 1.0, float(SLOT), ALU.add, ALU.mult).then_inc(*L.mark())
            v.tensor_scalar(table, more_e, float(E_N - 1), None, ALU.min).then_inc(*L.mark())
            dve.wait_ge(*L.own())
            v.tensor_copy(table[:, 15:16], cum[:, 31:32]).then_inc(*L.mark())
            dve.wait_ge(*L.own())
            v.tensor_copy(intab[0:1, :], table[0:1, :]).then_inc(*L.mark("table"))

            v.tensor_tensor(owner, more_e.unsqueeze(2).broadcast_to([P, 16, 32]),
                            const("iota32").unsqueeze(1).broadcast_to([P, 16, 32]), ALU.is_equal).then_inc(*L.mark())
            for src, dst in ([(pos[:, t], posb[:, t]) for t in range(2)] + [(gate[:, t], gateb[:, t]) for t in range(2)]
                             + [(const("eye96"), eyeb)]):
                dve.wait_ge(*L.own())
                v.tensor_copy(dst[:, 0:E_N], src).then_inc(*L.mark())
                v.tensor_tensor(more_le, owner, src.unsqueeze(1).broadcast_to([P, 16, 32]), ALU.mult).then_inc(*L.mark())
                dve.wait_ge(*L.own())
                v.tensor_reduce(dst[:, E_N:48], more_le, AX.X, ALU.add).then_inc(*L.mark())
            for t in range(2):
                v.tensor_tensor(posb[:, t, E_N:48], posb[:, t, E_N:48], more_b, ALU.subtract).then_inc(*L.mark())

            dve.wait_ge(*L.own())
            dve.wait_ge(*L.at("pe", "gather1"))
            dve.wait_ge(*L.at("pool", "zeros"))
            L.stage("moe")
            dve.sem_inc(*L.open_loop())

            def add_rows(t):
                for c_ in range(2):
                    s_ = slice(512 * c_, 512 * c_ + 512)
                    v.tensor_tensor(acc[:, t, s_], acc[:, t, s_], ps[3 + 2 * t + c_][:, :], ALU.add).then_inc(*L.mark(*(("acc",) if L.turn is not None else ("sum", t))))

            def block_of_rows(turn):
                L.begin_turn(turn)
                dve.wait_ge(*L.own())
                dve.wait_ge(*L.at("pe", "gather", back=1))
                choose(posb, bass.ds(turn, 1), ("Sb",))
                dve.wait_ge(*L.at("pe", "GT", back=1))
                for t in range(2):
                    v.tensor_scalar(Sg[:, t], const("slots"), posb[:, t, bass.ds(turn - 1, 1)], gateb[:, t, bass.ds(turn - 1, 1)],
                                    ALU.is_equal, ALU.mult).then_inc(*L.mark("Sg"))
                dve.wait_ge(*L.at("pe", "piece", 6))
                dve.wait_ge(*L.at("act", "sig", back=1))
                v.tensor_scalar(hid[:, 0], ps[0][:, :], LIMIT, None, ALU.min).then_inc(*L.mark("a"))
                dve.wait_ge(*L.at("pe", "piece", 7))
                v.tensor_scalar(hid[:, 2], ps[1][:, :], LIMIT, -LIMIT, ALU.min, ALU.max).then_inc(*L.mark())
                dve.wait_ge(*L.own())
                v.scalar_tensor_tensor(out=hid[:, 3], in0=hid[:, 2], scalar=1.0, in1=hid[:, 0], op0=ALU.add, op1=ALU.mult).then_inc(*L.mark())
                dve.wait_ge(*L.at("act", "sig"))
                dve.wait_ge(*L.own())
                v.tensor_tensor(hid[:, 4], hid[:, 3], hid[:, 1], ALU.mult).then_inc(*L.mark("hid"))
                dve.wait_ge(*L.at("pe", "back"))
                for t in range(2):
                    add_rows(t)
                dve.wait_ge(*L.at("pe", "piece", 8))
                choose_bias(eyeb, bass.ds(turn, 1), ("selb",))
                L.end_turn()

            with dve.Fori(1, E_N + 1) as i:
                block_of_rows(i)
            L.turn = None
            n_more = dve.value_load(intab[0:1, 15:16], min_val=0, max_val=MAX_MORE)
            with dve.Fori(0, MAX_MORE) as k:
                with dve.If(n_more > k):
                    block_of_rows(k + E_N + 1)
            L.begin_turn(n_more + E_N + 1)
            dve.wait_ge(*L.own())
            L.turn = None
            L.stage("end")
            dve.wait_ge(*L.at("pe", "back1"))
            for t in range(2):
                add_rows(t)
            dve.wait_ge(*L.at("act", "r3"))
            refine_both(8)
            for t in range(2):
                r = newt[:, t, 12:13]
                v.scalar_tensor_tensor(out=acc[:, t], in0=acc[:, t], scalar=r, in1=rows[:, 2], op0=ALU.mult, op1=ALU.mult).then_inc(*L.mark())
                dve.wait_ge(*L.own())
                v.tensor_tensor(hm[:, t], acc[:, t], xin[:, t], ALU.add).then_inc(*L.mark("out", t))

        @block.gpsimd
        def _(pool):
            L = lane("pool")
            g_ = nc.gpsimd
            L.stage("proj")
            pool.wait_ge(*L.at("act", "xmT", 3))
            for r in range(ROWS):
                dst = xmT[:, :, 512:768].rearrange("p k (w r) -> p k w r", r=ROWS)[:, :, :, r]
                pool.wait_ge(*L.own())
                g_.tensor_copy(dst, xmT[:, :, 256 + 64 * r:320 + 64 * r]).then_inc(*L.mark("perm"))

            for i in range(NKQ):
                kind, j, both = FM[i]
                src = {"k": kT, "q": qT}[kind][:, j]
                pool.wait_ge(*L.at("act", "silu", i))
                pool.wait_ge(*L.own())
                g_.tensor_tensor(norm_of(i), src, src, ALU.mult).then_inc(*L.mark("sq", i))
            for i in range(NKQ):
                kind, j, both = FM[i]
                dst = {"k": kT, "q": qT}[kind][:, j]
                pool.wait_ge(*L.at("act", "rn", i))
                pool.wait_ge(*L.own())
                g_.tensor_tensor(dst, dst, norm_of(i), ALU.mult).then_inc(*L.mark("kT", i))
            pool.wait_ge(*L.own())
            pool.nop().then_inc(*L.mark("end", "proj"))
            barrier(pool, L, "proj")

            L.stage("delta")
            def keg(g):
                t, hp = divmod(g, 4)
                pool.wait_ge(*L.at("pe", "P", g, LEVELS[-1]))
                for d in range(2):
                    e_ = eG[:, t, 8 * d + 2 * hp:8 * d + 2 * hp + 2].unsqueeze(2).broadcast_to([P, 2, C])
                    pool.wait_ge(*L.own())
                    g_.tensor_tensor(keG[g % 4][:, d], view(k_tm[:, t, 128 * hp:128 * hp + 128], 2, C), e_, ALU.mult).then_inc(*L.mark("keG", g))

            def unit_diagonal(g):
                b = g % 4
                pool.wait_ge(*L.at("dve", "N", g))
                pool.wait_ge(*L.own())
                g_.affine_select(out=MT[:, b], in_=MT[:, b], compare_op=ALU.not_equal, fill=1.0, base=0,
                                       pattern=[[0, 4], [-1, 128]], channel_multiplier=1).then_inc(*L.mark("unit", g))
                pool.wait_ge(*L.own())
                if g >= 4:
                    pool.wait_ge(*L.at("pe", "U", g - 4))
                for par in range(2):
                    pool.wait_ge(*L.own())
                    g_.tensor_tensor(XT[:, b, 2 * par:2 * par + 2], MT[:, b, 2 * par:2 * par + 2], m1t, ALU.mult).then_inc(*L.mark("X2T", g))

            parts = [(t, d, half) for t in range(NT) for d in range(2) for half in range(2)]
            unit_diagonal(0)
            unit_diagonal(1)
            for half in range(2):
                r = slice(64 * half, 64 * half + 64)
                for t in range(NT):
                    for d in range(2):
                        n = step_of(2 * t + half, d)
                        pool.wait_ge(*L.own())
                        g_.tensor_copy(betaS[r, n], beta[r, t, 8 * d:8 * d + 8]).then_inc(*L.mark("betaS"))
            for par in range(2):
                r = slice(64 * par, 64 * par + 64)
                for c_ in range(8):
                    for d in range(2):
                        pool.wait_ge(*L.own())
                        g_.tensor_copy(eglS[r, step_of(c_, d), d], eglb[r, c_ % 2, c_ // 2, 8 * d + par:8 * d + 8:2]).then_inc(*L.mark("eglS"))
            for g in range(0, 16, 2):
                if g < 14:
                    unit_diagonal(g + 2)
                    unit_diagonal(g + 3)
                keg(g)
                keg(g + 1)
                for t, d, half in parts[g:g + 2]:
                    r = slice(64 * half, 64 * half + 64)
                    e_ = ekd[r, t, 8 * d:8 * d + 8].unsqueeze(2).broadcast_to([64, H, C])
                    pool.wait_ge(*L.own())
                    g_.tensor_tensor(view(kdS[r, step_of(2 * t + half, d)], H, C), view(k_tm[r, t], H, C), e_, ALU.mult).then_inc(*L.mark("kdS"))
            for n in range(1, 7):
                cur = S[:, n - 4] if n >= 4 else Sx
                pool.wait_ge(*L.at("dve", "v", n))
                pool.wait_ge(*L.own())
                e_ = eglS[:, n].rearrange("p a b -> p (a b)").unsqueeze(2).broadcast_to([P, 8, C])
                pool.wait_ge(*L.own())
                g_.tensor_tensor(view(US[:, n], 8, C), view(cur, 8, C), e_, ALU.mult).then_inc(*L.mark("Se", n))
            pool.wait_ge(*L.own())
            pool.nop().then_inc(*L.mark("end", "delta"))
            barrier(pool, L, "delta")

            L.stage("ssd")
            for d in range(2):
                for t in range(NT):
                    pool.wait_ge(*L.own())
                    g_.tensor_tensor(wss[:, t, 8 * d:8 * d + 8], ekd[:, t, 16 + 8 * d:24 + 8 * d], sp_[:, t, 16 + 8 * d:24 + 8 * d], ALU.mult).then_inc(*L.mark())
            pool.wait_ge(*L.own())
            for g in range(8):
                t, hp = divmod(g, 4)
                pool.wait_ge(*L.at("dve", "smt", g))
                s4 = sDT[:, g % 2].rearrange("p (a b) c -> p a b c", a=2)
                pool.wait_ge(*L.own())
                g_.tensor_tensor(sMT[:, t, 2 * hp:2 * hp + 2], s4[:, :, 0], s4[:, :, 1], ALU.add).then_inc(*L.mark("sM", g))
                tile, d = ((0, 0), (1, 1), (1, 0), (0, 1), (2, 0), (3, 1), (3, 0), (2, 1))[g]
                e_ = wss[:, tile, 8 * d:8 * d + 8].unsqueeze(2).broadcast_to([P, H, C])
                pool.wait_ge(*L.own())
                g_.tensor_tensor(view(xw[:, tile, d], H, C), view(xs_tm[:, tile], H, C), e_, ALU.mult).then_inc(*L.mark("xw", tile, d))
            for n in range(1, 7):
                for d in range(2):
                    c_ = n if d == 0 else 4 * (n // 4) + 3 - n % 4
                    src = SS[:, n - 4, d] if n >= 4 else SSt[:, d]
                    dst = SS[:, n - 3, d] if n >= 3 else SSt[:, d]
                    pool.wait_ge(*L.at("dve", "SS", n, d))
                    pool.wait_ge(*L.own())
                    e_ = eglb[:, c_ % 2, c_ // 2, 16 + 8 * d:24 + 8 * d].unsqueeze(2).broadcast_to([P, H, C])
                    pool.wait_ge(*L.own())
                    g_.tensor_tensor(view(dst, H, C), view(src, H, C), e_, ALU.mult).then_inc(*L.mark("SSe", n, d))
            for t in range(2):
                pool.wait_ge(*L.own())
                g_.tensor_copy(mix[:, t, 0:512], zs[:, t]).then_inc(*L.mark("mix", 0, t))
            for t in range(2):
                pool.wait_ge(*L.at("dve", "yn", t))
                pool.wait_ge(*L.own())
                g_.tensor_tensor(mix[:, t, 512:1024], yt[:, 2 * t], snw, ALU.mult).then_inc(*L.mark("mix", 1, t))
            pool.wait_ge(*L.at("pe", "mixT", 1, 1))
            pool.wait_ge(*L.own())
            pool.nop().then_inc(*L.mark("end", "ssd"))
            barrier(pool, L, "ssd")

            L.stage("route")
            g_.memset(acc.rearrange("p a b -> p (a b)"), 0.0).then_inc(*L.mark())
            pool.wait_ge(*L.at("dve", "h", 1))
            for s_ in range(3):
                pool.wait_ge(*L.own())
                g_.tensor_copy(hparts[:, s_, 1], hm[:, 1] if s_ == 0 else x1[:, 1]).then_inc(*L.mark("hparts"))
                if s_ < 2:
                    pool.wait_ge(*L.own())
                    g_.tensor_tensor(x1[:, 1], hm[:, 1] if s_ == 0 else x1[:, 1], hparts[:, s_, 1], ALU.subtract).then_inc(*L.mark())
            pool.wait_ge(*L.at("pe", "logit", 1))
            g_.memset(GT.rearrange("p a b -> p (a b)"), 0.0).then_inc(*L.mark())
            g_.memset(ysb, 0.0).then_inc(*L.mark("zeros"))


def kernel(**inputs):
    import numpy as np
    import concourse.bacc as bacc
    from concourse.bass_utils import run_bass_kernel_spmd

    a = {k: np.asarray(v) for k, v in inputs.items()}

    def all_rows(v):
        return np.broadcast_to(v.reshape(1, -1), (P, v.size))

    def channels(v, n):
        return v.reshape(n, P).T if v.ndim == 1 else v.T.reshape(n, P, -1).transpose(1, 0, 2)

    w_in = a["w_in"][0]
    fm_at = {"q": 0, "k": 512, "v": 1024, "xs": 2080, "b": 2592, "c": 2848}

    def k_tiles(w):
        return w.reshape(KT, P, -1).transpose(1, 0, 2).reshape(P, -1)

    wfm = np.stack([k_tiles(w_in[:, fm_at[k] + 128 * j:fm_at[k] + 128 * j + 128]) for k, j, _ in FM])
    wz = np.stack([k_tiles(w_in[:, c0:c0 + 512]).reshape(P, KT, 512) for c0 in (1536, 2080 + 1024)])
    wsm = k_tiles(np.concatenate([w_in[:, 2048:2080], w_in[:, 2080 + 1536:2080 + 1552]], axis=1))
    cols = np.concatenate([channels(a["norm_pre_mix"][0], 8),
                           channels(np.concatenate([a["gdn_conv_w"][0], a["ssd_conv_w"][0]], axis=1), 20).reshape(P, 100),
                           channels(a["ssd_conv_b"][0], 8)], axis=1)
    small = np.concatenate([all_rows(a[n][0]) for n in ("gdn_A_log", "ssd_A_log", "gdn_dt_bias", "ssd_dt_bias",
                                                        "ssd_D", "gdn_norm_w", "ssd_norm_w", "b_router")]
                           + [np.zeros((P, 40), np.float32)], axis=1)
    wrow = np.concatenate([all_rows(a[n][0]) for n in ("norm_post_mix", "norm_pre_ffn", "norm_post_ffn")], axis=1)
    cc = np.stack([a["c"][0].reshape(KT, P), a["c_ctx"].reshape(KT, P)]).transpose(2, 1, 0).reshape(P, 2 * KT)

    arrays = {
        "x": a["x"][0], "ctx": a["ctx"][0], "consts": constants(np), "cc": cc, "b_ada": a["b_ada"],
        "w_ada": a["w_ada"][0], "wfm": wfm, "wz": wz, "wsm": wsm, "cols": cols, "small": small, "wrow": wrow,
        "w_out": a["w_out"][0], "w_router": k_tiles(a["w_router"][0]), "w_gate": a["w_gate"][0], "w_up": a["w_up"][0],
        "w_down": a["w_down"][0], "b_gate": a["b_gate"][0], "b_up": a["b_up"][0], "b_down": a["b_down"][0],
    }
    arrays = {k: np.ascontiguousarray(v) for k, v in arrays.items()}
    book = None
    for _ in range(2):
        nc = bacc.Bacc("TRN2", target_bir_lowering=False, num_devices=1)
        aps = {k: nc.dram_tensor(f"in_{k}", v.shape, F32, kind="ExternalInput").ap() for k, v in arrays.items()}
        out = nc.dram_tensor("out_0", (SEQ, D), F32, kind="ExternalOutput").ap()
        book = Book(book)
        layer_program(nc, book, out=out, **aps)
    result = run_bass_kernel_spmd(nc, [{f"in_{k}": v for k, v in arrays.items()}], core_ids=[0])
    return result.results[0]["out_0"].reshape(1, SEQ, D)


def constants(np):
    p, q = np.arange(P)[:, None], np.arange(P)[None, :]
    same = (p // C == q // C)
    z = {}
    z["ident"] = (p == q)
    z["tri"] = np.concatenate([same & (p <= q), same & (p >= q)], axis=1)
    reach = [same & (p <= q), same & (p >= q)]
    z["neg"] = np.concatenate([np.where(r, 0.0, -BIG) for r in reach], axis=1)
    z["same"] = same
    z["row"] = np.concatenate([(p == C * half) & (q >= 0) for half in range(2)], axis=1)

    def level(n, d, c, s):
        if d:
            c, s = s, c
        block = (c // (2 * n) == s // (2 * n)) & (c % (2 * n) >= n) & (s % (2 * n) < n)
        return (c == s) * 1.0 - block
    z["qmask"] = np.concatenate([level(n, d, p, q) for n in LEVELS for d in range(2)], axis=1)
    z["m1t"] = np.concatenate([level(1, d, q, p) for d in range(2)], axis=1)
    z["pick"] = (p % 32 == np.arange(2)[None, :])
    z["first"] = (np.arange(32)[None, :] < 2) & (p == 0)
    z["rowb"] = (p % 32 == 0) & (q >= 0)
    z["before"] = (p < q)
    z["ones"] = np.ones((P, P))
    z["slots"] = (q % SLOT) + 0 * p
    z["iota32"] = np.arange(32)[None, :] + 0 * p
    z["eps"] = np.full((P, 1), EPS)
    z["lnq"] = np.full((P, 1), np.log(C ** -0.5))
    z["zero"] = np.zeros((P, 1))
    z["eye96"] = (p % 32 == np.arange(32)[None, :]) & (p < 96)
    z["k16"] = np.arange(16)[None, :] + 0 * p
    return np.concatenate([np.asarray(z[n], np.float32) for n in CONSTS], axis=1)
```
